# Optimizing a Trainium2 kernel written in Bass

```python
import jax, jax.numpy as jnp
from jax import lax
import numpy as np

D_MODEL = 1024
BATCH = 1
SEQ = 512
DEPTH = 1

ROPE_THETA = 10000.0
NORM_EPS = 1e-6
GN_EPS = 1e-5

RET_HEADS = 4
RET_DK = 64
RET_DV = 128
RET_CHUNK = 128

NSA_HEADS = 8
NSA_KV_HEADS = 2
NSA_DK = 64
NSA_GROUP = NSA_HEADS // NSA_KV_HEADS
CMP_BLOCK = 32
CMP_STRIDE = 16
CMP_HID = 256
SLC_BLOCK = 64
SLC_TOPK = 16
SLC_LOCAL = 2
WINDOW = 512
NSA_QBLOCK = 128
SEL_BIG = 1e9
NEG = -1e30

D_RET = RET_HEADS * RET_DV
D_NSA = NSA_HEADS * NSA_DK
D_MIX = D_RET + D_NSA

RET_QK = RET_HEADS * RET_DK
NSA_KV = NSA_KV_HEADS * NSA_DK
NSA_GATES = 3 * NSA_HEADS
SPLITS = [RET_QK, RET_QK, D_RET, D_RET, D_NSA] + [NSA_KV] * 6 + [NSA_GATES]
IN_COLS = sum(SPLITS)

D_FF = 2816
CONV_WIDTH = 3


def rms_norm(x, w):
    xf = x.astype(jnp.float32)
    y = xf * lax.rsqrt(jnp.mean(xf * xf, axis=-1, keepdims=True) + NORM_EPS)
    return (y * w.astype(jnp.float32)).astype(x.dtype)

def rope_angles(pos, dim):
    inv = 1.0 / (ROPE_THETA ** (jnp.arange(0, dim, 2, dtype=jnp.float32) / dim))
    ang = pos.astype(jnp.float32)[:, None] * inv[None, :]
    return jnp.cos(ang), jnp.sin(ang)

def apply_rope(x, cos, sin):
    x1, x2 = jnp.split(x, 2, axis=-1)
    c = cos[:, None, :]
    s = sin[:, None, :]
    return jnp.concatenate([x1 * c - x2 * s, x1 * s + x2 * c], axis=-1)

def masked_softmax(s, mask):
    s = jnp.where(mask, s, NEG)
    m = jnp.max(s, axis=-1, keepdims=True)
    e = jnp.where(mask, jnp.exp(s - m), 0.0)
    return e / jnp.maximum(jnp.sum(e, axis=-1, keepdims=True), 1e-30)

def retention(q, k, v, g, gn_w, cos, sin):
    f32 = jnp.float32
    B, S = q.shape[0], q.shape[1]
    H, C = RET_HEADS, RET_CHUNK
    N = S // C
    q = apply_rope(q.astype(f32), cos, sin)
    k = apply_rope(k.astype(f32), cos, sin) * (RET_DK ** -0.5)
    v = v.astype(f32).reshape(B, S, H, RET_DV)
    qc = q.reshape(B, N, C, H, RET_DK).transpose(0, 3, 1, 2, 4)
    kc = k.reshape(B, N, C, H, RET_DK).transpose(0, 3, 1, 2, 4)
    vc = v.reshape(B, N, C, H, RET_DV).transpose(0, 3, 1, 2, 4)
    log_gamma = jnp.log(1.0 - 2.0 ** (-5.0 - jnp.arange(H, dtype=f32)))
    i = jnp.arange(C, dtype=f32)
    diff = i[:, None] - i[None, :]
    decay = jnp.where(diff >= 0, jnp.exp(log_gamma[:, None, None] * jnp.maximum(diff, 0.0)), 0.0)
    scores = jnp.einsum('bhnid,bhnjd->bhnij', qc, kc) * decay[None, :, None]
    o_inner = jnp.einsum('bhnij,bhnje->bhnie', scores, vc)
    zeta = jnp.exp(log_gamma[:, None] * (C - 1.0 - i)[None, :])
    xi = jnp.exp(log_gamma[:, None] * (i + 1.0)[None, :])
    kv = jnp.einsum('bhnjd,bhnje->bhnde', kc * zeta[None, :, None, :, None], vc)
    chunk_decay = jnp.exp(log_gamma * C)[None, :, None, None]

    def step(state, kv_n):
        return state * chunk_decay + kv_n, state

    _, prev = lax.scan(step, jnp.zeros((B, H, RET_DK, RET_DV), f32), kv.transpose(2, 0, 1, 3, 4))
    prev = prev.transpose(1, 2, 0, 3, 4)
    o_cross = jnp.einsum('bhnid,bhnde->bhnie', qc, prev) * xi[None, :, None, :, None]
    o = (o_inner + o_cross).transpose(0, 2, 3, 1, 4).reshape(B, S, H, RET_DV)
    mu = jnp.mean(o, axis=-1, keepdims=True)
    var = jnp.mean(jnp.square(o - mu), axis=-1, keepdims=True)
    o = ((o - mu) * lax.rsqrt(var + GN_EPS)).reshape(B, S, D_RET) * gn_w.astype(f32)
    return jax.nn.silu(g.astype(f32)) * o

def compress(kv, pos_emb, w1, w2):
    B, S, G, D = kv.shape
    n_cmp = (S - CMP_BLOCK) // CMP_STRIDE + 1
    idx = (np.arange(n_cmp)[:, None] * CMP_STRIDE + np.arange(CMP_BLOCK)[None, :]).astype(np.int32)
    blocks = kv[:, idx] + pos_emb.astype(jnp.float32)[None, None, :, None, :]
    flat = blocks.transpose(0, 1, 3, 2, 4).reshape(B, n_cmp, G, CMP_BLOCK * D)
    hid = jax.nn.gelu(flat @ w1.astype(jnp.float32))
    return hid @ w2.astype(jnp.float32)

def nsa(q, k_cmp, v_cmp, k_slc, v_slc, k_win, v_win, gate_logits,
        cmp_k_pos, cmp_k_w1, cmp_k_w2, cmp_v_pos, cmp_v_w1, cmp_v_w2, cos, sin):
    f32 = jnp.float32
    B, S = q.shape[0], q.shape[1]
    G, R, D, QB = NSA_KV_HEADS, NSA_GROUP, NSA_DK, NSA_QBLOCK
    q = apply_rope(q.astype(f32), cos, sin) * (D ** -0.5)
    kc = compress(k_cmp.astype(f32), cmp_k_pos, cmp_k_w1, cmp_k_w2)
    vc = compress(v_cmp.astype(f32), cmp_v_pos, cmp_v_w1, cmp_v_w2)
    n_cmp = kc.shape[1]
    cmp_start = np.arange(n_cmp) * CMP_STRIDE
    cmp_end = (cmp_start + CMP_BLOCK - 1).astype(np.int32)
    ccos, csin = rope_angles(jnp.asarray(cmp_end), D)
    kc = apply_rope(kc, ccos, csin)
    ks = apply_rope(k_slc.astype(f32), cos, sin)
    kw = apply_rope(k_win.astype(f32), cos, sin)
    n_slc = S // SLC_BLOCK
    topk = min(SLC_TOPK, n_slc)
    slc_start = np.arange(n_slc) * SLC_BLOCK
    overlap = ((cmp_start[:, None] < slc_start[None, :] + SLC_BLOCK)
               & (cmp_start[:, None] + CMP_BLOCK > slc_start[None, :])).astype(np.float32)

    qg = q.reshape(B, S, G, R, D).transpose(0, 2, 3, 1, 4)
    kc_g = kc.transpose(0, 2, 1, 3)
    vc_g = vc.transpose(0, 2, 1, 3)
    ks_blk = ks.reshape(B, n_slc, SLC_BLOCK, G, D).transpose(0, 3, 1, 2, 4)
    vs_blk = v_slc.astype(f32).reshape(B, n_slc, SLC_BLOCK, G, D).transpose(0, 3, 1, 2, 4)
    pad = ((0, 0), (0, 0), (WINDOW, 0), (0, 0))
    kw_pad = jnp.pad(kw.transpose(0, 2, 1, 3), pad)
    vw_pad = jnp.pad(v_win.astype(f32).transpose(0, 2, 1, 3), pad)
    nqb = S // QB
    q_blocks = qg.reshape(B, G, R, nqb, QB, D).transpose(3, 0, 1, 2, 4, 5)
    bi = jnp.arange(B)[:, None, None, None]
    gi = jnp.arange(G)[None, :, None, None]
    jsl = jnp.arange(n_slc, dtype=jnp.int32)

    def block_fn(args):
        qb, blk = args
        t = blk * QB + jnp.arange(QB, dtype=jnp.int32)
        valid_c = jnp.asarray(cmp_end)[None, :] <= t[:, None]
        p_cmp = masked_softmax(jnp.einsum('bgrtd,bgnd->bgrtn', qb, kc_g), valid_c)
        o_cmp = jnp.einsum('bgrtn,bgnd->bgrtd', p_cmp, vc_g)
        imp = jnp.einsum('bgrtn,nj->bgtj', p_cmp, overlap)
        qblk = t // SLC_BLOCK
        blk_valid = jsl[None, :] <= qblk[:, None]
        forced = (jsl[None, :] == 0) | (blk_valid & (jsl[None, :] > qblk[:, None] - SLC_LOCAL))
        score = jnp.where(forced, SEL_BIG, jnp.where(blk_valid, imp, -SEL_BIG))
        _, sel = lax.top_k(score, topk)
        kg = ks_blk[bi, gi, sel]
        vg = vs_blk[bi, gi, sel]
        tok = sel[..., None] * SLC_BLOCK + jnp.arange(SLC_BLOCK, dtype=jnp.int32)
        smask = (tok <= t[None, None, :, None, None]).reshape(B, G, 1, QB, topk * SLC_BLOCK)
        s_slc = jnp.einsum('bgrtd,bgtksd->bgrtks', qb, kg).reshape(B, G, R, QB, topk * SLC_BLOCK)
        p_slc = masked_softmax(s_slc, smask).reshape(B, G, R, QB, topk, SLC_BLOCK)
        o_slc = jnp.einsum('bgrtks,bgtksd->bgrtd', p_slc, vg)
        kwb = lax.dynamic_slice_in_dim(kw_pad, blk * QB, WINDOW + QB, axis=2)
        vwb = lax.dynamic_slice_in_dim(vw_pad, blk * QB, WINDOW + QB, axis=2)
        kpos = blk * QB - WINDOW + jnp.arange(WINDOW + QB, dtype=jnp.int32)
        wmask = (kpos[None, :] <= t[:, None]) & (kpos[None, :] > t[:, None] - WINDOW) & (kpos[None, :] >= 0)
        p_win = masked_softmax(jnp.einsum('bgrtd,bgsd->bgrts', qb, kwb), wmask)
        o_win = jnp.einsum('bgrts,bgsd->bgrtd', p_win, vwb)
        return o_cmp, o_slc, o_win

    o_cmp, o_slc, o_win = lax.map(block_fn, (q_blocks, jnp.arange(nqb, dtype=jnp.int32)))

    def to_bshd(o):
        return o.transpose(1, 0, 4, 2, 3, 5).reshape(B, S, NSA_HEADS, D)

    gates = jax.nn.sigmoid(gate_logits.astype(f32)).reshape(B, S, 3, NSA_HEADS)[..., None]
    out = gates[:, :, 0] * to_bshd(o_cmp) + gates[:, :, 1] * to_bshd(o_slc) + gates[:, :, 2] * to_bshd(o_win)
    return out.reshape(B, S, D_NSA)

def conv_ffn(x, w_up, conv_w, w_down):
    u = x @ w_up
    c = u.shape[-1]
    u = lax.conv_general_dilated(u, conv_w[:, None, :].astype(u.dtype), window_strides=(1,),
                                 padding=[(CONV_WIDTH - 1, 0)],
                                 dimension_numbers=('NWC', 'WIO', 'NWC'),
                                 feature_group_count=c)
    gate, val = jnp.split(u, 2, axis=-1)
    return (jax.nn.gelu(gate) * val) @ w_down

def first_inputs(seed: int = 0) -> dict:
    key = jax.random.key(seed)
    ks = jax.random.split(key, 20)
    L = DEPTH

    def nrm(k, shape, scale):
        return jax.random.normal(k, shape, jnp.float32) * scale

    def gain(k, shape):
        return 1.0 + 0.02 * jax.random.normal(k, shape, jnp.float32)

    return {
        'x': nrm(ks[0], (BATCH, SEQ, D_MODEL), 1.0),
        'norm_mix_pre': gain(ks[1], (L, D_MODEL)),
        'w_in': nrm(ks[2], (L, D_MODEL, IN_COLS), D_MODEL ** -0.5),
        'ret_gn_w': gain(ks[3], (L, D_RET)),
        'cmp_k_pos': nrm(ks[4], (L, CMP_BLOCK, NSA_DK), 0.02),
        'cmp_k_w1': nrm(ks[5], (L, CMP_BLOCK * NSA_DK, CMP_HID), (CMP_BLOCK * NSA_DK) ** -0.5),
        'cmp_k_w2': nrm(ks[6], (L, CMP_HID, NSA_DK), CMP_HID ** -0.5),
        'cmp_v_pos': nrm(ks[7], (L, CMP_BLOCK, NSA_DK), 0.02),
        'cmp_v_w1': nrm(ks[8], (L, CMP_BLOCK * NSA_DK, CMP_HID), (CMP_BLOCK * NSA_DK) ** -0.5),
        'cmp_v_w2': nrm(ks[9], (L, CMP_HID, NSA_DK), CMP_HID ** -0.5),
        'w_out': nrm(ks[10], (L, D_MIX, D_MODEL), D_MIX ** -0.5),
        'norm_mix_post': gain(ks[11], (L, D_MODEL)),
        'norm_ffn_pre': gain(ks[12], (L, D_MODEL)),
        'ffn_w_up': nrm(ks[13], (L, D_MODEL, 2 * D_FF), D_MODEL ** -0.5),
        'ffn_conv': nrm(ks[14], (L, CONV_WIDTH, 2 * D_FF), CONV_WIDTH ** -0.5),
        'ffn_w_down': nrm(ks[15], (L, D_FF, D_MODEL), D_FF ** -0.5),
        'norm_ffn_post': gain(ks[16], (L, D_MODEL)),
    }

def first_block(x, norm_mix_pre, w_in, ret_gn_w, cmp_k_pos, cmp_k_w1, cmp_k_w2,
              cmp_v_pos, cmp_v_w1, cmp_v_w2, w_out, norm_mix_post, norm_ffn_pre,
              ffn_w_up, ffn_conv, ffn_w_down, norm_ffn_post):
    B, S, _ = x.shape
    cos, sin = rope_angles(jnp.arange(S, dtype=jnp.int32), NSA_DK)
    split_at = [int(v) for v in np.cumsum(SPLITS)[:-1]]
    for l in range(DEPTH):
        h = rms_norm(x, norm_mix_pre[l])
        proj = h @ w_in[l]
        (rq, rk, rv, rg, nq, kcm, vcm, ksl, vsl, kwn, vwn, ng) = jnp.split(proj, split_at, axis=-1)
        y_ret = retention(rq.reshape(B, S, RET_HEADS, RET_DK), rk.reshape(B, S, RET_HEADS, RET_DK),
                          rv, rg, ret_gn_w[l], cos, sin)
        kv = lambda a: a.reshape(B, S, NSA_KV_HEADS, NSA_DK)
        y_nsa = nsa(nq.reshape(B, S, NSA_HEADS, NSA_DK), kv(kcm), kv(vcm), kv(ksl), kv(vsl), kv(kwn), kv(vwn), ng,
                    cmp_k_pos[l], cmp_k_w1[l], cmp_k_w2[l], cmp_v_pos[l], cmp_v_w1[l], cmp_v_w2[l], cos, sin)
        mix = jnp.concatenate([y_ret, y_nsa], axis=-1).astype(x.dtype) @ w_out[l]
        x = x + rms_norm(mix, norm_mix_post[l])
        h = rms_norm(x, norm_ffn_pre[l])
        x = x + rms_norm(conv_ffn(h, ffn_w_up[l], ffn_conv[l], ffn_w_down[l]), norm_ffn_post[l])
    return x


MIX_WIDTH = D_MODEL
HGRN_WIDTH = MIX_WIDTH // 2
CONV_WIDTH_2 = MIX_WIDTH - HGRN_WIDTH
HGRN_HEAD_DIM = 128
HGRN_HEADS = HGRN_WIDTH // HGRN_HEAD_DIM
CONV_GROUPS = 4
CONV_GROUP_DIM = CONV_WIDTH_2 // CONV_GROUPS
CONV_TAPS = 3
CHUNK = 64
IN_COLS_2 = 4 * HGRN_WIDTH + 3 * CONV_WIDTH_2
PEER_HEADS = 8
PEER_NKEYS = 128
PEER_EXPERTS = PEER_NKEYS * PEER_NKEYS
PEER_QDIM = 256
PEER_HALF = PEER_QDIM // 2
PEER_TOPK = 16
TOKEN_BLOCK = 128
EPS = 1e-6


def rmsnorm(x, w):
    xf = x.astype(jnp.float32)
    y = xf * lax.rsqrt(jnp.mean(xf * xf, axis=-1, keepdims=True) + EPS)
    return (y * w.astype(jnp.float32)).astype(x.dtype)

def group_rmsnorm(x, w, groups):
    shp = x.shape
    xg = x.reshape(shp[:-1] + (groups, shp[-1] // groups))
    return rmsnorm(xg, w.reshape(groups, shp[-1] // groups)).reshape(shp)

def hgrn2_chunkwise(q, k, v, log_f):
    B, H, S, DK = q.shape
    DV = v.shape[-1]
    n = S // CHUNK

    def to_chunks(t):
        return t.reshape(B, H, n, CHUNK, t.shape[-1]).transpose(2, 0, 1, 3, 4)

    qc, kc, vc, gc = to_chunks(q), to_chunks(k), to_chunks(v), to_chunks(log_f)
    causal = jnp.tril(jnp.ones((CHUNK, CHUNK), dtype=bool))[:, :, None]

    def step(state, inp):
        qb, kb, vb, gb = inp
        b = jnp.cumsum(gb, axis=2)
        diff = b[:, :, :, None, :] - b[:, :, None, :, :]
        decay = jnp.exp(jnp.where(causal, diff, -jnp.inf))
        scores = jnp.einsum('bhtd,bhsd,bhtsd->bhts', qb, kb, decay)
        o = (jnp.einsum('bhts,bhsv->bhtv', scores, vb)
             + jnp.einsum('bhtd,bhdv->bhtv', qb * jnp.exp(b), state))
        b_last = b[:, :, -1:, :]
        new_state = (jnp.exp(b_last[:, :, 0, :])[..., None] * state
                     + jnp.einsum('bhsd,bhsv->bhdv', kb * jnp.exp(b_last - b), vb))
        return new_state, o

    s0 = jnp.zeros((B, H, DK, DV), jnp.float32)
    _, o = lax.scan(step, s0, (qc, kc, vc, gc))
    return o.transpose(1, 2, 0, 3, 4).reshape(B, H, S, DV)

def hgrn2_group(p, lb, onorm_w):
    B, S, _ = p.shape
    pf = p.astype(jnp.float32)
    q, f_raw, i, g = jnp.split(pf, 4, axis=-1)
    f = lb + (1.0 - lb) * jax.nn.sigmoid(f_raw)
    log_f = jnp.log(f)
    k = (1.0 - lb) * jax.nn.sigmoid(-f_raw)

    def heads(t):
        return t.reshape(B, S, HGRN_HEADS, HGRN_HEAD_DIM).transpose(0, 2, 1, 3)

    o = hgrn2_chunkwise(heads(q), heads(k), heads(i), heads(log_f))
    o = o.transpose(0, 2, 1, 3).reshape(B, S, HGRN_WIDTH)
    o = group_rmsnorm(o, onorm_w, HGRN_HEADS) * jax.nn.silu(g)
    return o.astype(p.dtype)

def short_conv_group(p, conv_w, onorm_w):
    b_gate, c_gate, xin = jnp.split(p, 3, axis=-1)
    u = c_gate * xin
    y = lax.conv_general_dilated(
        u, conv_w[:, None, :].astype(u.dtype), window_strides=(1,),
        padding=[(CONV_TAPS - 1, 0)], dimension_numbers=('NWC', 'WIO', 'NWC'),
        feature_group_count=CONV_WIDTH_2)
    y = b_gate * y
    return group_rmsnorm(y, onorm_w, CONV_GROUPS)

def peer(h, w_query, sub_keys, expert_u, expert_v):
    B, S, D = h.shape
    hb = h.reshape(B * S // TOKEN_BLOCK, TOKEN_BLOCK, D)

    def block(xb):
        T = xb.shape[0]
        q = (xb @ w_query).reshape(T, PEER_HEADS, 2, PEER_HALF)
        s = jnp.einsum('thpk,hpnk->thpn', q, sub_keys).astype(jnp.float32)
        top_s, top_i = lax.top_k(s, PEER_TOPK)
        cand_s = top_s[:, :, 0, :, None] + top_s[:, :, 1, None, :]
        cand_i = top_i[:, :, 0, :, None] * PEER_NKEYS + top_i[:, :, 1, None, :]
        best_s, best_pos = lax.top_k(cand_s.reshape(T, PEER_HEADS, PEER_TOPK * PEER_TOPK), PEER_TOPK)
        idx = jnp.take_along_axis(cand_i.reshape(T, PEER_HEADS, PEER_TOPK * PEER_TOPK), best_pos, axis=-1)
        gate = jax.nn.softmax(best_s, axis=-1)
        u = expert_u[idx]
        v = expert_v[idx]
        act = jax.nn.gelu(jnp.einsum('td,thkd->thk', xb, u).astype(jnp.float32), approximate=False)
        return jnp.einsum('thk,thkd->td', (gate * act).astype(xb.dtype), v)

    return lax.map(block, hb).reshape(B, S, D)

def second_inputs(seed: int = 0) -> dict:
    key = jax.random.key(seed)
    ks = jax.random.split(key, 17)
    f32 = jnp.float32
    D = D_MODEL
    return {
        "x": jax.random.normal(ks[0], (BATCH, SEQ, D), f32),
        "c": jax.random.normal(ks[1], (BATCH, D), f32),
        "w_ada": jax.random.normal(ks[2], (DEPTH, D, 6 * D), f32) * (0.5 * D ** -0.5),
        "b_ada": jax.random.normal(ks[3], (DEPTH, 6 * D), f32) * 0.02,
        "norm1_w": 1.0 + 0.02 * jax.random.normal(ks[4], (DEPTH, D), f32),
        "w_in": jax.random.normal(ks[5], (DEPTH, D, IN_COLS_2), f32) * D ** -0.5,
        "hgrn_lb_logits": jax.random.normal(ks[6], (DEPTH + 1, HGRN_WIDTH), f32) * 0.5,
        "hgrn_onorm_w": 1.0 + 0.02 * jax.random.normal(ks[7], (DEPTH, HGRN_WIDTH), f32),
        "conv_w": jax.random.normal(ks[8], (DEPTH, CONV_TAPS, CONV_WIDTH_2), f32) * CONV_TAPS ** -0.5,
        "conv_onorm_w": 1.0 + 0.02 * jax.random.normal(ks[9], (DEPTH, CONV_WIDTH_2), f32),
        "w_out": jax.random.normal(ks[10], (DEPTH, MIX_WIDTH, D), f32) * MIX_WIDTH ** -0.5,
        "norm2_w": 1.0 + 0.02 * jax.random.normal(ks[11], (DEPTH, D), f32),
        "peer_w_query": jax.random.normal(ks[12], (DEPTH, D, PEER_HEADS * PEER_QDIM), f32) * D ** -0.5,
        "peer_sub_keys": jax.random.normal(ks[13], (DEPTH, PEER_HEADS, 2, PEER_NKEYS, PEER_HALF), f32) * PEER_HALF ** -0.5,
        "peer_u": jax.random.normal(ks[14], (DEPTH, PEER_EXPERTS, D), f32) * D ** -0.5,
        "peer_v": jax.random.normal(ks[15], (DEPTH, PEER_EXPERTS, D), f32),
        "final_norm_w": 1.0 + 0.02 * jax.random.normal(ks[16], (D,), f32),
    }

def second_block(x, c, w_ada, b_ada, norm1_w, w_in, hgrn_lb_logits, hgrn_onorm_w, conv_w,
              conv_onorm_w, w_out, norm2_w, peer_w_query, peer_sub_keys, peer_u, peer_v,
              final_norm_w):
    lower_bounds = jnp.cumsum(jax.nn.softmax(hgrn_lb_logits.astype(jnp.float32), axis=0), axis=0)
    c_act = jax.nn.silu(c)
    for l in range(DEPTH):
        mod = (c_act @ w_ada[l] + b_ada[l])[:, None, :]
        shift1, scale1, gate1, shift2, scale2, gate2 = jnp.split(mod, 6, axis=-1)

        h = rmsnorm(x, norm1_w[l]) * (1.0 + scale1) + shift1
        proj = h @ w_in[l]
        y_a = hgrn2_group(proj[..., :4 * HGRN_WIDTH], lower_bounds[l], hgrn_onorm_w[l])
        y_b = short_conv_group(proj[..., 4 * HGRN_WIDTH:], conv_w[l], conv_onorm_w[l])
        mix = jnp.concatenate([y_a, y_b], axis=-1) @ w_out[l]
        x = x + gate1 * mix

        h = rmsnorm(x, norm2_w[l]) * (1.0 + scale2) + shift2
        x = x + gate2 * peer(h, peer_w_query[l], peer_sub_keys[l], peer_u[l], peer_v[l])
    return rmsnorm(x, final_norm_w)


def setup_inputs(seed=0):
    out = dict(first_inputs(seed))
    for name, value in second_inputs(seed + 1).items():
        if name != "x":
            out[name + "_2"] = value
    return out


def reference(
    x, norm_mix_pre, w_in, ret_gn_w, cmp_k_pos, cmp_k_w1, cmp_k_w2, cmp_v_pos, cmp_v_w1,
    cmp_v_w2, w_out, norm_mix_post, norm_ffn_pre, ffn_w_up, ffn_conv, ffn_w_down, norm_ffn_post,
    c_2, w_ada_2, b_ada_2, norm1_w_2, w_in_2, hgrn_lb_logits_2, hgrn_onorm_w_2, conv_w_2,
    conv_onorm_w_2, w_out_2, norm2_w_2, peer_w_query_2, peer_sub_keys_2, peer_u_2, peer_v_2,
    final_norm_w_2,
):
    x = first_block(
        x, norm_mix_pre, w_in, ret_gn_w, cmp_k_pos, cmp_k_w1, cmp_k_w2, cmp_v_pos, cmp_v_w1,
        cmp_v_w2, w_out, norm_mix_post, norm_ffn_pre, ffn_w_up, ffn_conv, ffn_w_down,
        norm_ffn_post,
    )
    return second_block(
        x, c_2, w_ada_2, b_ada_2, norm1_w_2, w_in_2, hgrn_lb_logits_2, hgrn_onorm_w_2, conv_w_2,
        conv_onorm_w_2, w_out_2, norm2_w_2, peer_w_query_2, peer_sub_keys_2, peer_u_2, peer_v_2,
        final_norm_w_2,
    )


_drawn_inputs = setup_inputs


def setup_inputs(seed=0):
    import zlib

    import numpy as np

    out = dict(_drawn_inputs(seed))
    spreads = {}
    factors = {'ret_gn_w': 2.928,
     'cmp_k_pos': 44.85,
     'cmp_v_pos': 4.394,
     'norm_ffn_post': 3.514,
     'norm1_w_2': 6.204,
     'hgrn_onorm_w_2': 25.125,
     'conv_onorm_w_2': 64.0,
     'norm2_w_2': 22.139,
     'final_norm_w_2': 7.759}
    for name, (base, spread) in spreads.items():
        noise = np.random.default_rng([zlib.crc32(name.encode()), seed]).standard_normal(out[name].shape)
        drawn = base * np.exp(spread * noise) if base else spread * noise
        out[name] = __import__('jax').numpy.asarray(drawn.astype(out[name].dtype))
    for name, factor in factors.items():
        out[name] = (out[name] * factor).astype(out[name].dtype)
    return out
```

```python
from contextlib import ExitStack

import numpy as np
import concourse.bass as bass
from concourse import mybir

F32 = mybir.dt.float32
F32R = mybir.dt.float32r
U32 = mybir.dt.uint32
I32 = mybir.dt.int32
ACT = mybir.ActivationFunctionType
ALU = mybir.AluOpType
AX = mybir.AxisListType.X

P = 128
D = 1024
S = 512
NT = S // P
NK = D // P
EPS = 1e-6
GN_EPS = 1e-5
NEG = -1e30
RQ, RK, RV, RG, NQ = 0, 256, 512, 1024, 1536
KCM, VCM, KSL, VSL, KWN, VWN, NG = 2048, 2176, 2304, 2432, 2560, 2688, 2816
IN_COLS = 2840
TAIL = IN_COLS - 5 * 512
RH, NH, GR = 4, 8, 2
DK = 64
DFF = 2816
NF = DFF // P
CW = 1024
RING = 4
LEAD = 3
GROUP = 8
NGRP = P // GROUP
PH, PK, TOPK = 8, 128, 16

PHASES = [("win", 24), ("cmp", 8), ("wout", 8), ("up", 2 * NF), ("down", NF), ("ada_t", 32),
          ("ada_n", 16), ("win2", 28), ("wout2", 8), ("query", 16), ("experts", 2 * P)]
FIRST = {}
_n = 0
for _name, _count in PHASES:
    FIRST[_name] = _n
    _n += _count
CHUNKS = _n


def constants():
    f = np.float32
    inv = 1.0 / (10000.0 ** (np.arange(0, DK, 2, dtype=np.float64) / DK))

    def angles(pos):
        a = (pos.astype(f)[:, None] * inv.astype(f)[None, :]).astype(np.float64)
        c, s = np.cos(a), np.sin(a)
        return np.concatenate([c, c], 1).astype(f), np.concatenate([-s, s], 1).astype(f)

    cols = {}
    cols["ident"] = np.eye(P, dtype=f)
    cols["ones"] = np.ones((P, P), f)
    c, s = angles(np.arange(S))
    cols["cos"] = c.reshape(NT, P, DK).transpose(1, 0, 2).reshape(P, -1)
    cols["sin"] = s.reshape(NT, P, DK).transpose(1, 0, 2).reshape(P, -1)
    end = np.tile(np.arange(32) * 16 + 31, 4)
    c, s = angles(end)
    cols["ccos"], cols["csin"] = c, s
    i = np.arange(P)
    cols["causal"] = np.where(i[None, :] > i[:, None], NEG, 0.0).astype(f)
    t = np.arange(S).reshape(NT, P)
    ok = (end[None, None, :32] <= t[:, :, None]) & (np.arange(32) < 31)
    ok = ok.transpose(1, 0, 2).reshape(P, -1)
    cols["cmp_ok"] = ok.astype(f)
    cols["cmp_no"] = np.where(ok, 0.0, NEG).astype(f)
    cols["iota"] = np.tile(i.astype(f), (P, 1))
    cols["four"] = (i[:, None] // 32 == np.arange(4)[None, :]).astype(f)
    small = cols
    gamma = 1.0 - 2.0 ** (-5.0 - np.arange(RH))
    x = np.arange(S)[None, None, :] - i[:, None, None]
    decay = np.where(x >= 0, np.exp(np.log(gamma)[None, :, None] * np.maximum(x, 0)), 0.0) * DK ** -0.5
    lev = np.zeros((P, 8, P), np.uint32)
    for n, m in enumerate((64, 32, 16, 8, 4, 2, 1)):
        lev[:, n] = ((i[:, None] // (2 * m) == i[None, :] // (2 * m)) & (i[:, None] % (2 * m) < m)
                     & (i[None, :] % (2 * m) >= m))
    lev[:, 7] = np.eye(P)
    return small, decay.astype(f).reshape(P, -1), lev.reshape(P, -1)


CONST_COLS = [("ident", P), ("ones", P), ("cos", NT * DK), ("sin", NT * DK), ("ccos", DK), ("csin", DK),
              ("causal", P), ("cmp_ok", NT * 32), ("cmp_no", NT * 32), ("iota", P), ("four", 4)]
PARAM_COLS = [("nmp", 8), ("nfp", 8), ("n1", 8), ("n2", 8), ("gn", 4), ("bada", 48), ("c", 8), ("lb0", 4),
              ("lb1", 4), ("onorm", 4), ("conorm", 4), ("conv", 12), ("ffconv", 132)]


def offsets(cols):
    at, n = {}, 0
    for name, w in cols:
        at[name] = (n, w)
        n += w
    return at, n


def build(nc, d):
    const_at, n_const = offsets(CONST_COLS)
    param_at, n_param = offsets(PARAM_COLS)
    with ExitStack() as ctx:
        place = {}

        def sb(name, cols, dt=F32):
            place[name] = nc.sbuf_base
            return ctx.enter_context(nc.sbuf_tensor(name, [P, cols], dt))

        def over(parent, name, first, cols, dt):
            return nc.alloc_sbuf_tensor_at(name, [P, cols], dt, offset=(place[parent] + 31) // 32 * 32 + 4 * first)[:, :]

        sems = {}

        def sem(name):
            if name not in sems:
                sems[name] = ctx.enter_context(nc.semaphore(name))
            return sems[name]

        CON, PAR = sb("CON", n_const), sb("PAR", n_param)
        X = sb("X", NT * D)[:, :].rearrange("p (t n) -> p t n", t=NT)
        HHr = sb("HH", NK * S, F32R)[:, :].rearrange("p (k t) -> p k t", k=NK)
        HLr = sb("HL", NK * S, F32R)[:, :].rearrange("p (k t) -> p k t", k=NK)
        HH, HL = HHr.bitcast(F32), HLr.bitcast(F32)
        RAW = sb("RAW", RING * CW)[:, :].rearrange("p (r n) -> p r n", r=RING)
        WHr = sb("WH", RING * CW, F32R)[:, :].rearrange("p (r n) -> p r n", r=RING)
        WLr = sb("WL", RING * CW, F32R)[:, :].rearrange("p (r n) -> p r n", r=RING)
        WH = WHr.bitcast(F32)
        ROW = sb("ROW", D)
        GATE = sb("GATE", 2 * D)[:, :].rearrange("p (g n) -> p g n", g=2)
        MISC = sb("MISC", 1024)
        A = sb("A", 22528)
        PS = ctx.enter_context(nc.psum_tensor("PS", [P, 8, 512], F32))

        def con(name):
            o, w = const_at[name]
            return CON[:, o:o + w]

        def par(name, a=0, b=None):
            o, w = param_at[name]
            return PAR[:, o + a:o + (w if b is None else b)]

        used_misc = [0]

        def misc(n):
            used_misc[0] += n
            assert used_misc[0] <= 1024
            return MISC[:, used_misc[0] - n:used_misc[0]]

        ident = con("ident")
        sumsq, rstd = misc(4), misc(4)

        def wait(eng, s, v):
            if not (isinstance(v, int) and v <= 0):
                eng.wait_ge(sem(s), v)

        phase = {"pe": 0, "act": 0, "dve": 0}

        def barrier(eng, who):
            phase[who] += 1
            eng.drain().then_inc(sem("phase_ended"), 1)
            eng.wait_ge(sem("phase_ended"), 3 * phase[who])

        def link_for(eng, name):
            count = [0]

            def link(ins):
                count[0] += 1
                ins.then_inc(sem(name), 1)
                eng.wait_ge(sem(name), count[0])
            return link

        def slot(c):
            return c[0] % RING

        def plus(c, n):
            return (c[0] + n, c[1], c[2])

        def number(c, n=0):
            return c[0] + n + c[2] * c[1] if not isinstance(c[1], int) else c[0] + n

        def landed(c):
            if isinstance(c[1], int):
                return 16 * (c[0] // RING + 1)
            return 16 * (c[0] // RING + 1) + c[1] * (16 * c[2] // RING)

        def split_high(act, c, w=CW):
            if c[0] >= CHUNKS:
                return
            act.wait_ge(sem(f"raw_landed{slot(c)}"), landed(c))
            wait(act, "chunk_used", number(c, 1 - RING))
            nc.scalar.activation(WHr[:, slot(c), 0:w], RAW[:, slot(c), 0:w], ACT.Copy).then_inc(sem("high_done"), 1)

        def split_low(dve, c, w=CW):
            if c[0] >= CHUNKS:
                return
            dve.wait_ge(sem("high_done"), number(c, 1))
            nc.vector.tensor_tensor(WLr[:, slot(c), 0:w], RAW[:, slot(c), 0:w], WH[:, slot(c), 0:w],
                                    ALU.subtract).then_inc(sem("low_done"), 1)

        def mm3(out, L, R, first, last):
            nc.tensor.matmul(out, L[0], R[0], start=first, stop=False)
            nc.tensor.matmul(out, L[0], R[1], start=False, stop=False)
            return nc.tensor.matmul(out, L[1], R[0], start=False, stop=last)

        def mm_t(pe, c, out, rhs=None, n=S):
            pe.wait_ge(sem("low_done"), number(c, 1))
            wh = WHr[:, slot(c), :].rearrange("p (k n) -> p k n", k=NK)
            wl = WLr[:, slot(c), :].rearrange("p (k n) -> p k n", k=NK)
            for k in range(NK):
                r = (HHr[:, k, :], HLr[:, k, :]) if rhs is None else rhs(k)
                last = mm3(out, (wh[:, k, :], wl[:, k, :]), r, k == 0, k == NK - 1)
            last.then_inc(sem("chunk_used"), 1)

        def mm_n2(pe, c, q, bank, w=512):
            pe.wait_ge(sem("low_done"), number(c, 1))
            wh = WHr[:, slot(c), 0:2 * w].rearrange("p (k n) -> p k n", k=2)
            wl = WLr[:, slot(c), 0:2 * w].rearrange("p (k n) -> p k n", k=2)
            for kk in range(2):
                k = 2 * q + kk
                for t in range(NT):
                    ts = slice(t * P, (t + 1) * P)
                    last = mm3(PS[:, bank + t, 0:w], (HHr[:, k, ts], HLr[:, k, ts]), (wh[:, kk, :], wl[:, kk, :]),
                               k == 0, k == NK - 1)
            last.then_inc(sem("chunk_used"), 1)

        def mm_n1(pe, c, L, first, final):
            pe.wait_ge(sem("low_done"), number(c, 1))
            for t in range(NT):
                ts = slice(t * P, (t + 1) * P)
                for h in range(2):
                    hs = slice(h * 512, (h + 1) * 512)
                    last = mm3(PS[:, 2 * t + h, :], (L[0][:, ts], L[1][:, ts]),
                               (WHr[:, slot(c), hs], WLr[:, slot(c), hs]), first, final)
            last.then_inc(sem("chunk_used"), 1)

        XN = A[:, 0:4096].rearrange("p (t n) -> p t n", t=NT)
        JUNK = A[:, 4096:5120]
        TMP = A[:, 5120:6144].rearrange("p (r n) -> p r n", r=2)
        NORMS = ["pre1", "mixpost", "pre2", "ffpost", "pre3", "pre4", "final"]
        TURNS = ["pre1", "mix", "pre2", "pre3", "pre4"]
        ROWED = ["pre1", "pre2", "pre3", "pre4"]

        def rms_act(act, link, src, tag, n=NT):
            for t in range(n):
                ins = nc.scalar.activation(JUNK if len(src(t).shape) == 2 else JUNK.rearrange("p (a b) -> p a b", a=2),
                                           src(t), ACT.Square, accum_out=sumsq[:, t:t + 1])
                if t < n - 1:
                    link(ins)
            ins.then_inc(sem("rms_squares"), 1)
            act.wait_ge(sem("rms_mean"), NORMS.index(tag) + 1)
            nc.scalar.activation(rstd, rstd, ACT.Sqrt).then_inc(sem("rms_root"), 1)

        def rms_dve(dve, link, tag):
            dve.wait_ge(sem("rms_squares"), NORMS.index(tag) + 1)
            nc.vector.tensor_scalar(rstd, sumsq, 1.0 / D, EPS, ALU.mult, ALU.add).then_inc(sem("rms_mean"), 1)
            dve.wait_ge(sem("rms_root"), NORMS.index(tag) + 1)
            link(nc.vector.reciprocal(rstd, rstd))

        def turn_pe(pe, tag, src):
            for k in range(NK):
                for t in range(NT):
                    if k == 0 and src is XN:
                        pe.wait_ge(sem("rows_normed"), NT * ROWED.index(tag) + t + 1)
                    last = nc.tensor.transpose(PS[:, k, t * P:(t + 1) * P], src[:, t, k * P:(k + 1) * P], ident)
                last.then_inc(sem("tile_turned"), 1)

        def turn_dve(dve, link, tag, scale, bias=None, ready=None):
            for k in range(NK):
                n = NK * TURNS.index(tag) + k
                dve.wait_ge(sem("tile_turned"), n + 1)
                wait(dve, "tile_high", n - 1)
                sc = scale(k)
                if sc is None:
                    ins = nc.vector.tensor_copy(TMP[:, k % 2, :], PS[:, k, :])
                elif bias is None:
                    ins = nc.vector.tensor_scalar(TMP[:, k % 2, :], PS[:, k, :], sc, None, ALU.mult)
                else:
                    ins = nc.vector.tensor_scalar(TMP[:, k % 2, :], PS[:, k, :], sc, bias(k), ALU.mult, ALU.add)
                ins.then_inc(sem("tile_scaled"), 1)
                dve.wait_ge(sem("tile_high"), n + 1)
                link(nc.vector.tensor_tensor(HLr[:, k, :], TMP[:, k % 2, :], HH[:, k, :], ALU.subtract))

        def turn_act(act, tag):
            for k in range(NK):
                act.wait_ge(sem("tile_scaled"), NK * TURNS.index(tag) + k + 1)
                nc.scalar.activation(HHr[:, k, :], TMP[:, k % 2, :], ACT.Copy).then_inc(sem("tile_high"), 1)

        def norm_turn(eng, who, tag, link=None, scale=None, bias=None):
            if who == "act":
                rms_act(eng, link, lambda t: X[:, t, :], tag)
                turn_act(eng, tag)
            elif who == "dve":
                rms_dve(eng, link, tag)
                for t in range(NT):
                    nc.vector.tensor_scalar(XN[:, t, :], X[:, t, :], rstd[:, t:t + 1], None,
                                            ALU.mult).then_inc(sem("rows_normed"), 1)
                turn_dve(eng, link, tag, scale, bias)
            else:
                turn_pe(eng, tag, XN)
            barrier(eng, who)

        def banks(t):
            return PS[:, 2 * t:2 * t + 2, :]

        def add_normed(eng, who, tag, link=None):
            barrier(eng, who)
            if who == "act":
                rms_act(eng, link, banks, tag)
            elif who == "dve":
                rms_dve(eng, link, tag)
                for t in range(NT):
                    link(nc.vector.tensor_scalar(XN[:, t, :].rearrange("p (a b) -> p a b", a=2), banks(t),
                                                 rstd[:, t:t + 1], None, ALU.mult))
                eng.wait_ge(sem("row_landed"), 16 * {"mixpost": 1, "ffpost": 2}[tag])
                for t in range(NT):
                    link(nc.vector.tensor_tensor(XN[:, t, :], XN[:, t, :], ROW[:, :], ALU.mult))
                    link(nc.vector.tensor_tensor(X[:, t, :], X[:, t, :], XN[:, t, :], ALU.add))
            barrier(eng, who)

        PJ = A[:, 0:NT * IN_COLS].rearrange("p (t n) -> p t n", t=NT)
        o1 = NT * IN_COLS
        Y = A[:, o1:o1 + 4096].rearrange("p (t n) -> p t n", t=NT)
        o2 = o1 + 4096
        R1 = over("HH", "HH_scratch", 0, 4096, F32)
        R2 = over("HL", "HL_scratch", 0, 4096, F32)
        RT = R1.rearrange("p (k t) -> p k t", k=8)
        QT = R2.rearrange("p (k t) -> p k t", k=8)
        KT = A[:, o2:o2 + 2048].rearrange("p (k t) -> p k t", k=4)
        o3 = o2 + 2048
        W3 = A[:, o3:22528]
        assert 22528 - o3 >= 4608
        ROPED = [(RQ + 64 * h) for h in range(8)] + [NQ + 64 * h for h in range(8)] + \
                [KSL, KSL + 64, KWN, KWN + 64]


        def bc(ap, shape):
            return ap.to_broadcast(shape)

        def rope_dve(link):
            for t in range(NT):
                for o, n in ((RQ, 8), (NQ, 8), (KSL, 2), (KWN, 2)):
                    src = PJ[:, t, o:o + n * DK].rearrange("p (h x) -> p h x", x=DK)
                    c = con("cos")[:, t * DK:(t + 1) * DK].unsqueeze(1).to_broadcast([P, n, DK])
                    s = con("sin")[:, t * DK:(t + 1) * DK].unsqueeze(1)
                    a = R1[:, 0:n * DK].rearrange("p (h x) -> p h x", x=DK)
                    b = R2[:, 0:n * DK].rearrange("p (h x) -> p h x", x=DK)
                    nc.vector.tensor_tensor(a, src, c, ALU.mult)
                    nc.vector.tensor_tensor(b[:, :, 0:32], src[:, :, 32:64],
                                            s[:, :, 0:32].to_broadcast([P, n, 32]), ALU.mult)
                    link(nc.vector.tensor_tensor(b[:, :, 32:64], src[:, :, 0:32],
                                                 s[:, :, 32:64].to_broadcast([P, n, 32]), ALU.mult))
                    link(nc.vector.tensor_tensor(src, a, b, ALU.add))

        DEC = W3[:, 0:2048].rearrange("p (h x) -> p h x", h=RH)
        SR = W3[:, 2048:2048 + 2 * 1280].rearrange("p (r x) -> p r x", r=2)
        sr_at = [0, 512, 896, 1152]
        bn6, mv = misc(16 * 6), misc(32)

        BLK = W3[:, 0:1024].rearrange("p (k m) -> p k m", k=16)
        BLHr = over("A", "BLH", o3 + 1024, 1024, F32R).rearrange("p (k m) -> p k m", k=16)
        BLLr = over("A", "BLL", o3 + 2048, 1024, F32R).rearrange("p (k m) -> p k m", k=16)
        BLH = BLHr.bitcast(F32)
        HID = W3[:, 3072:3072 + 512].rearrange("p (f g r n) -> p f g r n", f=2, g=2, r=4)
        HIDK = R1[:, 1024:1152].rearrange("p (f m) -> p f m", f=2)
        DUP = R1[:, 0:1024].rearrange("p (t g j x) -> p t g j x", t=NT, g=2, j=2)
        W2 = W3[:, 3584:3584 + 256].rearrange("p (w f n) -> p w f n", w=2, f=2)
        POS = W3[:, 3840:3840 + 32].rearrange("p (w k) -> p w k", w=2)
        KC = W3[:, 3872:3872 + 192].rearrange("p (a n) -> p a n", a=3)
        KCT = W3[:, 4064:4128]
        VBD = W3[:, 4128:4640].rearrange("p (g r n) -> p g r n", g=2, r=4)
        CT = PJ[:, 0, RQ:RQ + 512], PJ[:, 1, RQ:RQ + 512]
        E4 = R1[:, 0:1024].rearrange("p (t h n) -> p t h n", t=NT, h=NH)
        PTC = R1[:, 1024:2048].rearrange("p (u t) -> p u t", u=8)
        mx4, z4 = misc(32), misc(32)
        gates = misc(NT * 24).rearrange("p (t g h) -> p t g h", t=NT, g=3)
        EX = W3[:, 0:1024].rearrange("p (r x) -> p r x", r=2)
        PT = W3[:, 1024:2048].rearrange("p (r x) -> p r x", r=2)
        OT = W3[:, 2048:3072].rearrange("p (r x) -> p r x", r=2)
        nmax, zsum = misc(64), misc(64)

        units = [(b, t, h) for b in range(2) for t in range(NT) for h in range(NH)]

        GT = A[:, 0:NF * S].rearrange("p (k t) -> p k t", k=NF)
        CV = A[:, NF * S:NF * S + 2048].rearrange("p (r t) -> p r t", r=4)
        GSHr = over("A", "GSH", NF * S + 2048, 2048, F32R).rearrange("p (r t) -> p r t", r=4)
        GSLr = over("A", "GSL", NF * S + 4096, 2048, F32R).rearrange("p (r t) -> p r t", r=4)
        GSH = GSHr.bitcast(F32)

        CA = misc(8)
        CA2r = over("A", "CA2", 0, 32, F32R).rearrange("p (s k n) -> p s k n", s=2, k=NK)
        CABr = over("A", "CAB", 64, 2048, F32R).rearrange("p (s k n) -> p s k n", s=2, k=NK)
        CA2, CAB = CA2r.bitcast(F32), CABr.bitcast(F32)
        CA8 = misc(8)
        MOD = misc(32)
        GB = A[:, 2112:2112 + 2048].rearrange("p (g n) -> p g n", g=2)

        LEVELS = (64, 32, 16, 8, 4, 2, 1)
        def reg(n, k=4):
            return A[:, n * 2048:(n + 1) * 2048].rearrange("p (k t) -> p k t", k=k)

        HQ, HF, HG, HV, CB, CC, CX = (reg(n) for n in range(7))
        HK, SC8, SC9 = reg(7), reg(8), reg(9)
        RST = A[:, 20992:22528]
        LEVEL = RST[:, 0:1024].bitcast(U32).rearrange("p (n t) -> p n t", n=8)
        STATE = RST.rearrange("p (c h n) -> p c h n", c=3, h=4)
        lb, oml, lbt = misc(4), misc(4), misc(12)
        eb = misc(16)

        SS = A[:, 0:8192].rearrange("p (t f n) -> p t f n", t=NT, f=16)
        SUBK = A[:, 8192:10240].rearrange("p (f n) -> p f n", f=16)
        QE = A[:, 10240:11264].rearrange("p (r t) -> p r t", r=2)
        TV = A[:, 16384:17408].rearrange("p (t f k) -> p t f k", t=NT, f=16)
        TIU = A[:, 17408:18432].rearrange("p (t f k) -> p t f k", t=NT, f=16)
        BV = A[:, 18432:18944].rearrange("p (u k) -> p u k", u=32)
        BI = A[:, 18944:19456].rearrange("p (u k) -> p u k", u=32)
        LST = A[:, 20992:22528].rearrange("p (l t) -> p l t", l=3)
        WORK = A[:, 19456:19712]
        CAND = A[:, 19712:19968]
        CAND2 = A[:, 19968:20224]
        PA = A[:, 8192:8704]
        PB = A[:, 8704:9216]
        TF = A[:, 9216:10240].rearrange("p (t f k) -> p t f k", t=NT, f=16)
        EQ = A[:, 10240:12288].rearrange("p (h k a) -> p h k a", h=PH, k=TOPK)
        N1 = A[:, 12288:12800].rearrange("p (t u) -> p t u", t=NT)
        N2 = A[:, 12800:13312].rearrange("p (t u) -> p t u", t=NT)
        zg = misc(32)
        STG = A[:, 0:16384].rearrange("p (i t) -> p i t", i=P)
        OH = A[:, 16384:16384 + 4096].rearrange("p (r s n) -> p r s n", r=16, s=2)
        WGTr = over("A", "WGT", 0, 16384, F32R).rearrange("p (b s i t) -> p b s i t", b=2, s=2, i=GROUP)
        WGT = WGTr.bitcast(F32)
        GR_ = A[:, 16384:18432].rearrange("p (r t) -> p r t", r=4)
        GE = A[:, 18432:19456].rearrange("p (r t) -> p r t", r=2)
        WF = A[:, 19456:20480].rearrange("p (r t) -> p r t", r=2)
        YA = X

        ffc = par("ffconv").rearrange("p (m w) -> p m w", w=3)
        def flat(r):
            return r.rearrange("p k t -> p (k t)")

        def experts(eng, step):
            cx = FIRST["experts"]
            step((cx, 0, 0), 0, 0, True, False)
            with eng.Fori(0, (NGRP - 2) // 2) as i:
                for s in range(2):
                    step((cx + GROUP + 2 * GROUP * s, i, 4 * GROUP), i * (2 * GROUP) + GROUP * (1 + s), (1 + s) % 2,
                         True, True)
            step((cx + GROUP + 2 * GROUP * (NGRP - 2), 0, 0), GROUP * (NGRP - 1), 1, True, True)
            step((cx + GROUP + 2 * GROUP * (NGRP - 1), 0, 0), GROUP * NGRP, 0, False, True)

        block = ctx.enter_context(nc.Block())
        dr = d

        @block.sync
        def _(sp):
            def load(c, src, w=CW):
                v = number(c, 1 - RING)
                wait(sp, "low_done", v)
                dst = RAW[:, slot(c), 0:w]
                if len(src.shape) == 3:
                    dst = dst.rearrange("p (a b) -> p a b", a=src.shape[1])
                sp.dma_start(dst, src).then_inc(sem(f"raw_landed{slot(c)}"), 16)

            win = dr["w_in"].rearrange("(q k p) n -> q p k n", q=4, p=P)
            for b in range(6):
                w = 512 if b < 5 else TAIL
                for q in range(4):
                    load((4 * b + q, 0, 0), win[q, :, :, b * 512:b * 512 + w], 2 * w)
            c0 = FIRST["cmp"]
            for n in range(8):
                load((c0 + n, 0, 0), dr["cmp_w1"][n])
            c0 = FIRST["wout"]
            for k in range(NK):
                load((c0 + k, 0, 0), dr["w_out"][k * P:(k + 1) * P, :])

            def looped(name, n, src, per=4):
                c0 = FIRST[name]
                with sp.Fori(0, n // per) as i:
                    for j in range(per):
                        load((c0 + j, i, per), src(i * per + j))

            looped("up", 2 * NF, lambda m: dr["ffn_up"][m])
            c0 = FIRST["down"]
            for k in range(NF):
                load((c0 + k, 0, 0), dr["ffn_down"][k * P:(k + 1) * P, :])
            looped("ada_t", 32, lambda m: dr["ada_t"][m])
            looped("ada_n", 16, lambda m: dr["ada_n"][m])
            looped("win2", 28, lambda m: dr["win2"][m])
            looped("wout2", 8, lambda m: dr["w_out2"].rearrange("(k p) n -> k p n", p=P)[m])
            looped("query", 16, lambda m: dr["query"][m])
            vv = dr["peer_v"].rearrange("(a g q r) n -> g q a r n", a=P, g=NGRP, r=2)

            def step(c, g8, b, u, v):
                n = 0
                g = g8 // GROUP if isinstance(g8, int) else group_of(c)
                for half in range(2):
                    if u:
                        for m in range(4 * half, 4 * half + 4):
                            load(plus(c, n), dr["peer_u"][g8 + m])
                            n += 1
                    if v:
                        for q in range(4):
                            load(plus(c, n), vv[g - 1, q][:, :, half * 512:(half + 1) * 512])
                            n += 1

            def group_of(c):
                return c[1] * 2 + (c[0] - FIRST["experts"] + GROUP) // (2 * GROUP)
            experts(sp, step)

        @block.gpsimd
        def _(pool):
            xt = dr["x"].rearrange("(t p) n -> p t n", p=P)
            pool.dma_start(X, xt).then_inc(sem("x_landed"), 16)
            pool.dma_start(CON[:, :], dr["const"]).then_inc(sem("const_landed"), 16)
            pool.dma_start(PAR[:, :], dr["param"]).then_inc(sem("param_landed"), 16)
            pool.dma_start(ROW[:, :], dr["nm_post"].partition_broadcast(P)).then_inc(sem("row_landed"), 16)
            pool.wait_ge(sem("phase_ended"), 3 * 2)
            pool.dma_start(DEC, dr["decay"].rearrange("p (h x) -> p h x", h=RH)).then_inc(sem("decay_landed"), 16)
            pool.wait_ge(sem("phase_ended"), 3 * 4)
            pool.dma_start(W2, dr["cmp_w2"].rearrange("w (f p) n -> p w f n", p=P)).then_inc(sem("w2_landed"), 16)
            pool.dma_start(POS, dr["cmp_pos"]).then_inc(sem("w2_landed"), 16)
            pool.wait_ge(sem("phase_ended"), 3 * 10)
            pool.dma_start(ROW[:, :], dr["nf_post"].partition_broadcast(P)).then_inc(sem("row_landed"), 16)
            pool.wait_ge(sem("phase_ended"), 3 * 14)
            for g in range(2):
                pool.dma_start(GB[:, g, :], dr["bada_gate"][g].partition_broadcast(P)).then_inc(sem("gb_landed"), 16)
            pool.dma_start(ROW[:, :], dr["final_w"].partition_broadcast(P)).then_inc(sem("row_landed"), 16)
            pool.wait_ge(sem("phase_ended"), 3 * 16)
            pool.dma_start(RST[:, 0:1024], dr["levels"].bitcast(F32)).then_inc(sem("levels_landed"), 16)
            pool.wait_ge(sem("phase_ended"), 3 * 21)
            pool.dma_start(dr["x3"], X).then_inc(sem("x3_saved"), 16)
            pool.dma_start(SUBK, dr["subk"]).then_inc(sem("subkeys_landed"), 16)
            pool.wait_ge(sem("phase_ended"), 3 * 26)
            pool.dma_start(XN, dr["x3"]).then_inc(sem("x3_back"), 16)
            pool.wait_ge(sem("x3_back"), 16)
            pool.wait_ge(sem("out_ready"), NT)
            pool.dma_start(dr["out"].rearrange("(t p) n -> p t n", p=P), X).then_inc(sem("out_landed"), 16)
            pool.wait_ge(sem("out_landed"), 16)
            pool.wait_ge(sem("gates_written"), 16 * NT)

        @block.scalar
        def _(act):
            link = link_for(act, "act_step")
            for n in range(LEAD):
                split_high(act, (n, 0, 0))
            act.wait_ge(sem("const_landed"), 16)
            act.wait_ge(sem("param_landed"), 16)
            act.wait_ge(sem("x_landed"), 16)
            norm_turn(act, "act", "pre1", link)
            for b in range(6):
                w = 512 if b < 5 else TAIL
                for q in range(4):
                    n = 4 * b + q + LEAD
                    split_high(act, (n, 0, 0), CW if n < 20 or n >= 24 else 2 * TAIL)
                act.wait_ge(sem("chunk_used"), 4 * b + 4)
                for t in range(NT):
                    last = nc.scalar.activation(PJ[:, t, b * 512:b * 512 + w], PS[:, 4 * (b % 2) + t, 0:w], ACT.Copy)
                last.then_inc(sem("proj_stored"), 1)
            barrier(act, "act")
            nc.scalar.activation(gates.rearrange("p t g h -> p t (g h)"), PJ[:, :, NG:NG + 24], ACT.Sigmoid)
            link(nc.scalar.activation(PJ[:, :, RG:RG + 512], PJ[:, :, RG:RG + 512], ACT.Silu))
            barrier(act, "act")
            for n in range(20):
                act.wait_ge(sem("head_turned"), n + 1)
                dst = RT[0:64, n, :] if n < 8 else QT[0:64, n - 8, :] if n < 16 else KT[0:64, n - 16, :]
                nc.scalar.activation(dst, PS[0:64, n % 8, :], ACT.Copy,
                                     scale=DK ** -0.5 if 8 <= n < 16 else 1.0).then_inc(sem("head_stored"), 1)
            act.wait_ge(sem("gn_var"), 1)
            nc.scalar.activation(mv.rearrange("p (u s) -> p u s", s=2)[:, :, 1], mv.rearrange("p (u s) -> p u s", s=2)[:, :, 1],
                                 ACT.Sqrt).then_inc(sem("gn_root"), 1)
            barrier(act, "act")
            for w in range(2):
                act.wait_ge(sem("cmp_turned"), w + 1)
                for g in range(2):
                    last = nc.scalar.activation(CT[g], PS[:, g, :], ACT.Copy)
                last.then_inc(sem("cmp_stored"), 1)
                act.wait_ge(sem("blk_ready"), w + 1)
                nc.scalar.activation(BLHr, BLK, ACT.Copy).then_inc(sem("blk_high"), 1)
                for q in range(4):
                    split_high(act, (FIRST["cmp"] + 4 * w + q + LEAD, 0, 0))
                act.wait_ge(sem("chunk_used"), FIRST["cmp"] + 4 * w + 4)
                for f in range(2):
                    for g in range(2):
                        src = PS[:, 2 + f, 32 * g:32 * g + 32]
                        if w == 0:
                            last = nc.scalar.activation(HIDK[:, f, 32 * g:32 * g + 32], src, ACT.Gelu_apprx_tanh)
                        else:
                            last = nc.scalar.activation(HID[:, f, g], src.unsqueeze(1).to_broadcast([P, 4, 32]),
                                                        ACT.Gelu_apprx_tanh)
                last.then_inc(sem("hid_gelu"), 1)
            barrier(act, "act")
            act.wait_ge(sem("cmp_shifted"), 1)
            nc.scalar.activation(E4, E4, ACT.Exp).then_inc(sem("cmp_exp"), 1)
            act.wait_ge(sem("cmp_pt"), 1)
            for n in range(2):
                last = nc.scalar.activation(PTC[:, 4 * n:4 * n + 4, :], PS[:, 4 + n, :].rearrange("p (a b) -> p a b", a=4), ACT.Copy)
            last.then_inc(sem("cmp_pt_stored"), 1)
            barrier(act, "act")
            for s in range(len(units) + 1):
                if s < len(units):
                    b, t, h = units[s]
                    w = (t + 1) * P
                    act.wait_ge(sem("at_max"), s + 1)
                    wait(act, "at_turned", s - 1)
                    nc.scalar.activation(EX[:, s % 2, 0:w], PS[:, s % 2, 0:w], ACT.Exp, bias=nmax[:, s:s + 1],
                                         accum_out=zsum[:, s:s + 1]).then_inc(sem("at_exp"), 1)
                u = s - 1
                if u >= 0 and u % 2 == 0:
                    w = (units[u][1] + 1) * P
                    act.wait_ge(sem("at_turned"), u + 1)
                    wait(act, "at_pv", u - 1)
                    nc.scalar.activation(PT[:, u % 2, 0:w], PS[:, 2 + u % 2, 0:w], ACT.Copy).then_inc(sem("at_stored0"), 1)
            barrier(act, "act")
            turn_act(act, "mix")
            barrier(act, "act")
            for k in range(NK):
                split_high(act, (FIRST["wout"] + k + LEAD, 0, 0))
            add_normed(act, "act", "mixpost", link)
            norm_turn(act, "act", "pre2", link)
            nc.scalar.preload_act_table(ACT.Gelu_apprx_tanh)
            cu = FIRST["up"]
            with act.Fori(0, NF // 2) as i:
                for j in range(4):
                    split_high(act, (cu + j + LEAD, i, 4))
                    act.wait_ge(sem("chunk_used"), i * 4 + (cu + j + 1))
                    act.wait_ge(sem("up_free"), i * 4 + (j + 1))
                    nc.scalar.activation(CV[:, j, :], PS[:, j, :], ACT.Copy,
                                         scale=ffc[:, i * 4 + j, 2:3]).then_inc(sem("up_tap"), 1)
                    if j % 2 == 1:
                        act.wait_ge(sem("up_conv"), i * 4 + j)
                        nc.scalar.activation(CV[:, j - 1, :], CV[:, j - 1, :], ACT.Gelu_apprx_tanh)\
                            .then_inc(sem("up_gelu"), 1)
            barrier(act, "act")
            for k in range(NF):
                if k == 0:
                    for m in range(3):
                        nc.scalar.activation(GSHr[:, m, :], GT[:, m, :], ACT.Copy).then_inc(sem("gt_high"), 1)
                c = FIRST["down"] + k
                split_high(act, (c + LEAD, 0, 0))
                if k + 3 < NF:
                    act.wait_ge(sem("chunk_used"), c)
                    nc.scalar.activation(GSHr[:, (k + 3) % 4, :], GT[:, k + 3, :], ACT.Copy)\
                        .then_inc(sem("gt_high"), 1)
            add_normed(act, "act", "ffpost", link)
            act.wait_ge(sem("lb_shifted"), 1)
            nc.scalar.activation(lbt[:, 4:12], lbt[:, 4:12], ACT.Exp).then_inc(sem("lb_exp"), 1)
            link(nc.scalar.activation(CA, par("c"), ACT.Silu))
            nc.scalar.activation(CA2r[:, 0], CA.unsqueeze(2).to_broadcast([P, NK, 2]), ACT.Copy)
            nc.scalar.activation(CABr[:, 0], CA.unsqueeze(2).to_broadcast([P, NK, P]), ACT.Copy)\
                .then_inc(sem("ca_high"), 1)
            nc.scalar.preload_act_table(ACT.Copy)
            c0 = FIRST["ada_t"]
            with act.Fori(0, 48 // 4) as i:
                for j in range(4):
                    split_high(act, (c0 + j + LEAD, i, 4))
            barrier(act, "act")
            norm_turn(act, "act", "pre3", link)
            c0 = FIRST["win2"]
            for m in range(24):
                split_high(act, (c0 + m + LEAD, 0, 0))
                kind, n = m // 4, m % 4
                act.wait_ge(sem("chunk_used"), c0 + m + 1)
                src = PS[:, m % 4, :]
                if kind == 0:
                    ins = nc.scalar.activation(HQ[:, n, :], src, ACT.Copy)
                elif kind == 1:
                    nc.scalar.activation(HF[:, n, :], src, ACT.Sigmoid)
                    ins = nc.scalar.activation(HK[:, n, :], src, ACT.Sigmoid, scale=-1.0)
                elif kind == 2:
                    ins = nc.scalar.activation(HG[:, n, :], src, ACT.Silu)
                else:
                    ins = nc.scalar.activation((CB, CC, CX)[kind - 3][:, n, :], src, ACT.Copy)
                ins.then_inc(sem("p2_stored"), 1)
            for m in range(24, 28):
                split_high(act, (c0 + m + LEAD, 0, 0))
            act.wait_ge(sem("chunk_used"), c0 + 28)
            for t in range(NT):
                nc.scalar.activation(HV[:, t, :], PS[:, 4 + t, :], ACT.Copy)
            barrier(act, "act")
            act.wait_ge(sem("f_ready"), 1)
            nc.scalar.activation(HF, HF, ACT.Ln).then_inc(sem("logf"), 1)
            act.wait_ge(sem("cv_done"), 1)
            nc.scalar.activation(CC, CB, ACT.Square).then_inc(sem("cv_sq"), 1)
            act.wait_ge(sem("cv_mean"), 1)
            nc.scalar.activation(CC, CC, ACT.Sqrt).then_inc(sem("cv_root"), 1)
            barrier(act, "act")
            for n, m in enumerate(LEVELS):
                act.wait_ge(sem("lv_diff"), n + 1)
                e = flat(CC).rearrange("p (b s m) -> p b s m", s=2, m=m)
                nc.scalar.activation(e[:, :, 0, :], e[:, :, 0, :], ACT.Exp, scale=-1.0)
                nc.scalar.activation(e[:, :, 1, :], e[:, :, 1, :], ACT.Exp).then_inc(sem("lv_exp"), 1)
            barrier(act, "act")
            nc.scalar.activation(CC, CX, ACT.Exp)
            nc.scalar.activation(eb, flat(CX)[:, 127::128], ACT.Exp)
            act.wait_ge(sem("dk_diff"), 1)
            nc.scalar.activation(SC9, SC9, ACT.Exp).then_inc(sem("dk_exp"), 1)
            act.wait_ge(sem("kd_turned"), 1)
            for h in range(4):
                last = nc.scalar.activation(SC8[:, h, 0:384], PS[:, 4 + h, 0:384], ACT.Copy)
            last.then_inc(sem("kd_stored"), 1)
            act.wait_ge(sem("o_done"), 1)
            nc.scalar.activation(SC9, PS[:, 0:4, :], ACT.Square).then_inc(sem("o_sq"), 1)
            act.wait_ge(sem("o_mean"), 1)
            nc.scalar.activation(SC9, SC9, ACT.Sqrt).then_inc(sem("o_root"), 1)
            act.wait_ge(sem("y2_ready"), 1)
            nc.scalar.activation(HHr[:, 0:4, :], SC8, ACT.Copy)
            nc.scalar.activation(HHr[:, 4:8, :], CB, ACT.Copy).then_inc(sem("y2_high"), 1)
            barrier(act, "act")
            for k in range(NK):
                split_high(act, (FIRST["wout2"] + k + LEAD, 0, 0))
            barrier(act, "act")
            norm_turn(act, "act", "pre4", link)
            c0 = FIRST["query"]
            for m in range(17):
                if m < 16:
                    split_high(act, (c0 + m + LEAD, 0, 0))
                    act.wait_ge(sem("chunk_used"), c0 + m + 1)
                    wait(act, "keys_scored", m - 1)
                    nc.scalar.activation(QE[:, m % 2, :], PS[:, m % 4, :], ACT.Copy).then_inc(sem("query_stored"), 1)
                if m >= 1:
                    n = m - 1
                    act.wait_ge(sem("keys_scored"), n + 1)
                    nc.scalar.activation(SS[:, :, n, :], PS[:, 4 + n % 4, :].rearrange("p (t n) -> p t n", t=NT),
                                         ACT.Copy).then_inc(sem("scores_stored"), 1)
            barrier(act, "act")
            act.wait_ge(sem("best_shifted"), 1)
            nc.scalar.activation(BV, BV, ACT.Exp).then_inc(sem("best_exp"), 1)
            for n in range(3):
                act.wait_ge(sem("list_turned"), n + 1)
                nc.scalar.activation(LST[:, n, :], PS[:, n, :], ACT.Copy)
            barrier(act, "act")
            act.sem_inc(sem("gm_stored"), 4)
            for t in range(NT):
                wait(act, "gates_written", 16 * t)
                with act.Fori(0, 8) as i:
                    for q in range(4):
                        act.wait_ge(sem("gm_ready"), i * 4 + (32 * t + q + 5))
                        dst = STG.rearrange("p i t -> p t i")[:, bass.ds(i * 16 + 4 * q, 4), :]
                        nc.scalar.activation(dst, PS[:, q, :].rearrange("p (t n) -> p t n", t=4), ACT.Copy)\
                            .then_inc(sem("gm_stored"), 1)
                act.wait_ge(sem("gm_stored"), 32 * (t + 1) + 4)
                act.dma_start(dr["gate_matrices"][:, :, t * P:(t + 1) * P], STG).then_inc(sem("gates_written"), 16)
            barrier(act, "act")
            cx = FIRST["experts"]
            nc.scalar.preload_act_table(ACT.Gelu)
            act.sem_inc(sem("gelu_done"), 4)

            def load_gates(e, m):
                act.dma_start(GR_[:, m % 4, :], dr["gate_matrices"][:, e, :]).then_inc(sem(f"gates_landed{m % 4}"), 16)

            def high(e, m, b):
                act.wait_ge(sem("w_done"), e + 3)
                nc.scalar.activation(WGTr[:, b, 0, m, :], WF[:, m % 2, :], ACT.Copy).then_inc(sem("w_high"), 1)
                if not (isinstance(e, int) and e + 4 >= P):
                    load_gates(e + 4, m)

            act.wait_ge(sem("gates_written"), 16 * NT)
            for m in range(4):
                load_gates(m, m)

            def step(c, g8, b, u, v):
                n = 0
                for half in range(2):
                    if u:
                        for m in range(4 * half, 4 * half + 4):
                            split_high(act, plus(c, n + LEAD))
                            act.wait_ge(sem("chunk_used"), number(c, n + 1))
                            act.wait_ge(sem("w_done"), g8 + (m + 1))
                            nc.scalar.activation(GE[:, m % 2, :], PS[:, 4 + m % 4, :], ACT.Gelu)\
                                .then_inc(sem("gelu_done"), 1)
                            high(g8 + m, m, b)
                            n += 1
                    if v:
                        for q in range(4):
                            split_high(act, plus(c, n + LEAD))
                            n += 1
            experts(act, step)
            barrier(act, "act")
            act.wait_ge(sem("x4_ready"), 1)
            rms_act(act, link, lambda t: X[:, t, :], "final")

        @block.vector
        def _(dve):
            link = link_for(dve, "dve_step")
            for n in range(LEAD):
                split_low(dve, (n, 0, 0))
            dve.wait_ge(sem("param_landed"), 16)
            dve.wait_ge(sem("x_landed"), 16)
            norm_turn(dve, "dve", "pre1", link, lambda k: par("nmp", k, k + 1))
            for b in range(6):
                for q in range(4):
                    n = 4 * b + q + LEAD
                    split_low(dve, (n, 0, 0), CW if n < 20 or n >= 24 else 2 * TAIL)
            barrier(dve, "dve")
            rope_dve(link)
            barrier(dve, "dve")
            dve.wait_ge(sem("decay_landed"), 16)
            for u in range(4 * RH):
                h, j = u // 4, u % 4
                w = S - j * P
                dve.wait_ge(sem("rt_scores"), u + 1)
                if j == 0:
                    wait(dve, "rt_out", h - 1)
                nc.vector.tensor_tensor(SR[:, h % 2, sr_at[j]:sr_at[j] + w], PS[:, u % 4, 0:w], DEC[:, h, 0:w],
                                        ALU.mult).then_inc(sem("rt_decayed"), 1)
            dve.wait_ge(sem("rt_out"), RH)
            for t in range(NT):
                for h in range(RH):
                    u = t * 4 + h
                    last = nc.vector.bn_stats(bn6[:, 6 * u:6 * u + 6], PS[:, 4 + t, h * P:(h + 1) * P])
            link(last)
            for u in range(16):
                last = nc.vector.bn_aggr(mv[:, 2 * u:2 * u + 2], bn6[:, 6 * u:6 * u + 6])
            link(last)
            var = mv.rearrange("p (u s) -> p u s", s=2)[:, :, 1]
            nc.vector.tensor_scalar(var, var, GN_EPS, None, ALU.add).then_inc(sem("gn_var"), 1)
            dve.wait_ge(sem("gn_root"), 1)
            link(nc.vector.reciprocal(var, var))
            for t in range(NT):
                for h in range(RH):
                    u = t * 4 + h
                    link(nc.vector.tensor_scalar(Y[:, t, h * P:(h + 1) * P], PS[:, 4 + t, h * P:(h + 1) * P],
                                                 mv[:, 2 * u:2 * u + 1], mv[:, 2 * u + 1:2 * u + 2],
                                                 ALU.subtract, ALU.mult))
                link(nc.vector.tensor_tensor(Y[:, t, 0:512], Y[:, t, 0:512], PJ[:, t, RG:RG + 512], ALU.mult))
            barrier(dve, "dve")
            dve.wait_ge(sem("w2_landed"), 32)
            for w in range(2):
                o = (KCM, VCM)[w]
                for t in range(NT):
                    src = PJ[:, t, o:o + 128].rearrange("p (g x) -> p g x", g=2).unsqueeze(2).to_broadcast([P, 2, 2, 64])
                    last = nc.vector.tensor_copy(DUP[:, t], src)
                last.then_inc(sem("cmp_dup"), 1)
                link(nc.vector.memset(BLK, 0.0))
                dve.wait_ge(sem("cmp_stored"), w + 1)
                for jj in range(2):
                    for g in range(2):
                        ps = slice(64 * jj, 64 * jj + 64)
                        for half in range(2):
                            src = CT[g][ps, :].rearrange("p (n k j) -> p k n j", k=8, j=2)[:, :, half:half + 31, jj]
                            last = nc.vector.tensor_tensor(
                                BLK[ps, 8 * half:8 * half + 8, 32 * g:32 * g + 31], src,
                                POS[ps, w, 8 * half:8 * half + 8].unsqueeze(2).to_broadcast([64, 8, 31]), ALU.add)
                last.then_inc(sem("blk_ready"), 1)
                dve.wait_ge(sem("blk_high"), w + 1)
                nc.vector.tensor_tensor(BLLr, BLK, BLH, ALU.subtract).then_inc(sem("blk_low"), 1)
                for q in range(4):
                    split_low(dve, (FIRST["cmp"] + 4 * w + q + LEAD, 0, 0))
                if w == 0:
                    dve.wait_ge(sem("kc_ready"), 1)
                    src = PS[0:64, 4, 0:64]
                    link(nc.vector.tensor_copy(KC[0:64, 0, :], src))
                    nc.vector.tensor_tensor(KC[0:64, 1, :], KC[0:64, 0, :], con("ccos")[0:64, :], ALU.mult)
                    nc.vector.tensor_tensor(KC[0:64, 2, 0:32], KC[0:64, 0, 32:64], con("csin")[0:64, 0:32], ALU.mult)
                    link(nc.vector.tensor_tensor(KC[0:64, 2, 32:64], KC[0:64, 0, 0:32], con("csin")[0:64, 32:64], ALU.mult))
                    nc.vector.tensor_tensor(KC[0:64, 0, :], KC[0:64, 1, :], KC[0:64, 2, :], ALU.add)\
                        .then_inc(sem("kc_roped"), 1)
                    dve.wait_ge(sem("kct_ready"), 1)
                    nc.vector.tensor_copy(KCT[0:64, :], PS[0:64, 5, 0:64]).then_inc(sem("kct_stored"), 1)
                else:
                    dve.wait_ge(sem("vc_ready"), 1)
                    for g in range(2):
                        last = nc.vector.tensor_tensor(
                            VBD[:, g], PS[:, 6 + g, 0:64].unsqueeze(1).to_broadcast([P, 4, 64]),
                            con("four").unsqueeze(2).to_broadcast([P, 4, 64]), ALU.mult)
                    link(last)
            barrier(dve, "dve")
            dve.wait_ge(sem("cs_ready"), 1)
            sc = PS[:, 0:4, 0:256].rearrange("p t (h n) -> p t h n", h=NH)
            ok = con("cmp_ok").rearrange("p (t n) -> p t n", t=NT)
            no = con("cmp_no").rearrange("p (t n) -> p t n", t=NT)
            for t in range(NT):
                last = nc.vector.tensor_tensor(E4[:, t], sc[:, t], ok[:, t].unsqueeze(1).to_broadcast([P, NH, 32]), ALU.mult)
            link(last)
            for t in range(NT):
                last = nc.vector.tensor_tensor(E4[:, t], E4[:, t], no[:, t].unsqueeze(1).to_broadcast([P, NH, 32]), ALU.add)
            link(last)
            E4f = E4.rearrange("p t h n -> p (t h) n")
            link(nc.vector.tensor_reduce(mx4, E4f, AX, ALU.max))
            nc.vector.tensor_tensor(E4f, E4f, mx4.unsqueeze(2).to_broadcast([P, 32, 32]), ALU.subtract)\
                .then_inc(sem("cmp_shifted"), 1)
            dve.wait_ge(sem("cmp_exp"), 1)
            for t in range(NT):
                last = nc.vector.tensor_tensor(E4[:, t], E4[:, t], ok[:, t].unsqueeze(1).to_broadcast([P, NH, 32]), ALU.mult)
            link(last)
            link(nc.vector.tensor_reduce(z4, E4f, AX, ALU.add))
            link(nc.vector.tensor_scalar(z4, z4, 1e-30, None, ALU.max))
            link(nc.vector.reciprocal(z4, z4))
            nc.vector.tensor_tensor(E4f, E4f, z4.unsqueeze(2).to_broadcast([P, 32, 32]), ALU.mult)\
                .then_inc(sem("cmp_probs"), 1)
            dve.wait_ge(sem("cmp_out"), 1)
            for t in range(NT):
                last = nc.vector.tensor_tensor(
                    Y[:, t, 512:1024].rearrange("p (h n) -> p h n", h=NH), PS[:, t, :].rearrange("p (h n) -> p h n", h=NH),
                    gates[:, t, 0, :].unsqueeze(2).to_broadcast([P, NH, DK]), ALU.mult)
            link(last)
            barrier(dve, "dve")
            for s in range(len(units) + 2):
                if s < len(units):
                    b, t, h = units[s]
                    w = (t + 1) * P
                    dve.wait_ge(sem("at_scores"), s + 1)
                    link(nc.vector.tensor_tensor(PS[:, s % 2, w - P:w], PS[:, s % 2, w - P:w], con("causal"), ALU.add))
                    nc.vector.tensor_reduce(nmax[:, s:s + 1], PS[:, s % 2, 0:w], AX, ALU.max, negate=True)\
                        .then_inc(sem("at_max"), 1)
                u = s - 1
                if 0 <= u < len(units) and u % 2 == 1:
                    w = (units[u][1] + 1) * P
                    dve.wait_ge(sem("at_turned"), u + 1)
                    wait(dve, "at_pv", u - 1)
                    nc.vector.tensor_copy(PT[:, u % 2, 0:w], PS[:, 2 + u % 2, 0:w]).then_inc(sem("at_stored1"), 1)
                u = s - 2
                if u >= 0 and u % 8 == 7:
                    b, t, _ = units[u]
                    n = u // 8
                    dve.wait_ge(sem("at_pv"), u + 1)
                    zs = zsum[:, 8 * n:8 * n + 8]
                    link(nc.vector.reciprocal(zs, zs))
                    link(nc.vector.tensor_tensor(zs, zs, gates[:, t, 1 + b, :], ALU.mult))
                    ot = OT[:, n % 2, :].rearrange("p (h n) -> p h n", h=NH)
                    nc.vector.tensor_tensor(ot, PS[:, 4 + n % 2, :].rearrange("p (h n) -> p h n", h=NH),
                                            zs.unsqueeze(2).to_broadcast([P, NH, DK]), ALU.mult)\
                        .then_inc(sem("at_taken"), 1)
                    dve.wait_ge(sem("at_taken"), n + 1)
                    link(nc.vector.tensor_tensor(Y[:, t, 512:1024], Y[:, t, 512:1024], OT[:, n % 2, :], ALU.add))
            barrier(dve, "dve")
            turn_dve(dve, link, "mix", lambda k: par("gn", k, k + 1) if k < 4 else None)
            barrier(dve, "dve")
            for k in range(NK):
                split_low(dve, (FIRST["wout"] + k + LEAD, 0, 0))
            add_normed(dve, "dve", "mixpost", link)
            norm_turn(dve, "dve", "pre2", link, lambda k: par("nfp", k, k + 1))
            cu = FIRST["up"]
            for j in range(4):
                nc.vector.memset(CV[:, j, 0:1], 0.0).then_inc(sem("up_free"), 1)
            with dve.Fori(0, NF // 2) as i:
                for j in range(4):
                    split_low(dve, (cu + j + LEAD, i, 4))
                    dve.wait_ge(sem("up_tap"), i * 4 + (j + 1))
                    nc.vector.scalar_tensor_tensor(CV[:, j, 1:], PS[:, j, 0:S - 1], ffc[:, i * 4 + j, 1:2], CV[:, j, 1:],
                                                   ALU.mult, ALU.add).then_inc(sem("up_mid"), 1)
                    dve.wait_ge(sem("up_mid"), i * 4 + (j + 1))
                    nc.vector.scalar_tensor_tensor(CV[:, j, 2:], PS[:, j, 0:S - 2], ffc[:, i * 4 + j, 0:1], CV[:, j, 2:],
                                                   ALU.mult, ALU.add).then_inc(sem("up_conv"), 1)
                    if j % 2 == 1:
                        dve.wait_ge(sem("up_conv"), i * 4 + (j + 1))
                        dve.wait_ge(sem("up_gelu"), i * 2 + (j // 2 + 1))
                        nc.vector.tensor_tensor(GT[:, i * 2 + j // 2, :], CV[:, j - 1, :], CV[:, j, :], ALU.mult)\
                            .then_inc(sem("up_free"), 2)
            barrier(dve, "dve")
            for k in range(NF):
                if k == 0:
                    for m in range(3):
                        dve.wait_ge(sem("gt_high"), m + 1)
                        nc.vector.tensor_tensor(GSLr[:, m, :], GT[:, m, :], GSH[:, m, :], ALU.subtract)\
                            .then_inc(sem("gt_low"), 1)
                c = FIRST["down"] + k
                split_low(dve, (c + LEAD, 0, 0))
                if k + 3 < NF:
                    m = k + 3
                    dve.wait_ge(sem("gt_high"), m + 1)
                    nc.vector.tensor_tensor(GSLr[:, m % 4, :], GT[:, m, :], GSH[:, m % 4, :], ALU.subtract)\
                        .then_inc(sem("gt_low"), 1)
            add_normed(dve, "dve", "ffpost", link)
            l0, l1 = par("lb0"), par("lb1")
            link(nc.vector.tensor_tensor(lbt[:, 0:4], l0, l1, ALU.max))
            nc.vector.tensor_tensor(lbt[:, 4:8], l0, lbt[:, 0:4], ALU.subtract)
            nc.vector.tensor_tensor(lbt[:, 8:12], l1, lbt[:, 0:4], ALU.subtract).then_inc(sem("lb_shifted"), 1)
            dve.wait_ge(sem("lb_exp"), 1)
            link(nc.vector.tensor_tensor(lbt[:, 0:4], lbt[:, 4:8], lbt[:, 8:12], ALU.add))
            link(nc.vector.reciprocal(lbt[:, 0:4], lbt[:, 0:4]))
            link(nc.vector.tensor_tensor(lb, lbt[:, 4:8], lbt[:, 0:4], ALU.mult))
            link(nc.vector.tensor_scalar(oml, lb, -1.0, 1.0, ALU.mult, ALU.add))
            dve.wait_ge(sem("ca_high"), 1)
            nc.vector.tensor_tensor(CA2r[:, 1], CA.unsqueeze(2).to_broadcast([P, NK, 2]), CA2[:, 0], ALU.subtract)
            nc.vector.tensor_tensor(CABr[:, 1], CA.unsqueeze(2).to_broadcast([P, NK, P]), CAB[:, 0], ALU.subtract)\
                .then_inc(sem("ca_low"), 1)
            c0 = FIRST["ada_t"]
            with dve.Fori(0, 48 // 4) as i:
                for j in range(4):
                    split_low(dve, (c0 + j + LEAD, i, 4))
            dve.wait_ge(sem("chunk_used"), c0 + 48)
            dve.wait_ge(sem("gb_landed"), 32)
            mod = PS[:, 0, 0:64].rearrange("p (c n) -> p c n", n=2)[:, :, 0]
            nc.vector.tensor_tensor(MOD[:, 0:16], mod[:, 0:16], par("bada", 0, 16), ALU.add)
            link(nc.vector.tensor_tensor(MOD[:, 16:32], mod[:, 16:32], par("bada", 24, 40), ALU.add))
            for g, w in enumerate(("n1", "n2")):
                sc = MOD[:, 16 * g + 8:16 * g + 16]
                link(nc.vector.scalar_tensor_tensor(sc, sc, 1.0, par(w), ALU.add, ALU.mult))
                nc.vector.tensor_tensor(GATE[:, g, :].rearrange("p (a b) -> p a b", a=2), PS[:, 4 + 2 * g:6 + 2 * g, :],
                                        GB[:, g, :].rearrange("p (a b) -> p a b", a=2), ALU.add)
            barrier(dve, "dve")
            norm_turn(dve, "dve", "pre3", link, lambda k: MOD[:, 8 + k:9 + k], lambda k: MOD[:, k:k + 1])
            for m in range(28):
                split_low(dve, (FIRST["win2"] + m + LEAD, 0, 0))
            barrier(dve, "dve")
            for h in range(4):
                last = nc.vector.tensor_scalar(HF[:, h, :], HF[:, h, :], oml[:, h:h + 1], lb[:, h:h + 1], ALU.mult, ALU.add)
            last.then_inc(sem("f_ready"), 1)
            for h in range(4):
                nc.vector.tensor_scalar(HK[:, h, :], HK[:, h, :], oml[:, h:h + 1], None, ALU.mult)
            link(nc.vector.tensor_tensor(CC, CC, CX, ALU.mult))
            cw = par("conv").rearrange("p (n w) -> p n w", w=3)
            for n in range(4):
                link(nc.vector.tensor_scalar(CX[:, n, :], CC[:, n, :], cw[:, n, 2:3], None, ALU.mult))
                for w in (1, 0):
                    d_ = 2 - w
                    link(nc.vector.scalar_tensor_tensor(CX[:, n, d_:], CC[:, n, 0:S - d_], cw[:, n, w:w + 1], CX[:, n, d_:],
                                                        ALU.mult, ALU.add))
            nc.vector.tensor_tensor(CB, CB, CX, ALU.mult).then_inc(sem("cv_done"), 1)
            dve.wait_ge(sem("cv_sums"), 1)
            nc.vector.tensor_scalar(CC, PS[:, 0:4, :], 1.0 / P, EPS, ALU.mult, ALU.add).then_inc(sem("cv_mean"), 1)
            dve.wait_ge(sem("logf"), 1)
            dve.wait_ge(sem("cv_done"), 1)
            link(nc.vector.memset(SC8, 1.0))
            link(nc.vector.memset(flat(SC8)[:, 0::P], 0.0))
            link(nc.vector.tensor_tensor_scan(flat(CX), flat(SC8), flat(HF), 0.0, ALU.mult, ALU.add))
            dve.wait_ge(sem("cv_root"), 1)
            link(nc.vector.reciprocal(CC, CC))
            for n in range(4):
                link(nc.vector.scalar_tensor_tensor(CB[:, n, :], CB[:, n, :], par("conorm", n, n + 1), CC[:, n, :],
                                                    ALU.mult, ALU.mult))
            link(nc.vector.memset(HF, 0.0))
            link(nc.vector.memset(SC8, 0.0))
            link(nc.vector.memset(SC9, 0.0))
            barrier(dve, "dve")
            dve.wait_ge(sem("levels_landed"), 16)
            ST = HF

            def take(n):
                for h in range(4):
                    dve.wait_ge(sem("lv_scores"), 4 * n + h + 1)
                    last = nc.vector.copy_predicated(
                        ST[:, h, :].rearrange("p (c t) -> p c t", c=4),
                        LEVEL[:, n, :].unsqueeze(1).to_broadcast([P, 4, P]),
                        PS[:, 4 * (n % 2) + h, :].rearrange("p (c t) -> p c t", c=4))
                    last.then_inc(sem("lv_taken"), 1)
                dve.wait_ge(sem("lv_taken"), 4 * n + 4)

            for n, m in enumerate(LEVELS):
                b = flat(CX).rearrange("p (b x) -> p b x", x=2 * m)
                e = flat(CC).rearrange("p (b x) -> p b x", x=2 * m)
                nc.vector.tensor_tensor(e, b, b[:, :, m - 1:m].to_broadcast([P, S * 4 // (2 * m), 2 * m]), ALU.subtract)\
                    .then_inc(sem("lv_diff"), 1)
                if n >= 2:
                    take(n - 2)
                wait(dve, "lv_scores", 4 * n)
                dve.wait_ge(sem("lv_exp"), n + 1)
                view = lambda r: flat(r).rearrange("p (b s m) -> p b s m", s=2, m=m)
                nc.vector.tensor_tensor(view(SC8)[:, :, 1, :], view(HQ)[:, :, 1, :], view(CC)[:, :, 1, :], ALU.mult)
                nc.vector.tensor_tensor(view(SC9)[:, :, 0, :], view(HK)[:, :, 0, :], view(CC)[:, :, 0, :], ALU.mult)\
                    .then_inc(sem("lv_ready"), 1)
                dve.wait_ge(sem("lv_ready"), n + 1)
            for n in range(5, 8):
                take(n)
            b = flat(CX).rearrange("p (b x) -> p b x", x=P)
            nc.vector.tensor_tensor(flat(SC9).rearrange("p (b x) -> p b x", x=P), b[:, :, P - 1:P].to_broadcast([P, 16, P]), b,
                                    ALU.subtract).then_inc(sem("dk_diff"), 1)
            barrier(dve, "dve")
            dve.wait_ge(sem("dk_exp"), 1)
            nc.vector.tensor_tensor(SC9, SC9, HK, ALU.mult).then_inc(sem("kd_ready"), 1)
            nc.vector.tensor_tensor(CC, CC, HQ, ALU.mult).then_inc(sem("qx_ready"), 1)
            for c in range(3):
                dve.wait_ge(sem("kv_ready"), c + 1)
                for h in range(4):
                    ps = PS[:, 4 + c, h * P:(h + 1) * P]
                    if c == 0:
                        last = nc.vector.tensor_copy(STATE[:, 0, h, :], ps)
                    else:
                        last = nc.vector.scalar_tensor_tensor(STATE[:, c, h, :], STATE[:, c - 1, h, :],
                                                              eb[:, 4 * h + c:4 * h + c + 1], ps, ALU.mult, ALU.add)
                last.then_inc(sem("state_ready"), 1)
                dve.wait_ge(sem("state_ready"), c + 1)
            dve.wait_ge(sem("o_sums"), 1)
            nc.vector.tensor_scalar(SC9, PS[:, 4:8, :], 1.0 / P, EPS, ALU.mult, ALU.add).then_inc(sem("o_mean"), 1)
            dve.wait_ge(sem("o_root"), 1)
            link(nc.vector.reciprocal(SC9, SC9))
            for h in range(4):
                last = nc.vector.scalar_tensor_tensor(SC8[:, h, :], PS[:, h, :], par("onorm", h, h + 1), SC9[:, h, :],
                                                      ALU.mult, ALU.mult)
            link(last)
            nc.vector.tensor_tensor(SC8, SC8, HG, ALU.mult).then_inc(sem("y2_ready"), 1)
            dve.wait_ge(sem("y2_high"), 1)
            nc.vector.tensor_tensor(HLr[:, 0:4, :], SC8, HH[:, 0:4, :], ALU.subtract)
            nc.vector.tensor_tensor(HLr[:, 4:8, :], CB, HH[:, 4:8, :], ALU.subtract)
            barrier(dve, "dve")
            for k in range(NK):
                split_low(dve, (FIRST["wout2"] + k + LEAD, 0, 0))
            dve.wait_ge(sem("chunk_used"), FIRST["wout2"] + NK)
            for t in range(NT):
                x2 = XN[:, t, :].rearrange("p (a b) -> p a b", a=2)
                link(nc.vector.tensor_tensor(x2, banks(t), GATE[:, 0, :].rearrange("p (a b) -> p a b", a=2), ALU.mult))
                nc.vector.tensor_tensor(X[:, t, :], X[:, t, :], XN[:, t, :], ALU.add)
            barrier(dve, "dve")
            norm_turn(dve, "dve", "pre4", link, lambda k: MOD[:, 24 + k:25 + k], lambda k: MOD[:, 16 + k:17 + k])
            TI = TIU.bitcast(U32)
            c0 = FIRST["query"]

            def best16(vals, idx, src, work):
                link(nc.vector.max(vals[:, 0:8], src))
                nc.vector.max_index(idx[:, 0:8], vals[:, 0:8], src)
                link(nc.vector.match_replace(work, vals[:, 0:8], src, -3.0e38))
                link(nc.vector.max(vals[:, 8:16], work))
                link(nc.vector.max_index(idx[:, 8:16], vals[:, 8:16], work))

            for m in range(16):
                split_low(dve, (c0 + m + LEAD, 0, 0))
                if m >= 1:
                    dve.wait_ge(sem("scores_stored"), m)
                    for t in range(NT):
                        best16(TV[:, t, m - 1, :], TI[:, t, m - 1, :], SS[:, t, m - 1, :], WORK[:, 0:PK])
            dve.wait_ge(sem("scores_stored"), 16)
            for t in range(NT):
                best16(TV[:, t, 15, :], TI[:, t, 15, :], SS[:, t, 15, :], WORK[:, 0:PK])
            barrier(dve, "dve")
            BIu = BI.bitcast(U32)
            for u in range(32):
                t, h = u // 8, u % 8
                cand = CAND.rearrange("p (a b) -> p a b", a=TOPK)
                link(nc.vector.tensor_tensor(cand, TV[:, t, 2 * h, :].unsqueeze(2).to_broadcast([P, TOPK, TOPK]),
                                             TV[:, t, 2 * h + 1, :].unsqueeze(1).to_broadcast([P, TOPK, TOPK]), ALU.add))
                best16(BV[:, u, :], BIu[:, u, :], CAND, CAND2)
            link(nc.vector.tensor_copy(zg, BV[:, :, 0]))
            nc.vector.tensor_tensor(BV, BV, zg.unsqueeze(2).to_broadcast([P, 32, TOPK]), ALU.subtract)\
                .then_inc(sem("best_shifted"), 1)
            bi = BIu.rearrange("p u k -> p (u k)")
            link(nc.vector.tensor_scalar(PA.bitcast(U32), bi, 4, None, ALU.logical_shift_right))
            link(nc.vector.tensor_scalar(PB.bitcast(U32), bi, 15, None, ALU.bitwise_and))
            link(nc.vector.tensor_copy(PA, PA.bitcast(U32)))
            link(nc.vector.tensor_copy(PB, PB.bitcast(U32)))
            link(nc.vector.tensor_copy(TF, TI))
            for side, (pos, out) in enumerate(((PA, N1), (PB, N2))):
                for t in range(NT):
                    p3 = pos[:, t * P:(t + 1) * P].rearrange("p (h k) -> p h k", h=PH).unsqueeze(3)
                    it = con("iota")[:, 0:TOPK].unsqueeze(1).unsqueeze(1)
                    link(nc.vector.tensor_tensor(EQ, p3.to_broadcast([P, PH, TOPK, TOPK]),
                                                 it.to_broadcast([P, PH, TOPK, TOPK]), ALU.is_equal))
                    num = TF[:, t, side::2, :].unsqueeze(2).to_broadcast([P, PH, TOPK, TOPK])
                    link(nc.vector.tensor_tensor(EQ, EQ, num, ALU.mult))
                    last = nc.vector.tensor_reduce(out[:, t, :], EQ.rearrange("p h k a -> p (h k) a"), AX, ALU.add)
                    if t < NT - 1:
                        link(last)
                last.then_inc(sem("list_ready"), 1)
                dve.wait_ge(sem("list_ready"), side + 1)
            dve.wait_ge(sem("best_exp"), 1)
            link(nc.vector.tensor_reduce(zg, BV, AX, ALU.add))
            link(nc.vector.reciprocal(zg, zg))
            nc.vector.tensor_tensor(BV, BV, zg.unsqueeze(2).to_broadcast([P, 32, TOPK]), ALU.mult)\
                .then_inc(sem("list_ready"), 1)
            barrier(dve, "dve")
            for t in range(NT):
                with dve.Fori(0, 8) as i:
                    for j in range(16):
                        if j % 4 == 0:
                            dve.wait_ge(sem("gm_ready"), i * 4 + (32 * t + j // 4 + 1))
                        tok = i * 16 + (t * P + j)
                        nc.vector.tensor_scalar(OH[:, j, 0, :], con("iota"), LST[:, 0, bass.ds(tok, 1)], None, ALU.is_equal)
                        nc.vector.tensor_scalar(OH[:, j, 1, :], con("iota"), LST[:, 1, bass.ds(tok, 1)],
                                                LST[:, 2, bass.ds(tok, 1)], ALU.is_equal, ALU.mult)\
                            .then_inc(sem("onehot_ready"), 1)
            barrier(dve, "dve")
            dve.wait_ge(sem("x3_saved"), 16)
            for t in range(NT):
                nc.vector.memset(YA[:, t, :], 0.0)
            dve.drain().then_inc(sem("acc_done"), 1)
            dve.wait_ge(sem("acc_done"), 1)
            nc.vector.memset(WF[:, 0, 0:1], 0.0).then_inc(sem("w_done"), 2)

            def step(c, g8, b, u, v):
                n = 0
                for half in range(2):
                    if u:
                        for m in range(4 * half, 4 * half + 4):
                            split_low(dve, plus(c, n + LEAD))
                            dve.wait_ge(sem("gelu_done"), g8 + (m + 5))
                            dve.wait_ge(sem(f"gates_landed{m % 4}"), (g8 * 4 + 16) if m < 4 else (g8 * 4 + 32))
                            dve.wait_ge(sem("w_done"), g8 + (m + 2))
                            nc.vector.tensor_tensor(WF[:, m % 2, :], GE[:, m % 2, :], GR_[:, m % 4, :], ALU.mult)\
                                .then_inc(sem("w_done"), 1)
                            dve.wait_ge(sem("w_high"), g8 + (m + 1))
                            nc.vector.tensor_tensor(WGTr[:, b, 1, m, :], WF[:, m % 2, :], WGT[:, b, 0, m, :],
                                                    ALU.subtract).then_inc(sem("w_low"), 1)
                            n += 1
                    if v:
                        for q in range(4):
                            split_low(dve, plus(c, n + LEAD))
                            n += 1
                        dve.wait_ge(sem("chunk_used"), number(c, n))
                        for t in range(NT):
                            acc = YA[:, t, half * 512:(half + 1) * 512]
                            last = nc.vector.tensor_tensor(acc, acc, PS[:, t, :], ALU.add)
                        last.then_inc(sem("acc_done"), 1)
            experts(dve, step)
            barrier(dve, "dve")
            dve.wait_ge(sem("x3_back"), 16)
            for t in range(NT):
                link(nc.vector.tensor_tensor(YA[:, t, :], YA[:, t, :], GATE[:, 1, :], ALU.mult))
                link(nc.vector.tensor_tensor(X[:, t, :], YA[:, t, :], XN[:, t, :], ALU.add))
            nc.vector.memset(WF[:, 0, 0:1], 0.0).then_inc(sem("x4_ready"), 1)
            rms_dve(dve, link, "final")
            dve.wait_ge(sem("row_landed"), 48)
            for t in range(NT):
                nc.vector.scalar_tensor_tensor(X[:, t, :], X[:, t, :], rstd[:, t:t + 1], ROW[:, :], ALU.mult, ALU.mult)\
                    .then_inc(sem("out_ready"), 1)

        @block.tensor
        def _(pe):
            pe.wait_ge(sem("const_landed"), 16)
            norm_turn(pe, "pe", "pre1")
            for b in range(6):
                w = 512 if b < 5 else TAIL
                wait(pe, "proj_stored", b - 1)
                for q in range(4):
                    mm_n2(pe, (4 * b + q, 0, 0), q, 4 * (b % 2), w)
            barrier(pe, "pe")
            barrier(pe, "pe")
            for n in range(20):
                wait(pe, "head_stored", n - 7)
                o = ROPED[n]
                for t in range(NT):
                    last = nc.tensor.transpose(PS[0:64, n % 8, t * P:(t + 1) * P], PJ[:, t, o:o + DK], ident)
                last.then_inc(sem("head_turned"), 1)
            pe.wait_ge(sem("head_stored"), 20)
            def rt_out(h):
                pe.wait_ge(sem("rt_decayed"), 4 * h + 4)
                for t in range(NT):
                    for j in range(t + 1):
                        o = sr_at[j] + (t - j) * P
                        last = nc.tensor.matmul(PS[:, 4 + t, h * P:(h + 1) * P], SR[:, h % 2, o:o + P],
                                                PJ[:, j, RV + h * P:RV + (h + 1) * P], start=(j == 0), stop=(j == t))
                last.then_inc(sem("rt_out"), 1)

            for h in range(RH):
                for j in range(NT):
                    u = 4 * h + j
                    wait(pe, "rt_decayed", u - 3)
                    nc.tensor.matmul(PS[:, u % 4, 0:S - j * P], RT[0:64, 4 + h, j * P:(j + 1) * P],
                                     RT[0:64, h, j * P:S], start=True, stop=True).then_inc(sem("rt_scores"), 1)
                if h >= 1:
                    rt_out(h - 1)
            rt_out(RH - 1)
            barrier(pe, "pe")
            for w in range(2):
                pe.wait_ge(sem("cmp_dup"), w + 1)
                for g in range(2):
                    for t in range(NT):
                        last = nc.tensor.transpose(PS[:, g, t * P:(t + 1) * P],
                                                   DUP[:, t, g].rearrange("p j x -> p (j x)"), ident)
                last.then_inc(sem("cmp_turned"), 1)
                pe.wait_ge(sem("blk_low"), w + 1)
                for q in range(4):
                    c = (FIRST["cmp"] + 4 * w + q, 0, 0)
                    pe.wait_ge(sem("low_done"), number(c, 1))
                    wh = WHr[:, slot(c), :].rearrange("p (k n) -> p k n", k=4)
                    wl = WLr[:, slot(c), :].rearrange("p (k n) -> p k n", k=4)
                    for kk in range(4):
                        k = 4 * q + kk
                        for f in range(2):
                            fs = slice(f * P, (f + 1) * P)
                            last = mm3(PS[:, 2 + f, 0:64], (wh[:, kk, fs], wl[:, kk, fs]),
                                       (BLHr[:, k, :], BLLr[:, k, :]), k == 0, k == 15)
                    last.then_inc(sem("chunk_used"), 1)
                pe.wait_ge(sem("hid_gelu"), w + 1)
                pe.wait_ge(sem("w2_landed"), 32)
                if w == 0:
                    for f in range(2):
                        last = nc.tensor.matmul(PS[0:64, 4, 0:64], HIDK[:, f, :], W2[:, 0, f, :],
                                                start=(f == 0), stop=(f == 1))
                    last.then_inc(sem("kc_ready"), 1)
                    pe.wait_ge(sem("kc_roped"), 1)
                    nc.tensor.transpose(PS[0:64, 5, 0:64], KC[0:64, 0, :], ident[0:64, 0:64]).then_inc(sem("kct_ready"), 1)
                else:
                    for g in range(2):
                        for f in range(2):
                            last = nc.tensor.matmul(PS[:, 6 + g, 0:64], HID[:, f, g].rearrange("p r n -> p (r n)"), W2[:, 1, f, :],
                                                    start=(f == 0), stop=(f == 1))
                    last.then_inc(sem("vc_ready"), 1)
            barrier(pe, "pe")
            for t in range(NT):
                for h in range(NH):
                    g = h // 4
                    last = nc.tensor.matmul(PS[:, t, 32 * h:32 * h + 32], QT[0:64, h, t * P:(t + 1) * P],
                                            KCT[0:64, 32 * g:32 * g + 32], start=True, stop=True)
            last.then_inc(sem("cs_ready"), 1)
            pe.wait_ge(sem("cmp_probs"), 1)
            for t in range(NT):
                for g in range(2):
                    u = 2 * t + g
                    last = nc.tensor.transpose(PS[:, 4 + u // 4, (u % 4) * P:(u % 4 + 1) * P],
                                               E4[:, t, 4 * g:4 * g + 4, :].rearrange("p h n -> p (h n)"), ident)
            last.then_inc(sem("cmp_pt"), 1)
            pe.wait_ge(sem("cmp_pt_stored"), 1)
            for t in range(NT):
                for g in range(2):
                    last = nc.tensor.matmul(PS[:, t, 256 * g:256 * g + 256], PTC[:, 2 * t + g, :],
                                            VBD[:, g].rearrange("p r n -> p (r n)"), start=True, stop=True)
            last.then_inc(sem("cmp_out"), 1)
            barrier(pe, "pe")
            for s in range(len(units) + 2):
                if s < len(units):
                    b, t, h = units[s]
                    wait(pe, "at_exp", s - 1)
                    nc.tensor.matmul(PS[:, s % 2, 0:(t + 1) * P], QT[0:64, h, t * P:(t + 1) * P],
                                     KT[0:64, 2 * b + h // 4, 0:(t + 1) * P], start=True, stop=True)\
                        .then_inc(sem("at_scores"), 1)
                u = s - 1
                if 0 <= u < len(units):
                    b, t, h = units[u]
                    pe.wait_ge(sem("at_exp"), u + 1)
                    v = u - 2
                    if v >= 0:
                        pe.wait_ge(sem(f"at_stored{v % 2}"), v // 2 + 1)
                    for j in range(t + 1):
                        last = nc.tensor.transpose(PS[:, 2 + u % 2, j * P:(j + 1) * P], EX[:, u % 2, j * P:(j + 1) * P], ident)
                    last.then_inc(sem("at_turned"), 1)
                u = s - 2
                if u >= 0:
                    b, t, h = units[u]
                    n = u // 8
                    pe.wait_ge(sem(f"at_stored{u % 2}"), u // 2 + 1)
                    if h == 0:
                        wait(pe, "at_taken", n - 1)
                    o = (VSL, VWN)[b] + 64 * (h // 4)
                    for j in range(t + 1):
                        last = nc.tensor.matmul(PS[:, 4 + n % 2, h * DK:(h + 1) * DK], PT[:, u % 2, j * P:(j + 1) * P],
                                                PJ[:, j, o:o + DK], start=(j == 0), stop=(j == t))
                    last.then_inc(sem("at_pv"), 1)
            barrier(pe, "pe")
            turn_pe(pe, "mix", Y)
            barrier(pe, "pe")
            for k in range(NK):
                mm_n1(pe, (FIRST["wout"] + k, 0, 0), (HHr[:, k, :], HLr[:, k, :]), k == 0, k == NK - 1)
            add_normed(pe, "pe", "mixpost")
            norm_turn(pe, "pe", "pre2")
            cu = FIRST["up"]
            with pe.Fori(0, NF // 2) as i:
                for j in range(4):
                    pe.wait_ge(sem("up_free"), i * 4 + (j + 1))
                    mm_t(pe, (cu + j, i, 4), PS[:, j, :])
            barrier(pe, "pe")
            for k in range(NF):
                pe.wait_ge(sem("gt_low"), k + 1)
                mm_n1(pe, (FIRST["down"] + k, 0, 0), (GSHr[:, k % 4, :], GSLr[:, k % 4, :]),
                      k == 0, k == NF - 1)
            add_normed(pe, "pe", "ffpost")
            pe.wait_ge(sem("ca_low"), 1)
            c0 = FIRST["ada_t"]
            with pe.Fori(0, 8) as i:
                for j in range(4):
                    mm_t(pe, (c0 + j, i, 4), PS[:, 0, bass.ds(i * 8 + 2 * j, 2)],
                         lambda k: (CA2r[:, 0, k, :], CA2r[:, 1, k, :]))
            for g in range(2):
                for k in range(NK):
                    c = (FIRST["ada_n"] + 8 * g + k, 0, 0)
                    pe.wait_ge(sem("low_done"), number(c, 1))
                    for h in range(2):
                        hs = slice(h * 512, (h + 1) * 512)
                        last = mm3(PS[:, 4 + 2 * g + h, :], (CABr[:, 0, k, :], CABr[:, 1, k, :]),
                                   (WHr[:, slot(c), hs], WLr[:, slot(c), hs]), k == 0, k == NK - 1)
                    last.then_inc(sem("chunk_used"), 1)
            barrier(pe, "pe")
            norm_turn(pe, "pe", "pre3")
            c0 = FIRST["win2"]
            for m in range(24):
                wait(pe, "p2_stored", m - 3)
                mm_t(pe, (c0 + m, 0, 0), PS[:, m % 4, :])
            for q in range(4):
                mm_n2(pe, (c0 + 24 + q, 0, 0), q, 4)
            barrier(pe, "pe")
            pe.wait_ge(sem("cv_sq"), 1)
            for n in range(4):
                last = nc.tensor.matmul(PS[:, n, :], con("ones"), CC[:, n, :], start=True, stop=True)
            last.then_inc(sem("cv_sums"), 1)
            barrier(pe, "pe")
            for n in range(8):
                kl, ql = (SC9, SC8) if n < 7 else (HK, HQ)
                if n < 7:
                    pe.wait_ge(sem("lv_ready"), n + 1)
                for h in range(4):
                    wait(pe, "lv_taken", 4 * (n - 2) + h + 1)
                    for c in range(4):
                        cs = slice(c * P, (c + 1) * P)
                        last = nc.tensor.matmul(PS[:, 4 * (n % 2) + h, cs], kl[:, h, cs], ql[:, h, cs], start=True, stop=True)
                    last.then_inc(sem("lv_scores"), 1)
            barrier(pe, "pe")
            pe.wait_ge(sem("kd_ready"), 1)
            for h in range(4):
                for c in range(3):
                    cs = slice(c * P, (c + 1) * P)
                    last = nc.tensor.transpose(PS[:, 4 + h, cs], SC9[:, h, cs], ident)
            last.then_inc(sem("kd_turned"), 1)
            pe.wait_ge(sem("kd_stored"), 1)
            for c in range(3):
                for h in range(4):
                    last = nc.tensor.matmul(PS[:, 4 + c, h * P:(h + 1) * P], SC8[:, h, c * P:(c + 1) * P],
                                            HV[:, c, h * P:(h + 1) * P], start=True, stop=True)
                last.then_inc(sem("kv_ready"), 1)
            pe.wait_ge(sem("qx_ready"), 1)
            for c in range(4):
                wait(pe, "state_ready", c)
                cs = slice(c * P, (c + 1) * P)
                for h in range(4):
                    last = nc.tensor.matmul(PS[:, h, cs], HV[:, c, h * P:(h + 1) * P], HF[:, h, cs], start=True, stop=(c == 0))
                    if c:
                        last = nc.tensor.matmul(PS[:, h, cs], STATE[:, c - 1, h, :], CC[:, h, cs], start=False, stop=True)
            last.then_inc(sem("o_done"), 1)
            pe.wait_ge(sem("o_sq"), 1)
            for h in range(4):
                last = nc.tensor.matmul(PS[:, 4 + h, :], con("ones"), SC9[:, h, :], start=True, stop=True)
            last.then_inc(sem("o_sums"), 1)
            barrier(pe, "pe")
            for k in range(NK):
                mm_n1(pe, (FIRST["wout2"] + k, 0, 0), (HHr[:, k, :], HLr[:, k, :]), k == 0, k == NK - 1)
            barrier(pe, "pe")
            norm_turn(pe, "pe", "pre4")
            pe.wait_ge(sem("subkeys_landed"), 16)
            c0 = FIRST["query"]
            for m in range(17):
                if m < 16:
                    wait(pe, "query_stored", m - 3)
                    mm_t(pe, (c0 + m, 0, 0), PS[:, m % 4, :])
                if m >= 1:
                    n = m - 1
                    pe.wait_ge(sem("query_stored"), n + 1)
                    wait(pe, "scores_stored", n - 3)
                    for t in range(NT):
                        last = nc.tensor.matmul(PS[:, 4 + n % 4, t * P:(t + 1) * P], QE[:, n % 2, t * P:(t + 1) * P],
                                                SUBK[:, n, :], start=True, stop=True)
                    last.then_inc(sem("keys_scored"), 1)
            barrier(pe, "pe")
            for n in range(3):
                pe.wait_ge(sem("list_ready"), n + 1)
                src = (N1, N2, BV.rearrange("p (t h) k -> p t (h k)", t=NT))[n]
                for t in range(NT):
                    last = nc.tensor.transpose(PS[:, n, t * P:(t + 1) * P], src[:, t, :], ident)
                last.then_inc(sem("list_turned"), 1)
            barrier(pe, "pe")
            pe.sem_inc(sem("gm_ready"), 4)
            for t in range(NT):
                with pe.Fori(0, 8) as i:
                    for q in range(4):
                        pe.wait_ge(sem("gm_stored"), i * 4 + (32 * t + q + 1))
                        for j in range(4 * q, 4 * q + 4):
                            pe.wait_ge(sem("onehot_ready"), i * 16 + (P * t + j + 1))
                            last = nc.tensor.matmul(PS[:, q, (j % 4) * P:(j % 4 + 1) * P], OH[:, j, 0, :], OH[:, j, 1, :],
                                                    start=True, stop=True)
                        last.then_inc(sem("gm_ready"), 1)
            barrier(pe, "pe")

            def step(c, g8, b, u, v):
                n = 0
                for half in range(2):
                    if u:
                        for m in range(4 * half, 4 * half + 4):
                            pe.wait_ge(sem("gelu_done"), g8 + (m + 1))
                            mm_t(pe, plus(c, n), PS[:, 4 + m % 4, :])
                            n += 1
                    if v:
                        pe.wait_ge(sem("acc_done"), (g8 // 4 + (half - 1)) if isinstance(g8, int)
                                   else (acc_of(c) + half))
                        for q in range(4):
                            cc = plus(c, n)
                            pe.wait_ge(sem("low_done"), number(cc, 1))
                            pe.wait_ge(sem("w_low"), g8 + (2 * q + 2 - GROUP))
                            for r in range(2):
                                i2 = 2 * q + r
                                for t in range(NT):
                                    ts = slice(t * P, (t + 1) * P)
                                    rs = slice(r * 512, (r + 1) * 512)
                                    last = mm3(PS[:, t, :], (WGTr[:, 1 - b, 0, i2, ts], WGTr[:, 1 - b, 1, i2, ts]),
                                               (WHr[:, slot(cc), rs], WLr[:, slot(cc), rs]), i2 == 0, i2 == GROUP - 1)
                            last.then_inc(sem("chunk_used"), 1)
                            n += 1

            def acc_of(c):
                s_ = (c[0] - FIRST["experts"] - GROUP) // (2 * GROUP)
                return c[1] * 4 + (2 * s_ + 1)
            experts(pe, step)
            barrier(pe, "pe")


def kernel(**inputs):
    import concourse.bacc as bacc
    from concourse.bass_utils import run_bass_kernel_spmd

    nc = bacc.Bacc("TRN2", target_bir_lowering=False, num_devices=1)
    v = {k: np.asarray(a) for k, a in inputs.items()}

    def tiles(a, n):
        return a.reshape(n, P).T

    def columns(w):
        return w.reshape(NK, P, -1, P).transpose(2, 1, 0, 3).reshape(-1, P, NK * P)

    small, decay, levels = constants()
    par = [tiles(v["norm_mix_pre"][0], 8), tiles(v["norm_ffn_pre"][0], 8), tiles(v["norm1_w_2"][0], 8),
           tiles(v["norm2_w_2"][0], 8), tiles(v["ret_gn_w"][0], 4), tiles(v["b_ada_2"][0], 48),
           tiles(v["c_2"][0], 8), tiles(v["hgrn_lb_logits_2"][0], 4), tiles(v["hgrn_lb_logits_2"][1], 4),
           tiles(v["hgrn_onorm_w_2"][0], 4), tiles(v["conv_onorm_w_2"][0], 4),
           v["conv_w_2"][0].reshape(3, 4, P).transpose(2, 1, 0).reshape(P, 12),
           v["ffn_conv"][0].reshape(3, 2, NF, P).transpose(3, 2, 1, 0).reshape(P, 132)]
    up = columns(v["ffn_w_up"][0])
    ada = v["w_ada_2"][0]
    adac = columns(ada)
    w2 = v["w_in_2"][0]
    w2c = columns(w2)
    arrays = {
        "x": v["x"][0],
        "const": np.concatenate([small[n] for n, _ in CONST_COLS], axis=1),
        "param": np.concatenate(par, axis=1),
        "decay": decay, "levels": levels,
        "nm_post": v["norm_mix_post"][0], "nf_post": v["norm_ffn_post"][0], "final_w": v["final_norm_w_2"],
        "w_in": v["w_in"][0],
        "cmp_w1": np.stack([v["cmp_k_w1"][0], v["cmp_v_w1"][0]]).reshape(2, 4, 4, P, 256).transpose(0, 1, 3, 2, 4)
                    .reshape(8, P, 1024),
        "cmp_w2": np.stack([v["cmp_k_w2"][0], v["cmp_v_w2"][0]]),
        "cmp_pos": np.stack([v["cmp_k_pos"][0], v["cmp_v_pos"][0]]).reshape(2, 16, 2, DK).transpose(2, 3, 0, 1)
                     .reshape(P, 2, 16),
        "w_out": v["w_out"][0],
        "ffn_up": np.stack([up[:NF], up[NF:]], axis=1).reshape(2 * NF, P, 1024),
        "ffn_down": v["ffn_w_down"][0],
        "ada_t": adac.reshape(6, 8, P, 1024)[[0, 1, 3, 4]].reshape(32, P, 1024),
        "ada_n": ada.reshape(NK, P, 6, D)[:, :, [2, 5]].transpose(2, 0, 1, 3).reshape(16, P, 1024),
        "bada_gate": v["b_ada_2"][0].reshape(6, D)[[2, 5]],
        "win2": np.concatenate([w2c[0:8], w2c[12:28],
                                w2[:, 1024:1536].reshape(4, 2, P, 512).transpose(0, 2, 1, 3).reshape(4, P, 1024)]),
        "w_out2": v["w_out_2"][0],
        "query": columns(v["peer_w_query_2"][0]),
        "subk": v["peer_sub_keys_2"][0].reshape(16, PK, P).transpose(2, 0, 1),
        "peer_u": v["peer_u_2"][0].reshape(P, P, NK, P).transpose(1, 3, 2, 0).reshape(P, P, 1024),
        "peer_v": v["peer_v_2"][0],
    }
    arrays = {k: np.ascontiguousarray(a) for k, a in arrays.items()}
    d = {}
    for name, a in arrays.items():
        d[name] = nc.dram_tensor("in_" + name, a.shape, mybir.dt.from_np(a.dtype), kind="ExternalInput").ap()
    d["gate_matrices"] = nc.dram_tensor("gate_matrices", (P, P, S), F32, kind="Internal").ap()
    d["x3"] = nc.dram_tensor("x3", (P, NT, D), F32, kind="Internal").ap()
    d["out"] = nc.dram_tensor("out_0", (S, D), F32, kind="ExternalOutput").ap()
    build(nc, d)
    r = run_bass_kernel_spmd(nc, [{"in_" + k: a for k, a in arrays.items()}], core_ids=[0])
    return r.results[0]["out_0"].reshape(1, S, D)
```

```python
from contextlib import ExitStack

import numpy as np
import concourse.bass as bass
from concourse import mybir

F32 = mybir.dt.float32
F32R = mybir.dt.float32r
U32 = mybir.dt.uint32
I32 = mybir.dt.int32
ACT = mybir.ActivationFunctionType
ALU = mybir.AluOpType
AX = mybir.AxisListType.X

P = 128
D = 1024
S = 512
NT = S // P
NK = D // P
EPS = 1e-6
GN_EPS = 1e-5
NEG = -1e30
RQ, RK, RV, RG, NQ = 0, 256, 512, 1024, 1536
KCM, VCM, KSL, VSL, KWN, VWN, NG = 2048, 2176, 2304, 2432, 2560, 2688, 2816
IN_COLS = 2840
TAIL = IN_COLS - 5 * 512
RH, NH, GR = 4, 8, 2
DK = 64
DFF = 2816
NF = DFF // P
CW = 1024
RING = 4
LEAD = 3
GROUP = 8
NGRP = P // GROUP
PH, PK, TOPK = 8, 128, 16

PHASES = [("win", 24), ("cmp", 8), ("ada", 6 * NK), ("wout", 8), ("up", 2 * NF), ("down", NF),
          ("win2", 28), ("wout2", 8), ("query", 16), ("experts", 2 * P)]
FIRST = {}
_n = 0
for _name, _count in PHASES:
    FIRST[_name] = _n
    _n += _count
CHUNKS = _n


def constants():
    f = np.float32
    inv = 1.0 / (10000.0 ** (np.arange(0, DK, 2, dtype=np.float64) / DK))

    def angles(pos):
        a = (pos.astype(f)[:, None] * inv.astype(f)[None, :]).astype(np.float64)
        c, s = np.cos(a), np.sin(a)
        return np.concatenate([c, c], 1).astype(f), np.concatenate([-s, s], 1).astype(f)

    cols = {}
    cols["ident"] = np.eye(P, dtype=f)
    cols["ones"] = np.ones((P, P), f)
    c, s = angles(np.arange(S))
    cols["cos"] = c.reshape(NT, P, DK).transpose(1, 0, 2).reshape(P, -1)
    cols["sin"] = s.reshape(NT, P, DK).transpose(1, 0, 2).reshape(P, -1)
    end = np.tile(np.arange(32) * 16 + 31, 4)
    c, s = angles(end)
    cols["ccos"], cols["csin"] = c, s
    i = np.arange(P)
    cols["causal"] = np.where(i[None, :] > i[:, None], NEG, 0.0).astype(f)
    t = np.arange(S).reshape(NT, P)
    ok = (end[None, None, :32] <= t[:, :, None]) & (np.arange(32) < 31)
    ok = ok.transpose(1, 0, 2).reshape(P, -1)
    cols["cmp_ok"] = ok.astype(f)
    cols["cmp_no"] = np.where(ok, 0.0, NEG).astype(f)
    cols["iota"] = np.tile(i.astype(f), (P, 1))
    cols["four"] = (i[:, None] // 32 == np.arange(4)[None, :]).astype(f)
    small = cols
    gamma = 1.0 - 2.0 ** (-5.0 - np.arange(RH))
    x = np.arange(S)[None, None, :] - i[:, None, None]
    decay = np.where(x >= 0, np.exp(np.log(gamma)[None, :, None] * np.maximum(x, 0)), 0.0) * DK ** -0.5
    lev = np.zeros((P, 8, P), np.uint32)
    for n, m in enumerate((64, 32, 16, 8, 4, 2, 1)):
        lev[:, n] = ((i[:, None] // (2 * m) == i[None, :] // (2 * m)) & (i[:, None] % (2 * m) < m)
                     & (i[None, :] % (2 * m) >= m))
    lev[:, 7] = np.eye(P)
    return small, decay.astype(f).reshape(P, -1), lev.reshape(P, -1)


CONST_COLS = [("ident", P), ("ones", P), ("cos", NT * DK), ("sin", NT * DK), ("ccos", DK), ("csin", DK),
              ("causal", P), ("cmp_ok", NT * 32), ("cmp_no", NT * 32), ("iota", P), ("four", 4)]
PARAM_COLS = [("nmp", 8), ("nfp", 8), ("n1", 8), ("n2", 8), ("gn", 4), ("bada", 48), ("c", 8), ("lb0", 4),
              ("lb1", 4), ("onorm", 4), ("conorm", 4), ("conv", 12), ("ffconv", 132)]


def offsets(cols):
    at, n = {}, 0
    for name, w in cols:
        at[name] = (n, w)
        n += w
    return at, n


def build(nc, d):
    const_at, n_const = offsets(CONST_COLS)
    param_at, n_param = offsets(PARAM_COLS)
    with ExitStack() as ctx:
        place = {}

        def sb(name, cols, dt=F32):
            place[name] = nc.sbuf_base
            return ctx.enter_context(nc.sbuf_tensor(name, [P, cols], dt))

        def over(parent, name, first, cols, dt):
            return nc.alloc_sbuf_tensor_at(name, [P, cols], dt, offset=(place[parent] + 31) // 32 * 32 + 4 * first)[:, :]

        sems = {}

        def sem(name):
            if name not in sems:
                sems[name] = ctx.enter_context(nc.semaphore(name))
            return sems[name]

        CON, PAR = sb("CON", n_const), sb("PAR", n_param)
        X = sb("X", NT * D)[:, :].rearrange("p (t n) -> p t n", t=NT)
        HHr = sb("HH", NK * S, F32R)[:, :].rearrange("p (k t) -> p k t", k=NK)
        HLr = sb("HL", NK * S, F32R)[:, :].rearrange("p (k t) -> p k t", k=NK)
        HH, HL = HHr.bitcast(F32), HLr.bitcast(F32)
        RAW = sb("RAW", RING * CW)[:, :].rearrange("p (r n) -> p r n", r=RING)
        WHr = sb("WH", RING * CW, F32R)[:, :].rearrange("p (r n) -> p r n", r=RING)
        WLr = sb("WL", RING * CW, F32R)[:, :].rearrange("p (r n) -> p r n", r=RING)
        WH = WHr.bitcast(F32)
        ROW = sb("ROW", D)
        GATE = sb("GATE", 2 * D)[:, :].rearrange("p (g n) -> p g n", g=2)
        MISC = sb("MISC", 1024)
        A = sb("A", 22528)
        PS = ctx.enter_context(nc.psum_tensor("PS", [P, 8, 512], F32))

        def con(name):
            o, w = const_at[name]
            return CON[:, o:o + w]

        def par(name, a=0, b=None):
            o, w = param_at[name]
            return PAR[:, o + a:o + (w if b is None else b)]

        used_misc = [0]

        def misc(n):
            used_misc[0] += n
            assert used_misc[0] <= 1024
            return MISC[:, used_misc[0] - n:used_misc[0]]

        ident = con("ident")
        sumsq, rstd = misc(4), misc(4)

        def wait(eng, s, v):
            if not (isinstance(v, int) and v <= 0):
                eng.wait_ge(sem(s), v)

        phase = {"pe": 0, "act": 0, "dve": 0}

        def barrier(eng, who):
            phase[who] += 1
            eng.drain().then_inc(sem("phase_ended"), 1)
            eng.wait_ge(sem("phase_ended"), 3 * phase[who])

        def link_for(eng, name):
            count = [0]

            def link(ins):
                count[0] += 1
                ins.then_inc(sem(name), 1)
                eng.wait_ge(sem(name), count[0])
            return link

        def slot(c):
            return c[0] % RING

        def plus(c, n):
            return (c[0] + n, c[1], c[2])

        def number(c, n=0):
            return c[0] + n + c[2] * c[1] if not isinstance(c[1], int) else c[0] + n

        def landed(c):
            if isinstance(c[1], int):
                return 16 * (c[0] // RING + 1)
            return 16 * (c[0] // RING + 1) + c[1] * (16 * c[2] // RING)

        def split_high(act, c, w=CW):
            if c[0] >= CHUNKS:
                return
            act.wait_ge(sem(f"raw_landed{slot(c)}"), landed(c))
            wait(act, "chunk_used", number(c, 1 - RING))
            nc.scalar.activation(WHr[:, slot(c), 0:w], RAW[:, slot(c), 0:w], ACT.Copy).then_inc(sem("high_done"), 1)

        def split_low(dve, c, w=CW):
            if c[0] >= CHUNKS:
                return
            dve.wait_ge(sem("high_done"), number(c, 1))
            nc.vector.tensor_tensor(WLr[:, slot(c), 0:w], RAW[:, slot(c), 0:w], WH[:, slot(c), 0:w],
                                    ALU.subtract).then_inc(sem("low_done"), 1)

        def mm3(out, L, R, first, last):
            nc.tensor.matmul(out, L[0], R[0], start=first, stop=False)
            nc.tensor.matmul(out, L[0], R[1], start=False, stop=False)
            return nc.tensor.matmul(out, L[1], R[0], start=False, stop=last)

        def mm_t(pe, c, out, rhs=None, n=S):
            pe.wait_ge(sem("low_done"), number(c, 1))
            wh = WHr[:, slot(c), :].rearrange("p (k n) -> p k n", k=NK)
            wl = WLr[:, slot(c), :].rearrange("p (k n) -> p k n", k=NK)
            for k in range(NK):
                r = (HHr[:, k, :], HLr[:, k, :]) if rhs is None else rhs(k)
                last = mm3(out, (wh[:, k, :], wl[:, k, :]), r, k == 0, k == NK - 1)
            last.then_inc(sem("chunk_used"), 1)

        def mm_n2(pe, c, q, bank, w=512):
            pe.wait_ge(sem("low_done"), number(c, 1))
            wh = WHr[:, slot(c), 0:2 * w].rearrange("p (k n) -> p k n", k=2)
            wl = WLr[:, slot(c), 0:2 * w].rearrange("p (k n) -> p k n", k=2)
            for kk in range(2):
                k = 2 * q + kk
                for t in range(NT):
                    ts = slice(t * P, (t + 1) * P)
                    last = mm3(PS[:, bank + t, 0:w], (HHr[:, k, ts], HLr[:, k, ts]), (wh[:, kk, :], wl[:, kk, :]),
                               k == 0, k == NK - 1)
            last.then_inc(sem("chunk_used"), 1)

        def mm_n1(pe, c, L, first, final):
            pe.wait_ge(sem("low_done"), number(c, 1))
            for t in range(NT):
                ts = slice(t * P, (t + 1) * P)
                for h in range(2):
                    hs = slice(h * 512, (h + 1) * 512)
                    last = mm3(PS[:, 2 * t + h, :], (L[0][:, ts], L[1][:, ts]),
                               (WHr[:, slot(c), hs], WLr[:, slot(c), hs]), first, final)
            last.then_inc(sem("chunk_used"), 1)

        XN = A[:, 0:4096].rearrange("p (t n) -> p t n", t=NT)
        JUNK = A[:, 4096:5120]
        TMP = A[:, 5120:6144].rearrange("p (r n) -> p r n", r=2)
        NORMS = ["pre1", "mixpost", "pre2", "ffpost", "pre3", "pre4", "final"]
        TURNS = ["pre1", "mix", "pre2", "pre3", "pre4"]
        ROWED = ["pre1", "pre2", "pre3", "pre4"]

        def rms_act(act, link, src, tag, n=NT):
            for t in range(n):
                ins = nc.scalar.activation(JUNK if len(src(t).shape) == 2 else JUNK.rearrange("p (a b) -> p a b", a=2),
                                           src(t), ACT.Square, accum_out=sumsq[:, t:t + 1])
                if t < n - 1:
                    link(ins)
            ins.then_inc(sem("rms_squares"), 1)
            act.wait_ge(sem("rms_mean"), NORMS.index(tag) + 1)
            nc.scalar.activation(rstd, rstd, ACT.Sqrt).then_inc(sem("rms_root"), 1)

        def rms_dve(dve, link, tag):
            dve.wait_ge(sem("rms_squares"), NORMS.index(tag) + 1)
            nc.vector.tensor_scalar(rstd, sumsq, 1.0 / D, EPS, ALU.mult, ALU.add).then_inc(sem("rms_mean"), 1)
            dve.wait_ge(sem("rms_root"), NORMS.index(tag) + 1)
            link(nc.vector.reciprocal(rstd, rstd))

        def turn_pe(pe, tag, src):
            for k in range(NK):
                for t in range(NT):
                    if k == 0 and src is XN:
                        pe.wait_ge(sem("rows_normed"), NT * ROWED.index(tag) + t + 1)
                    last = nc.tensor.transpose(PS[:, k, t * P:(t + 1) * P], src[:, t, k * P:(k + 1) * P], ident)
                last.then_inc(sem("tile_turned"), 1)

        def turn_dve(dve, link, tag, scale, bias=None, ready=None):
            for k in range(NK):
                n = NK * TURNS.index(tag) + k
                dve.wait_ge(sem("tile_turned"), n + 1)
                wait(dve, "tile_high", n - 1)
                sc = scale(k)
                if sc is None:
                    ins = nc.vector.tensor_copy(TMP[:, k % 2, :], PS[:, k, :])
                elif bias is None:
                    ins = nc.vector.tensor_scalar(TMP[:, k % 2, :], PS[:, k, :], sc, None, ALU.mult)
                else:
                    ins = nc.vector.tensor_scalar(TMP[:, k % 2, :], PS[:, k, :], sc, bias(k), ALU.mult, ALU.add)
                ins.then_inc(sem("tile_scaled"), 1)
                dve.wait_ge(sem("tile_high"), n + 1)
                link(nc.vector.tensor_tensor(HLr[:, k, :], TMP[:, k % 2, :], HH[:, k, :], ALU.subtract))

        def turn_act(act, tag):
            for k in range(NK):
                act.wait_ge(sem("tile_scaled"), NK * TURNS.index(tag) + k + 1)
                nc.scalar.activation(HHr[:, k, :], TMP[:, k % 2, :], ACT.Copy).then_inc(sem("tile_high"), 1)

        def norm_turn(eng, who, tag, link=None, scale=None, bias=None):
            if who == "act":
                rms_act(eng, link, lambda t: X[:, t, :], tag)
                turn_act(eng, tag)
            elif who == "dve":
                rms_dve(eng, link, tag)
                for t in range(NT):
                    nc.vector.tensor_scalar(XN[:, t, :], X[:, t, :], rstd[:, t:t + 1], None,
                                            ALU.mult).then_inc(sem("rows_normed"), 1)
                turn_dve(eng, link, tag, scale, bias)
            else:
                turn_pe(eng, tag, XN)
            barrier(eng, who)

        def banks(t):
            return PS[:, 2 * t:2 * t + 2, :]

        def add_normed(eng, who, tag, link=None):
            barrier(eng, who)
            if who == "act":
                rms_act(eng, link, banks, tag)
            elif who == "dve":
                rms_dve(eng, link, tag)
                for t in range(NT):
                    link(nc.vector.tensor_scalar(XN[:, t, :].rearrange("p (a b) -> p a b", a=2), banks(t),
                                                 rstd[:, t:t + 1], None, ALU.mult))
                eng.wait_ge(sem("row_landed"), 16 * {"mixpost": 1, "ffpost": 2}[tag])
                for t in range(NT):
                    link(nc.vector.tensor_tensor(XN[:, t, :], XN[:, t, :], ROW[:, :], ALU.mult))
                    link(nc.vector.tensor_tensor(X[:, t, :], X[:, t, :], XN[:, t, :], ALU.add))
            barrier(eng, who)

        PJ = A[:, 0:NT * IN_COLS].rearrange("p (t n) -> p t n", t=NT)
        o1 = NT * IN_COLS
        Y = A[:, o1:o1 + 4096].rearrange("p (t n) -> p t n", t=NT)
        o2 = o1 + 4096
        R1 = over("HH", "HH_scratch", 0, 4096, F32)
        R2 = over("HL", "HL_scratch", 0, 4096, F32)
        RT = R1.rearrange("p (k t) -> p k t", k=8)
        QT = R2.rearrange("p (k t) -> p k t", k=8)
        KT = A[:, o2:o2 + 2048].rearrange("p (k t) -> p k t", k=4)
        o3 = o2 + 2048
        W3 = A[:, o3:22528]
        assert 22528 - o3 >= 4608
        ROPED = [(RQ + 64 * h) for h in range(8)] + [NQ + 64 * h for h in range(8)] + \
                [KSL, KSL + 64, KWN, KWN + 64]


        def bc(ap, shape):
            return ap.to_broadcast(shape)

        def rope_dve(link):
            for t in range(NT):
                for o, n in ((RQ, 8), (NQ, 8), (KSL, 2), (KWN, 2)):
                    src = PJ[:, t, o:o + n * DK].rearrange("p (h x) -> p h x", x=DK)
                    c = con("cos")[:, t * DK:(t + 1) * DK].unsqueeze(1).to_broadcast([P, n, DK])
                    s = con("sin")[:, t * DK:(t + 1) * DK].unsqueeze(1)
                    a = R1[:, 0:n * DK].rearrange("p (h x) -> p h x", x=DK)
                    b = R2[:, 0:n * DK].rearrange("p (h x) -> p h x", x=DK)
                    nc.vector.tensor_tensor(a, src, c, ALU.mult)
                    nc.vector.tensor_tensor(b[:, :, 0:32], src[:, :, 32:64],
                                            s[:, :, 0:32].to_broadcast([P, n, 32]), ALU.mult)
                    link(nc.vector.tensor_tensor(b[:, :, 32:64], src[:, :, 0:32],
                                                 s[:, :, 32:64].to_broadcast([P, n, 32]), ALU.mult))
                    link(nc.vector.tensor_tensor(src, a, b, ALU.add))

        DEC = W3[:, 0:2048].rearrange("p (h x) -> p h x", h=RH)
        SR = W3[:, 2048:2048 + 2 * 1280].rearrange("p (r x) -> p r x", r=2)
        sr_at = [0, 512, 896, 1152]
        bn6, mv = misc(16 * 6), misc(32)

        BLK = W3[:, 0:1024].rearrange("p (k m) -> p k m", k=16)
        BLHr = over("A", "BLH", o3 + 1024, 1024, F32R).rearrange("p (k m) -> p k m", k=16)
        BLLr = over("A", "BLL", o3 + 2048, 1024, F32R).rearrange("p (k m) -> p k m", k=16)
        BLH = BLHr.bitcast(F32)
        HID = W3[:, 3072:3072 + 512].rearrange("p (f g r n) -> p f g r n", f=2, g=2, r=4)
        HIDK = R1[:, 1024:1152].rearrange("p (f m) -> p f m", f=2)
        DUP = R1[:, 0:1024].rearrange("p (t g j x) -> p t g j x", t=NT, g=2, j=2)
        W2 = W3[:, 3584:3584 + 256].rearrange("p (w f n) -> p w f n", w=2, f=2)
        POS = W3[:, 3840:3840 + 32].rearrange("p (w k) -> p w k", w=2)
        KC = W3[:, 3872:3872 + 192].rearrange("p (a n) -> p a n", a=3)
        KCT = W3[:, 4064:4128]
        VBD = W3[:, 4128:4640].rearrange("p (g r n) -> p g r n", g=2, r=4)
        CT = PJ[:, 0, RQ:RQ + 512], PJ[:, 1, RQ:RQ + 512]
        E4 = R1[:, 0:1024].rearrange("p (t h n) -> p t h n", t=NT, h=NH)
        PTC = R1[:, 1024:2048].rearrange("p (u t) -> p u t", u=8)
        mx4, z4 = misc(32), misc(32)
        gates = misc(NT * 24).rearrange("p (t g h) -> p t g h", t=NT, g=3)
        EX = W3[:, 0:1024].rearrange("p (r x) -> p r x", r=2)
        PT = W3[:, 1024:2048].rearrange("p (r x) -> p r x", r=2)
        OT = W3[:, 2048:3072].rearrange("p (r x) -> p r x", r=2)
        nmax, zsum = misc(64), misc(64)

        units = [(b, t, h) for b in range(2) for t in range(NT) for h in range(NH)]

        GT = A[:, 0:NF * S].rearrange("p (k t) -> p k t", k=NF)
        CV = A[:, NF * S:NF * S + 2048].rearrange("p (r t) -> p r t", r=4)
        GSHr = over("A", "GSH", NF * S + 2048, 2048, F32R).rearrange("p (r t) -> p r t", r=4)
        GSLr = over("A", "GSL", NF * S + 4096, 2048, F32R).rearrange("p (r t) -> p r t", r=4)
        GSH = GSHr.bitcast(F32)

        CA = misc(8)
        CABr = over("HH", "CAB", 2048, 2048, F32R).rearrange("p (s k n) -> p s k n", s=2, k=NK)
        CAB = CABr.bitcast(F32)
        MOD = misc(32)
        MASKr = over("A", "MASK", o3 + 4640, 2 * P, F32R).rearrange("p (s n) -> p s n", s=2)
        MODROW = W3[:, 3072:4096]
        ADA_EVERY = 10

        def ada_at(s):
            return (s // ADA_EVERY, s % ADA_EVERY) if s < 6 * ADA_EVERY else (6, 0)

        LEVELS = (64, 32, 16, 8, 4, 2, 1)
        def reg(n, k=4):
            return A[:, n * 2048:(n + 1) * 2048].rearrange("p (k t) -> p k t", k=k)

        HQ, HF, HG, HV, CB, CC, CX = (reg(n) for n in range(7))
        HK, SC8, SC9 = reg(7), reg(8), reg(9)
        RST = A[:, 20992:22528]
        LEVEL = RST[:, 0:1024].bitcast(U32).rearrange("p (n t) -> p n t", n=8)
        STATE = RST.rearrange("p (c h n) -> p c h n", c=3, h=4)
        lb, oml, lbt = misc(4), misc(4), misc(12)
        eb = misc(16)

        SS = A[:, 0:8192].rearrange("p (t f n) -> p t f n", t=NT, f=16)
        SUBK = A[:, 8192:10240].rearrange("p (f n) -> p f n", f=16)
        QE = A[:, 10240:11264].rearrange("p (r t) -> p r t", r=2)
        XF = X.rearrange("p t n -> p (t n)")
        TV = XF[:, 0:1024].rearrange("p (t f k) -> p t f k", t=NT, f=16)
        TIU = XF[:, 1024:2048].rearrange("p (t f k) -> p t f k", t=NT, f=16)
        BV = XF[:, 2048:2304].rearrange("p (r h k) -> p r h k", r=2, h=PH)
        BI = XF[:, 2304:2432].rearrange("p (h k) -> p h k", h=PH)
        CAND, CAND2 = XF[:, 2432:2688], XF[:, 2688:2944]
        PAB = XF[:, 2944:3200].rearrange("p (s u) -> p s u", s=2)
        N12 = XF[:, 3200:3712].rearrange("p (r s u) -> p r s u", r=2, s=2)
        TFf = XF[:, 3712:3968]
        TF = TFf.rearrange("p (s h k) -> p s h k", s=2, h=PH)
        WORK = XF[:, 3968:4096]
        EQ = A[:, 20480:21504].rearrange("p (h k a) -> p h k a", h=PH // 2, k=TOPK)
        LST = A[:, 21504:22272].rearrange("p (r l t) -> p r l t", r=2, l=3)
        zg, zs8 = misc(8), misc(8)
        HALF = 64
        STG = A[:, 0:16384].rearrange("p (r i t) -> p r i t", r=2, i=P)
        OHA = A[:, 16384:18432].rearrange("p (r n) -> p r n", r=16)
        OHB = A[:, 18432:20480].rearrange("p (r n) -> p r n", r=16)
        WGTr = over("A", "WGT", 0, 16384, F32R).rearrange("p (b s i t) -> p b s i t", b=2, s=2, i=GROUP)
        WGT = WGTr.bitcast(F32)
        GR_ = A[:, 16384:18432].rearrange("p (r t) -> p r t", r=4)
        GE = A[:, 18432:19456].rearrange("p (r t) -> p r t", r=2)
        WF = A[:, 19456:20480].rearrange("p (r t) -> p r t", r=2)
        YA = X

        ffc = par("ffconv").rearrange("p (m w) -> p m w", w=3)
        def flat(r):
            return r.rearrange("p k t -> p (k t)")

        def experts(eng, step):
            cx = FIRST["experts"]
            step((cx, 0, 0), 0, 0, True, False)
            with eng.Fori(0, (NGRP - 2) // 2) as i:
                for s in range(2):
                    step((cx + GROUP + 2 * GROUP * s, i, 4 * GROUP), i * (2 * GROUP) + GROUP * (1 + s), (1 + s) % 2,
                         True, True)
            step((cx + GROUP + 2 * GROUP * (NGRP - 2), 0, 0), GROUP * (NGRP - 1), 1, True, True)
            step((cx + GROUP + 2 * GROUP * (NGRP - 1), 0, 0), GROUP * NGRP, 0, False, True)

        block = ctx.enter_context(nc.Block())
        dr = d

        @block.sync
        def _(sp):
            def load(c, src, w=CW):
                v = number(c, 1 - RING)
                wait(sp, "low_done", v)
                dst = RAW[:, slot(c), 0:w]
                if len(src.shape) == 3:
                    dst = dst.rearrange("p (a b) -> p a b", a=src.shape[1])
                sp.dma_start(dst, src).then_inc(sem(f"raw_landed{slot(c)}"), 16)

            win = dr["w_in"].rearrange("(q k p) n -> q p k n", q=4, p=P)
            for b in range(6):
                w = 512 if b < 5 else TAIL
                for q in range(4):
                    load((4 * b + q, 0, 0), win[q, :, :, b * 512:b * 512 + w], 2 * w)
            c0 = FIRST["cmp"]
            for n in range(8):
                load((c0 + n, 0, 0), dr["cmp_w1"][n])

            def looped(name, n, src, per=4):
                c0 = FIRST[name]
                with sp.Fori(0, n // per) as i:
                    for j in range(per):
                        load((c0 + j, i, per), src(i * per + j))

            c0 = FIRST["ada"]
            ada = dr["w_ada"].rearrange("(k p) (v n) -> v k p n", p=P, v=6)
            with sp.Fori(0, 6) as i:
                for k in range(NK):
                    load((c0 + k, i, NK), ada[i, k])
            c0 = FIRST["wout"]
            for k in range(NK):
                load((c0 + k, 0, 0), dr["w_out"][k * P:(k + 1) * P, :])
            looped("up", 2 * NF, lambda m: dr["ffn_up"][m])
            c0 = FIRST["down"]
            for k in range(NF):
                load((c0 + k, 0, 0), dr["ffn_down"][k * P:(k + 1) * P, :])
            looped("win2", 28, lambda m: dr["win2"][m])
            looped("wout2", 8, lambda m: dr["w_out2"].rearrange("(k p) n -> k p n", p=P)[m])
            looped("query", 16, lambda m: dr["query"][m])
            vv = dr["peer_v"].rearrange("(a g q r) n -> g q a r n", a=P, g=NGRP, r=2)

            def step(c, g8, b, u, v):
                n = 0
                g = g8 // GROUP if isinstance(g8, int) else group_of(c)
                for half in range(2):
                    if u:
                        for m in range(4 * half, 4 * half + 4):
                            load(plus(c, n), dr["peer_u"][g8 + m])
                            n += 1
                    if v:
                        for q in range(4):
                            load(plus(c, n), vv[g - 1, q][:, :, half * 512:(half + 1) * 512])
                            n += 1

            def group_of(c):
                return c[1] * 2 + (c[0] - FIRST["experts"] + GROUP) // (2 * GROUP)
            experts(sp, step)

        @block.gpsimd
        def _(pool):
            xt = dr["x"].rearrange("(t p) n -> p t n", p=P)
            pool.dma_start(X, xt).then_inc(sem("x_landed"), 16)
            pool.dma_start(CON[:, :], dr["const"]).then_inc(sem("const_landed"), 16)
            pool.dma_start(PAR[:, :], dr["param"]).then_inc(sem("param_landed"), 16)
            pool.dma_start(ROW[:, :], dr["nm_post"].partition_broadcast(P)).then_inc(sem("row_landed"), 16)
            for g in range(2):
                pool.dma_start(GATE[:, g, :], dr["bada_gate"][g].partition_broadcast(P)).then_inc(sem("gb_landed"), 16)
            pool.wait_ge(sem("phase_ended"), 3 * 2)
            pool.dma_start(DEC, dr["decay"].rearrange("p (h x) -> p h x", h=RH)).then_inc(sem("decay_landed"), 16)
            pool.wait_ge(sem("phase_ended"), 3 * 4)
            pool.dma_start(W2, dr["cmp_w2"].rearrange("w (f p) n -> p w f n", p=P)).then_inc(sem("w2_landed"), 16)
            pool.dma_start(POS, dr["cmp_pos"]).then_inc(sem("w2_landed"), 16)
            pool.wait_ge(sem("phase_ended"), 3 * 10)
            pool.dma_start(ROW[:, :], dr["nf_post"].partition_broadcast(P)).then_inc(sem("row_landed"), 16)
            pool.wait_ge(sem("phase_ended"), 3 * 14)
            pool.dma_start(ROW[:, :], dr["final_w"].partition_broadcast(P)).then_inc(sem("row_landed"), 16)
            pool.dma_start(RST[:, 0:1024], dr["levels"].bitcast(F32)).then_inc(sem("levels_landed"), 16)
            pool.wait_ge(sem("phase_ended"), 3 * 20)
            pool.dma_start(dr["x3"], X).then_inc(sem("x3_saved"), 16)
            pool.dma_start(SUBK, dr["subk"]).then_inc(sem("subkeys_landed"), 16)

            def places_apart(t, i):
                pool.wait_ge(sem("eq_summed"), i + (4 * t + 1))
                p3 = PAB.rearrange("p s u -> p (s u)")[:, bass.ds(i * 64, 64)].rearrange("p (h k) -> p h k", k=TOPK).unsqueeze(3)
                it = con("iota")[:, 0:TOPK].unsqueeze(1).unsqueeze(1)
                nc.gpsimd.tensor_tensor(EQ, p3.to_broadcast([P, PH // 2, TOPK, TOPK]),
                                        it.to_broadcast([P, PH // 2, TOPK, TOPK]), ALU.subtract).then_inc(sem("eq_ready"), 1)

            def rows_apart(t, i, rs):
                for r in rs:
                    pool.wait_ge(sem("gm_ready"), i * 8 + (32 * t + 2 * r + 2))
                    rows = OHA[:, 8 * (r % 2):8 * (r % 2) + 8, :]
                    nums = LST[:, t % 2, 0, bass.ds(i * 32 + 8 * r, 8)].unsqueeze(2).to_broadcast([P, 8, P])
                    nc.gpsimd.tensor_tensor(rows, con("iota").unsqueeze(1).to_broadcast([P, 8, P]), nums,
                                            ALU.subtract).then_inc(sem("rows_apart"), 1)

            for s_ in range(1, NT + 2):
                if s_ <= NT:
                    pool.wait_ge(sem("places_ready"), s_)
                if s_ >= 2:
                    pool.wait_ge(sem("list_stored"), s_ - 1)
                with pool.Fori(0, 4) as i:
                    if s_ >= 2:
                        rows_apart(s_ - 2, i, range(2))
                    if s_ <= NT:
                        places_apart(s_ - 1, i)
                    if s_ >= 2:
                        rows_apart(s_ - 2, i, range(2, 4))
            pool.wait_ge(sem("phase_ended"), 3 * 24)
            pool.dma_start(XN, dr["x3"]).then_inc(sem("x3_back"), 16)
            pool.wait_ge(sem("x3_back"), 16)
            pool.wait_ge(sem("out_ready"), NT)
            pool.dma_start(dr["out"].rearrange("(t p) n -> p t n", p=P), X).then_inc(sem("out_landed"), 16)
            pool.wait_ge(sem("out_landed"), 16)
            for r in range(2):
                pool.wait_ge(sem(f"gates_written{r}"), 16 * NT)

        @block.scalar
        def _(act):
            link = link_for(act, "act_step")
            for n in range(LEAD):
                split_high(act, (n, 0, 0))
            act.wait_ge(sem("const_landed"), 16)
            act.wait_ge(sem("param_landed"), 16)
            act.wait_ge(sem("x_landed"), 16)
            norm_turn(act, "act", "pre1", link)
            for b in range(6):
                w = 512 if b < 5 else TAIL
                for q in range(4):
                    n = 4 * b + q + LEAD
                    split_high(act, (n, 0, 0), CW if n < 20 or n >= 24 else 2 * TAIL)
                act.wait_ge(sem("chunk_used"), 4 * b + 4)
                for t in range(NT):
                    last = nc.scalar.activation(PJ[:, t, b * 512:b * 512 + w], PS[:, 4 * (b % 2) + t, 0:w], ACT.Copy)
                last.then_inc(sem("proj_stored"), 1)
            barrier(act, "act")
            nc.scalar.activation(gates.rearrange("p t g h -> p t (g h)"), PJ[:, :, NG:NG + 24], ACT.Sigmoid)
            link(nc.scalar.activation(PJ[:, :, RG:RG + 512], PJ[:, :, RG:RG + 512], ACT.Silu))
            barrier(act, "act")
            for n in range(20):
                act.wait_ge(sem("head_turned"), n + 1)
                dst = RT[0:64, n, :] if n < 8 else QT[0:64, n - 8, :] if n < 16 else KT[0:64, n - 16, :]
                nc.scalar.activation(dst, PS[0:64, n % 8, :], ACT.Copy,
                                     scale=DK ** -0.5 if 8 <= n < 16 else 1.0).then_inc(sem("head_stored"), 1)
            act.wait_ge(sem("gn_var"), 1)
            nc.scalar.activation(mv.rearrange("p (u s) -> p u s", s=2)[:, :, 1], mv.rearrange("p (u s) -> p u s", s=2)[:, :, 1],
                                 ACT.Sqrt).then_inc(sem("gn_root"), 1)
            barrier(act, "act")
            for w in range(2):
                act.wait_ge(sem("cmp_turned"), w + 1)
                for g in range(2):
                    last = nc.scalar.activation(CT[g], PS[:, g, :], ACT.Copy)
                last.then_inc(sem("cmp_stored"), 1)
                act.wait_ge(sem("blk_ready"), w + 1)
                nc.scalar.activation(BLHr, BLK, ACT.Copy).then_inc(sem("blk_high"), 1)
                for q in range(4):
                    split_high(act, (FIRST["cmp"] + 4 * w + q + LEAD, 0, 0))
                act.wait_ge(sem("chunk_used"), FIRST["cmp"] + 4 * w + 4)
                for f in range(2):
                    for g in range(2):
                        src = PS[:, 2 + f, 32 * g:32 * g + 32]
                        if w == 0:
                            last = nc.scalar.activation(HIDK[:, f, 32 * g:32 * g + 32], src, ACT.Gelu_apprx_tanh)
                        else:
                            last = nc.scalar.activation(HID[:, f, g], src.unsqueeze(1).to_broadcast([P, 4, 32]),
                                                        ACT.Gelu_apprx_tanh)
                last.then_inc(sem("hid_gelu"), 1)
            barrier(act, "act")
            link(nc.scalar.activation(CA, par("c"), ACT.Silu))
            nc.scalar.activation(CABr[:, 0], CA.unsqueeze(2).to_broadcast([P, NK, P]), ACT.Copy)\
                .then_inc(sem("ca_high"), 1)
            nc.scalar.activation(MASKr[:, 0, :], ident, ACT.Copy)
            nc.scalar.activation(MASKr[:, 1, :], con("causal"), ACT.Copy)
            act.wait_ge(sem("cmp_shifted"), 1)
            nc.scalar.activation(E4, E4, ACT.Exp).then_inc(sem("cmp_exp"), 1)
            act.wait_ge(sem("cmp_pt"), 1)
            for n in range(2):
                last = nc.scalar.activation(PTC[:, 4 * n:4 * n + 4, :], PS[:, 4 + n, :].rearrange("p (a b) -> p a b", a=4), ACT.Copy)
            last.then_inc(sem("cmp_pt_stored"), 1)
            barrier(act, "act")
            for s in range(len(units) + 1):
                if s < len(units):
                    b, t, h = units[s]
                    w = (t + 1) * P
                    act.wait_ge(sem("at_max"), s + 1)
                    wait(act, "at_turned", s - 1)
                    nc.scalar.activation(EX[:, s % 2, 0:w], PS[:, s % 2, 0:w], ACT.Exp, bias=nmax[:, s:s + 1],
                                         accum_out=zsum[:, s:s + 1]).then_inc(sem("at_exp"), 1)
                u = s - 1
                if u >= 0 and u % 2 == 0:
                    w = (units[u][1] + 1) * P
                    act.wait_ge(sem("at_turned"), u + 1)
                    wait(act, "at_pv", u - 1)
                    nc.scalar.activation(PT[:, u % 2, 0:w], PS[:, 2 + u % 2, 0:w], ACT.Copy).then_inc(sem("at_stored0"), 1)
                v, k = ada_at(s)
                if v < 6 and k < NK:
                    split_high(act, (FIRST["ada"] + NK * v + k + LEAD, 0, 0))
                elif v in (0, 1, 3, 4) and k == NK:
                    act.wait_ge(sem("chunk_used"), FIRST["ada"] + NK * (v + 1))
                    wait(act, "mod_taken", v)
                    nc.scalar.activation(MODROW.rearrange("p (a b) -> p a b", a=2), PS[:, 6:8, :], ACT.Copy)\
                        .then_inc(sem("mod_row"), 1)
            barrier(act, "act")
            turn_act(act, "mix")
            barrier(act, "act")
            for k in range(NK):
                split_high(act, (FIRST["wout"] + k + LEAD, 0, 0))
            add_normed(act, "act", "mixpost", link)
            norm_turn(act, "act", "pre2", link)
            nc.scalar.preload_act_table(ACT.Gelu_apprx_tanh)
            cu = FIRST["up"]
            with act.Fori(0, NF // 2) as i:
                for j in range(4):
                    split_high(act, (cu + j + LEAD, i, 4))
                    act.wait_ge(sem("chunk_used"), i * 4 + (cu + j + 1))
                    act.wait_ge(sem("up_free"), i * 4 + (j + 1))
                    nc.scalar.activation(CV[:, j, :], PS[:, j, :], ACT.Copy,
                                         scale=ffc[:, i * 4 + j, 2:3]).then_inc(sem("up_tap"), 1)
                    if j % 2 == 1:
                        act.wait_ge(sem("up_conv"), i * 4 + j)
                        nc.scalar.activation(CV[:, j - 1, :], CV[:, j - 1, :], ACT.Gelu_apprx_tanh)\
                            .then_inc(sem("up_gelu"), 1)
            barrier(act, "act")
            for k in range(NF):
                if k == 0:
                    for m in range(3):
                        nc.scalar.activation(GSHr[:, m, :], GT[:, m, :], ACT.Copy).then_inc(sem("gt_high"), 1)
                c = FIRST["down"] + k
                split_high(act, (c + LEAD, 0, 0))
                if k + 3 < NF:
                    act.wait_ge(sem("chunk_used"), c)
                    nc.scalar.activation(GSHr[:, (k + 3) % 4, :], GT[:, k + 3, :], ACT.Copy)\
                        .then_inc(sem("gt_high"), 1)
            add_normed(act, "act", "ffpost", link)
            act.wait_ge(sem("lb_shifted"), 1)
            nc.scalar.activation(lbt[:, 4:12], lbt[:, 4:12], ACT.Exp).then_inc(sem("lb_exp"), 1)
            norm_turn(act, "act", "pre3", link)
            c0 = FIRST["win2"]
            for m in range(24):
                split_high(act, (c0 + m + LEAD, 0, 0))
                kind, n = m // 4, m % 4
                act.wait_ge(sem("chunk_used"), c0 + m + 1)
                src = PS[:, m % 4, :]
                if kind == 0:
                    ins = nc.scalar.activation(HQ[:, n, :], src, ACT.Copy)
                elif kind == 1:
                    nc.scalar.activation(HF[:, n, :], src, ACT.Sigmoid)
                    ins = nc.scalar.activation(HK[:, n, :], src, ACT.Sigmoid, scale=-1.0)
                elif kind == 2:
                    ins = nc.scalar.activation(HG[:, n, :], src, ACT.Silu)
                else:
                    ins = nc.scalar.activation((CB, CC, CX)[kind - 3][:, n, :], src, ACT.Copy)
                ins.then_inc(sem("p2_stored"), 1)
            for m in range(24, 28):
                split_high(act, (c0 + m + LEAD, 0, 0))
            act.wait_ge(sem("chunk_used"), c0 + 28)
            for t in range(NT):
                nc.scalar.activation(HV[:, t, :], PS[:, 4 + t, :], ACT.Copy)
            barrier(act, "act")
            act.wait_ge(sem("f_ready"), 1)
            nc.scalar.activation(HF, HF, ACT.Ln).then_inc(sem("logf"), 1)
            act.wait_ge(sem("cv_done"), 1)
            nc.scalar.activation(CC, CB, ACT.Square).then_inc(sem("cv_sq"), 1)
            act.wait_ge(sem("cv_mean"), 1)
            nc.scalar.activation(CC, CC, ACT.Sqrt).then_inc(sem("cv_root"), 1)
            barrier(act, "act")
            for n, m in enumerate(LEVELS):
                act.wait_ge(sem("lv_diff"), n + 1)
                e = flat(CC).rearrange("p (b s m) -> p b s m", s=2, m=m)
                nc.scalar.activation(e[:, :, 0, :], e[:, :, 0, :], ACT.Exp, scale=-1.0)
                nc.scalar.activation(e[:, :, 1, :], e[:, :, 1, :], ACT.Exp).then_inc(sem("lv_exp"), 1)
            barrier(act, "act")
            nc.scalar.activation(CC, CX, ACT.Exp)
            nc.scalar.activation(eb, flat(CX)[:, 127::128], ACT.Exp)
            act.wait_ge(sem("dk_diff"), 1)
            nc.scalar.activation(SC9, SC9, ACT.Exp).then_inc(sem("dk_exp"), 1)
            act.wait_ge(sem("kd_turned"), 1)
            for h in range(4):
                last = nc.scalar.activation(SC8[:, h, 0:384], PS[:, 4 + h, 0:384], ACT.Copy)
            last.then_inc(sem("kd_stored"), 1)
            act.wait_ge(sem("o_done"), 1)
            nc.scalar.activation(SC9, PS[:, 0:4, :], ACT.Square).then_inc(sem("o_sq"), 1)
            act.wait_ge(sem("o_mean"), 1)
            nc.scalar.activation(SC9, SC9, ACT.Sqrt).then_inc(sem("o_root"), 1)
            act.wait_ge(sem("y2_ready"), 1)
            nc.scalar.activation(HHr[:, 0:4, :], SC8, ACT.Copy)
            nc.scalar.activation(HHr[:, 4:8, :], CB, ACT.Copy).then_inc(sem("y2_high"), 1)
            barrier(act, "act")
            for k in range(NK):
                split_high(act, (FIRST["wout2"] + k + LEAD, 0, 0))
            barrier(act, "act")
            norm_turn(act, "act", "pre4", link)
            c0 = FIRST["query"]
            for m in range(17):
                if m < 16:
                    split_high(act, (c0 + m + LEAD, 0, 0))
                    act.wait_ge(sem("chunk_used"), c0 + m + 1)
                    wait(act, "keys_scored", m - 1)
                    nc.scalar.activation(QE[:, m % 2, :], PS[:, m % 4, :], ACT.Copy).then_inc(sem("query_stored"), 1)
                if m >= 1:
                    n = m - 1
                    act.wait_ge(sem("keys_scored"), n + 1)
                    nc.scalar.activation(SS[:, :, n, :], PS[:, 4 + n % 4, :].rearrange("p (t n) -> p t n", t=NT),
                                         ACT.Copy).then_inc(sem("scores_stored"), 1)
            barrier(act, "act")
            act.sem_inc(sem("gm_stored"), 4)
            gm = dr["gate_matrices"]
            for s_ in range(NT + 2):
                for u in (2 * s_ - 4, 2 * s_ - 3):
                    if u < 0:
                        continue

                    def onehot(i, r):
                        rows = OHA[:, 8 * r:8 * r + 8, :]
                        act.wait_ge(sem("rows_apart"), i * 2 + (8 * u + r + 1))
                        nc.scalar.activation(rows, rows, ACT.Square).then_inc(sem("rows_squared"), 1)
                        act.wait_ge(sem("rows_squared"), i * 2 + (8 * u + r + 1))
                        nc.scalar.activation(rows, rows, ACT.Relu, bias=1.0, scale=-1.0).then_inc(sem("rows_ready"), 1)

                    def store(i, qs):
                        for q in qs:
                            act.wait_ge(sem("gm_ready"), i * 4 + (16 * u + q + 5))
                            dst = STG[:, u % 2].rearrange("p i t -> p t i")[:, bass.ds(i * 16 + 4 * q, 4), :]
                            nc.scalar.activation(dst, PS[:, q, :].rearrange("p (t n) -> p t n", t=4), ACT.Copy)\
                                .then_inc(sem("gm_stored"), 1)

                    onehot(0, 0)
                    onehot(0, 1)
                    wait(act, f"gates_written{u % 2}", 16 * (u // 2))
                    store(0, (0, 1))
                    with act.Fori(1, 4) as i:
                        onehot(i, 0)
                        store(i - 1, (2, 3))
                        onehot(i, 1)
                        store(i, (0, 1))
                    store(3, (2, 3))
                    act.wait_ge(sem("gm_stored"), 16 * (u + 1) + 4)
                    act.dma_start(gm[u], STG[:, u % 2]).then_inc(sem(f"gates_written{u % 2}"), 16)
                if 1 <= s_ <= NT:
                    act.wait_ge(sem("list_turned"), s_)
                    nc.scalar.activation(LST[:, (s_ - 1) % 2], PS[:, 4, 0:3 * P].rearrange("p (l t) -> p l t", l=3), ACT.Copy)\
                        .then_inc(sem("list_stored"), 1)
                if s_ < NT:
                    act.wait_ge(sem("best_shifted"), s_ + 1)
                    nc.scalar.activation(BV[:, s_ % 2], BV[:, s_ % 2], ACT.Exp).then_inc(sem("best_exp"), 1)
            barrier(act, "act")
            cx = FIRST["experts"]
            nc.scalar.preload_act_table(ACT.Gelu)
            act.sem_inc(sem("gelu_done"), 4)

            def load_gates(e, m):
                act.dma_start(GR_[:, m % 4, :].rearrange("p (u t) -> p u t", t=HALF),
                              gm.rearrange("u p i t -> i p u t")[e]).then_inc(sem(f"gates_landed{m % 4}"), 16)

            def high(e, m, b):
                act.wait_ge(sem("w_done"), e + 3)
                nc.scalar.activation(WGTr[:, b, 0, m, :], WF[:, m % 2, :], ACT.Copy).then_inc(sem("w_high"), 1)
                if not (isinstance(e, int) and e + 4 >= P):
                    load_gates(e + 4, m)

            for r in range(2):
                act.wait_ge(sem(f"gates_written{r}"), 16 * NT)
            for m in range(4):
                load_gates(m, m)

            def step(c, g8, b, u, v):
                n = 0
                for half in range(2):
                    if u:
                        for m in range(4 * half, 4 * half + 4):
                            split_high(act, plus(c, n + LEAD))
                            act.wait_ge(sem("chunk_used"), number(c, n + 1))
                            act.wait_ge(sem("w_done"), g8 + (m + 1))
                            nc.scalar.activation(GE[:, m % 2, :], PS[:, 4 + m % 4, :], ACT.Gelu)\
                                .then_inc(sem("gelu_done"), 1)
                            high(g8 + m, m, b)
                            n += 1
                    if v:
                        for q in range(4):
                            split_high(act, plus(c, n + LEAD))
                            n += 1
            experts(act, step)
            barrier(act, "act")
            act.wait_ge(sem("x4_ready"), 1)
            rms_act(act, link, lambda t: X[:, t, :], "final")

        @block.vector
        def _(dve):
            link = link_for(dve, "dve_step")
            for n in range(LEAD):
                split_low(dve, (n, 0, 0))
            dve.wait_ge(sem("param_landed"), 16)
            dve.wait_ge(sem("x_landed"), 16)
            norm_turn(dve, "dve", "pre1", link, lambda k: par("nmp", k, k + 1))
            for b in range(6):
                for q in range(4):
                    n = 4 * b + q + LEAD
                    split_low(dve, (n, 0, 0), CW if n < 20 or n >= 24 else 2 * TAIL)
            barrier(dve, "dve")
            rope_dve(link)
            barrier(dve, "dve")
            dve.wait_ge(sem("decay_landed"), 16)
            for u in range(4 * RH):
                h, j = u // 4, u % 4
                w = S - j * P
                dve.wait_ge(sem("rt_scores"), u + 1)
                if j == 0:
                    wait(dve, "rt_out", h - 1)
                nc.vector.tensor_tensor(SR[:, h % 2, sr_at[j]:sr_at[j] + w], PS[:, u % 4, 0:w], DEC[:, h, 0:w],
                                        ALU.mult).then_inc(sem("rt_decayed"), 1)
            dve.wait_ge(sem("rt_out"), RH)
            for t in range(NT):
                for h in range(RH):
                    u = t * 4 + h
                    last = nc.vector.bn_stats(bn6[:, 6 * u:6 * u + 6], PS[:, 4 + t, h * P:(h + 1) * P])
            link(last)
            for u in range(16):
                last = nc.vector.bn_aggr(mv[:, 2 * u:2 * u + 2], bn6[:, 6 * u:6 * u + 6])
            link(last)
            var = mv.rearrange("p (u s) -> p u s", s=2)[:, :, 1]
            nc.vector.tensor_scalar(var, var, GN_EPS, None, ALU.add).then_inc(sem("gn_var"), 1)
            dve.wait_ge(sem("gn_root"), 1)
            link(nc.vector.reciprocal(var, var))
            for t in range(NT):
                for h in range(RH):
                    u = t * 4 + h
                    link(nc.vector.tensor_scalar(Y[:, t, h * P:(h + 1) * P], PS[:, 4 + t, h * P:(h + 1) * P],
                                                 mv[:, 2 * u:2 * u + 1], mv[:, 2 * u + 1:2 * u + 2],
                                                 ALU.subtract, ALU.mult))
                link(nc.vector.tensor_tensor(Y[:, t, 0:512], Y[:, t, 0:512], PJ[:, t, RG:RG + 512], ALU.mult))
            barrier(dve, "dve")
            dve.wait_ge(sem("w2_landed"), 32)
            for w in range(2):
                o = (KCM, VCM)[w]
                for t in range(NT):
                    src = PJ[:, t, o:o + 128].rearrange("p (g x) -> p g x", g=2).unsqueeze(2).to_broadcast([P, 2, 2, 64])
                    last = nc.vector.tensor_copy(DUP[:, t], src)
                last.then_inc(sem("cmp_dup"), 1)
                link(nc.vector.memset(BLK, 0.0))
                dve.wait_ge(sem("cmp_stored"), w + 1)
                for jj in range(2):
                    for g in range(2):
                        ps = slice(64 * jj, 64 * jj + 64)
                        for half in range(2):
                            src = CT[g][ps, :].rearrange("p (n k j) -> p k n j", k=8, j=2)[:, :, half:half + 31, jj]
                            last = nc.vector.tensor_tensor(
                                BLK[ps, 8 * half:8 * half + 8, 32 * g:32 * g + 31], src,
                                POS[ps, w, 8 * half:8 * half + 8].unsqueeze(2).to_broadcast([64, 8, 31]), ALU.add)
                last.then_inc(sem("blk_ready"), 1)
                dve.wait_ge(sem("blk_high"), w + 1)
                nc.vector.tensor_tensor(BLLr, BLK, BLH, ALU.subtract).then_inc(sem("blk_low"), 1)
                for q in range(4):
                    split_low(dve, (FIRST["cmp"] + 4 * w + q + LEAD, 0, 0))
                if w == 0:
                    dve.wait_ge(sem("kc_ready"), 1)
                    src = PS[0:64, 4, 0:64]
                    link(nc.vector.tensor_copy(KC[0:64, 0, :], src))
                    nc.vector.tensor_tensor(KC[0:64, 1, :], KC[0:64, 0, :], con("ccos")[0:64, :], ALU.mult)
                    nc.vector.tensor_tensor(KC[0:64, 2, 0:32], KC[0:64, 0, 32:64], con("csin")[0:64, 0:32], ALU.mult)
                    link(nc.vector.tensor_tensor(KC[0:64, 2, 32:64], KC[0:64, 0, 0:32], con("csin")[0:64, 32:64], ALU.mult))
                    nc.vector.tensor_tensor(KC[0:64, 0, :], KC[0:64, 1, :], KC[0:64, 2, :], ALU.add)\
                        .then_inc(sem("kc_roped"), 1)
                    dve.wait_ge(sem("kct_ready"), 1)
                    nc.vector.tensor_copy(KCT[0:64, :], PS[0:64, 5, 0:64]).then_inc(sem("kct_stored"), 1)
                else:
                    dve.wait_ge(sem("vc_ready"), 1)
                    for g in range(2):
                        last = nc.vector.tensor_tensor(
                            VBD[:, g], PS[:, 6 + g, 0:64].unsqueeze(1).to_broadcast([P, 4, 64]),
                            con("four").unsqueeze(2).to_broadcast([P, 4, 64]), ALU.mult)
                    link(last)
            barrier(dve, "dve")
            dve.wait_ge(sem("ca_high"), 1)
            nc.vector.tensor_tensor(CABr[:, 1], CA.unsqueeze(2).to_broadcast([P, NK, P]), CAB[:, 0], ALU.subtract)\
                .then_inc(sem("ca_low"), 1)
            dve.wait_ge(sem("cs_ready"), 1)
            sc = PS[:, 0:4, 0:256].rearrange("p t (h n) -> p t h n", h=NH)
            ok = con("cmp_ok").rearrange("p (t n) -> p t n", t=NT)
            no = con("cmp_no").rearrange("p (t n) -> p t n", t=NT)
            for t in range(NT):
                last = nc.vector.tensor_tensor(E4[:, t], sc[:, t], ok[:, t].unsqueeze(1).to_broadcast([P, NH, 32]), ALU.mult)
            link(last)
            for t in range(NT):
                last = nc.vector.tensor_tensor(E4[:, t], E4[:, t], no[:, t].unsqueeze(1).to_broadcast([P, NH, 32]), ALU.add)
            link(last)
            E4f = E4.rearrange("p t h n -> p (t h) n")
            link(nc.vector.tensor_reduce(mx4, E4f, AX, ALU.max))
            nc.vector.tensor_tensor(E4f, E4f, mx4.unsqueeze(2).to_broadcast([P, 32, 32]), ALU.subtract)\
                .then_inc(sem("cmp_shifted"), 1)
            dve.wait_ge(sem("cmp_exp"), 1)
            for t in range(NT):
                last = nc.vector.tensor_tensor(E4[:, t], E4[:, t], ok[:, t].unsqueeze(1).to_broadcast([P, NH, 32]), ALU.mult)
            link(last)
            link(nc.vector.tensor_reduce(z4, E4f, AX, ALU.add))
            link(nc.vector.tensor_scalar(z4, z4, 1e-30, None, ALU.max))
            link(nc.vector.reciprocal(z4, z4))
            nc.vector.tensor_tensor(E4f, E4f, z4.unsqueeze(2).to_broadcast([P, 32, 32]), ALU.mult)\
                .then_inc(sem("cmp_probs"), 1)
            dve.wait_ge(sem("cmp_out"), 1)
            for t in range(NT):
                last = nc.vector.tensor_tensor(
                    Y[:, t, 512:1024].rearrange("p (h n) -> p h n", h=NH), PS[:, t, :].rearrange("p (h n) -> p h n", h=NH),
                    gates[:, t, 0, :].unsqueeze(2).to_broadcast([P, NH, DK]), ALU.mult)
            link(last)
            barrier(dve, "dve")
            for s in range(len(units) + 2):
                if s < len(units):
                    b, t, h = units[s]
                    w = (t + 1) * P
                    dve.wait_ge(sem("at_scores"), s + 1)
                    nc.vector.tensor_reduce(nmax[:, s:s + 1], PS[:, s % 2, 0:w], AX, ALU.max, negate=True)\
                        .then_inc(sem("at_max"), 1)
                u = s - 1
                if 0 <= u < len(units) and u % 2 == 1:
                    w = (units[u][1] + 1) * P
                    dve.wait_ge(sem("at_turned"), u + 1)
                    wait(dve, "at_pv", u - 1)
                    nc.vector.tensor_copy(PT[:, u % 2, 0:w], PS[:, 2 + u % 2, 0:w]).then_inc(sem("at_stored1"), 1)
                v, k = ada_at(s)
                if v < 6 and k < NK:
                    if v + k > 0:
                        split_low(dve, (FIRST["ada"] + NK * v + k + LEAD - 1, 0, 0))
                elif v < 6 and k == NK and v % 3 == 2:
                    dve.wait_ge(sem("chunk_used"), FIRST["ada"] + NK * (v + 1))
                    dve.wait_ge(sem("gb_landed"), 32)
                    g2 = GATE[:, v // 3, :].rearrange("p (a b) -> p a b", a=2)
                    nc.vector.tensor_tensor(g2, g2, PS[:, 6:8, :], ALU.add).then_inc(sem("mod_taken"), 1)
                elif v < 6 and k == NK + 1 and v % 3 < 2:
                    dve.wait_ge(sem("mod_turned"), v - v // 3 + 1)
                    md = MOD[:, 16 * (v // 3) + 8 * (v % 3):16 * (v // 3) + 8 * (v % 3) + 8]
                    last = nc.vector.tensor_tensor(md, PS[:, 6, 0:8], par("bada", 8 * v, 8 * v + 8), ALU.add)
                    if v % 3 == 1:
                        link(last)
                        last = nc.vector.scalar_tensor_tensor(md, md, 1.0, par(("n1", "n2")[v // 3]), ALU.add, ALU.mult)
                    last.then_inc(sem("mod_taken"), 1)
                u = s - 2
                if u >= 0 and u % 8 == 7:
                    b, t, _ = units[u]
                    n = u // 8
                    dve.wait_ge(sem("at_pv"), u + 1)
                    zs = zsum[:, 8 * n:8 * n + 8]
                    link(nc.vector.reciprocal(zs, zs))
                    link(nc.vector.tensor_tensor(zs, zs, gates[:, t, 1 + b, :], ALU.mult))
                    ot = OT[:, n % 2, :].rearrange("p (h n) -> p h n", h=NH)
                    nc.vector.tensor_tensor(ot, PS[:, 4 + n % 2, :].rearrange("p (h n) -> p h n", h=NH),
                                            zs.unsqueeze(2).to_broadcast([P, NH, DK]), ALU.mult)\
                        .then_inc(sem("at_taken"), 1)
                    dve.wait_ge(sem("at_taken"), n + 1)
                    link(nc.vector.tensor_tensor(Y[:, t, 512:1024], Y[:, t, 512:1024], OT[:, n % 2, :], ALU.add))
            split_low(dve, (FIRST["wout"] + LEAD - 1, 0, 0))
            barrier(dve, "dve")
            turn_dve(dve, link, "mix", lambda k: par("gn", k, k + 1) if k < 4 else None)
            barrier(dve, "dve")
            for k in range(NK):
                split_low(dve, (FIRST["wout"] + k + LEAD, 0, 0))
            add_normed(dve, "dve", "mixpost", link)
            norm_turn(dve, "dve", "pre2", link, lambda k: par("nfp", k, k + 1))
            cu = FIRST["up"]
            for j in range(4):
                nc.vector.memset(CV[:, j, 0:1], 0.0).then_inc(sem("up_free"), 1)
            with dve.Fori(0, NF // 2) as i:
                for j in range(4):
                    split_low(dve, (cu + j + LEAD, i, 4))
                    dve.wait_ge(sem("up_tap"), i * 4 + (j + 1))
                    nc.vector.scalar_tensor_tensor(CV[:, j, 1:], PS[:, j, 0:S - 1], ffc[:, i * 4 + j, 1:2], CV[:, j, 1:],
                                                   ALU.mult, ALU.add).then_inc(sem("up_mid"), 1)
                    dve.wait_ge(sem("up_mid"), i * 4 + (j + 1))
                    nc.vector.scalar_tensor_tensor(CV[:, j, 2:], PS[:, j, 0:S - 2], ffc[:, i * 4 + j, 0:1], CV[:, j, 2:],
                                                   ALU.mult, ALU.add).then_inc(sem("up_conv"), 1)
                    if j % 2 == 1:
                        dve.wait_ge(sem("up_conv"), i * 4 + (j + 1))
                        dve.wait_ge(sem("up_gelu"), i * 2 + (j // 2 + 1))
                        nc.vector.tensor_tensor(GT[:, i * 2 + j // 2, :], CV[:, j - 1, :], CV[:, j, :], ALU.mult)\
                            .then_inc(sem("up_free"), 2)
            barrier(dve, "dve")
            for k in range(NF):
                if k == 0:
                    for m in range(3):
                        dve.wait_ge(sem("gt_high"), m + 1)
                        nc.vector.tensor_tensor(GSLr[:, m, :], GT[:, m, :], GSH[:, m, :], ALU.subtract)\
                            .then_inc(sem("gt_low"), 1)
                c = FIRST["down"] + k
                split_low(dve, (c + LEAD, 0, 0))
                if k + 3 < NF:
                    m = k + 3
                    dve.wait_ge(sem("gt_high"), m + 1)
                    nc.vector.tensor_tensor(GSLr[:, m % 4, :], GT[:, m, :], GSH[:, m % 4, :], ALU.subtract)\
                        .then_inc(sem("gt_low"), 1)
            add_normed(dve, "dve", "ffpost", link)
            l0, l1 = par("lb0"), par("lb1")
            link(nc.vector.tensor_tensor(lbt[:, 0:4], l0, l1, ALU.max))
            nc.vector.tensor_tensor(lbt[:, 4:8], l0, lbt[:, 0:4], ALU.subtract)
            nc.vector.tensor_tensor(lbt[:, 8:12], l1, lbt[:, 0:4], ALU.subtract).then_inc(sem("lb_shifted"), 1)
            dve.wait_ge(sem("lb_exp"), 1)
            link(nc.vector.tensor_tensor(lbt[:, 0:4], lbt[:, 4:8], lbt[:, 8:12], ALU.add))
            link(nc.vector.reciprocal(lbt[:, 0:4], lbt[:, 0:4]))
            link(nc.vector.tensor_tensor(lb, lbt[:, 4:8], lbt[:, 0:4], ALU.mult))
            link(nc.vector.tensor_scalar(oml, lb, -1.0, 1.0, ALU.mult, ALU.add))
            norm_turn(dve, "dve", "pre3", link, lambda k: MOD[:, 8 + k:9 + k], lambda k: MOD[:, k:k + 1])
            for m in range(28):
                split_low(dve, (FIRST["win2"] + m + LEAD, 0, 0))
            barrier(dve, "dve")
            for h in range(4):
                last = nc.vector.tensor_scalar(HF[:, h, :], HF[:, h, :], oml[:, h:h + 1], lb[:, h:h + 1], ALU.mult, ALU.add)
            last.then_inc(sem("f_ready"), 1)
            for h in range(4):
                nc.vector.tensor_scalar(HK[:, h, :], HK[:, h, :], oml[:, h:h + 1], None, ALU.mult)
            link(nc.vector.tensor_tensor(CC, CC, CX, ALU.mult))
            cw = par("conv").rearrange("p (n w) -> p n w", w=3)
            for n in range(4):
                link(nc.vector.tensor_scalar(CX[:, n, :], CC[:, n, :], cw[:, n, 2:3], None, ALU.mult))
                for w in (1, 0):
                    d_ = 2 - w
                    link(nc.vector.scalar_tensor_tensor(CX[:, n, d_:], CC[:, n, 0:S - d_], cw[:, n, w:w + 1], CX[:, n, d_:],
                                                        ALU.mult, ALU.add))
            nc.vector.tensor_tensor(CB, CB, CX, ALU.mult).then_inc(sem("cv_done"), 1)
            dve.wait_ge(sem("cv_sums"), 1)
            nc.vector.tensor_scalar(CC, PS[:, 0:4, :], 1.0 / P, EPS, ALU.mult, ALU.add).then_inc(sem("cv_mean"), 1)
            dve.wait_ge(sem("logf"), 1)
            dve.wait_ge(sem("cv_done"), 1)
            link(nc.vector.memset(SC8, 1.0))
            link(nc.vector.memset(flat(SC8)[:, 0::P], 0.0))
            link(nc.vector.tensor_tensor_scan(flat(CX), flat(SC8), flat(HF), 0.0, ALU.mult, ALU.add))
            dve.wait_ge(sem("cv_root"), 1)
            link(nc.vector.reciprocal(CC, CC))
            for n in range(4):
                link(nc.vector.scalar_tensor_tensor(CB[:, n, :], CB[:, n, :], par("conorm", n, n + 1), CC[:, n, :],
                                                    ALU.mult, ALU.mult))
            link(nc.vector.memset(HF, 0.0))
            link(nc.vector.memset(SC8, 0.0))
            link(nc.vector.memset(SC9, 0.0))
            barrier(dve, "dve")
            dve.wait_ge(sem("levels_landed"), 16)
            ST = HF

            def take(n):
                for h in range(4):
                    dve.wait_ge(sem("lv_scores"), 4 * n + h + 1)
                    last = nc.vector.copy_predicated(
                        ST[:, h, :].rearrange("p (c t) -> p c t", c=4),
                        LEVEL[:, n, :].unsqueeze(1).to_broadcast([P, 4, P]),
                        PS[:, 4 * (n % 2) + h, :].rearrange("p (c t) -> p c t", c=4))
                    last.then_inc(sem("lv_taken"), 1)
                dve.wait_ge(sem("lv_taken"), 4 * n + 4)

            for n, m in enumerate(LEVELS):
                b = flat(CX).rearrange("p (b x) -> p b x", x=2 * m)
                e = flat(CC).rearrange("p (b x) -> p b x", x=2 * m)
                nc.vector.tensor_tensor(e, b, b[:, :, m - 1:m].to_broadcast([P, S * 4 // (2 * m), 2 * m]), ALU.subtract)\
                    .then_inc(sem("lv_diff"), 1)
                if n >= 2:
                    take(n - 2)
                wait(dve, "lv_scores", 4 * n)
                dve.wait_ge(sem("lv_exp"), n + 1)
                view = lambda r: flat(r).rearrange("p (b s m) -> p b s m", s=2, m=m)
                nc.vector.tensor_tensor(view(SC8)[:, :, 1, :], view(HQ)[:, :, 1, :], view(CC)[:, :, 1, :], ALU.mult)
                nc.vector.tensor_tensor(view(SC9)[:, :, 0, :], view(HK)[:, :, 0, :], view(CC)[:, :, 0, :], ALU.mult)\
                    .then_inc(sem("lv_ready"), 1)
                dve.wait_ge(sem("lv_ready"), n + 1)
            for n in range(5, 8):
                take(n)
            b = flat(CX).rearrange("p (b x) -> p b x", x=P)
            nc.vector.tensor_tensor(flat(SC9).rearrange("p (b x) -> p b x", x=P), b[:, :, P - 1:P].to_broadcast([P, 16, P]), b,
                                    ALU.subtract).then_inc(sem("dk_diff"), 1)
            barrier(dve, "dve")
            dve.wait_ge(sem("dk_exp"), 1)
            nc.vector.tensor_tensor(SC9, SC9, HK, ALU.mult).then_inc(sem("kd_ready"), 1)
            nc.vector.tensor_tensor(CC, CC, HQ, ALU.mult).then_inc(sem("qx_ready"), 1)
            for c in range(3):
                dve.wait_ge(sem("kv_ready"), c + 1)
                for h in range(4):
                    ps = PS[:, 4 + c, h * P:(h + 1) * P]
                    if c == 0:
                        last = nc.vector.tensor_copy(STATE[:, 0, h, :], ps)
                    else:
                        last = nc.vector.scalar_tensor_tensor(STATE[:, c, h, :], STATE[:, c - 1, h, :],
                                                              eb[:, 4 * h + c:4 * h + c + 1], ps, ALU.mult, ALU.add)
                last.then_inc(sem("state_ready"), 1)
                dve.wait_ge(sem("state_ready"), c + 1)
            dve.wait_ge(sem("o_sums"), 1)
            nc.vector.tensor_scalar(SC9, PS[:, 4:8, :], 1.0 / P, EPS, ALU.mult, ALU.add).then_inc(sem("o_mean"), 1)
            dve.wait_ge(sem("o_root"), 1)
            link(nc.vector.reciprocal(SC9, SC9))
            for h in range(4):
                last = nc.vector.scalar_tensor_tensor(SC8[:, h, :], PS[:, h, :], par("onorm", h, h + 1), SC9[:, h, :],
                                                      ALU.mult, ALU.mult)
            link(last)
            nc.vector.tensor_tensor(SC8, SC8, HG, ALU.mult).then_inc(sem("y2_ready"), 1)
            dve.wait_ge(sem("y2_high"), 1)
            nc.vector.tensor_tensor(HLr[:, 0:4, :], SC8, HH[:, 0:4, :], ALU.subtract)
            nc.vector.tensor_tensor(HLr[:, 4:8, :], CB, HH[:, 4:8, :], ALU.subtract)
            barrier(dve, "dve")
            for k in range(NK):
                split_low(dve, (FIRST["wout2"] + k + LEAD, 0, 0))
            dve.wait_ge(sem("chunk_used"), FIRST["wout2"] + NK)
            for t in range(NT):
                x2 = XN[:, t, :].rearrange("p (a b) -> p a b", a=2)
                link(nc.vector.tensor_tensor(x2, banks(t), GATE[:, 0, :].rearrange("p (a b) -> p a b", a=2), ALU.mult))
                nc.vector.tensor_tensor(X[:, t, :], X[:, t, :], XN[:, t, :], ALU.add)
            barrier(dve, "dve")
            norm_turn(dve, "dve", "pre4", link, lambda k: MOD[:, 24 + k:25 + k], lambda k: MOD[:, 16 + k:17 + k])
            TI = TIU.bitcast(U32)
            c0 = FIRST["query"]

            def best16(vals, idx, src, work):
                link(nc.vector.max(vals[:, 0:8], src))
                nc.vector.max_index(idx[:, 0:8], vals[:, 0:8], src)
                link(nc.vector.match_replace(work, vals[:, 0:8], src, -3.0e38))
                link(nc.vector.max(vals[:, 8:16], work))
                link(nc.vector.max_index(idx[:, 8:16], vals[:, 8:16], work))

            dve.wait_ge(sem("x3_saved"), 16)
            for m in range(16):
                split_low(dve, (c0 + m + LEAD, 0, 0))
                if m >= 1:
                    dve.wait_ge(sem("scores_stored"), m)
                    for t in range(NT):
                        best16(TV[:, t, m - 1, :], TI[:, t, m - 1, :], SS[:, t, m - 1, :], WORK[:, 0:PK])
            dve.wait_ge(sem("scores_stored"), 16)
            for t in range(NT):
                best16(TV[:, t, 15, :], TI[:, t, 15, :], SS[:, t, 15, :], WORK[:, 0:PK])
            barrier(dve, "dve")
            BIu = BI.bitcast(U32)
            PABu = PAB.bitcast(U32)

            TVf = TV.rearrange("p t f k -> p (t f k)")

            def pairs(t, i, h):
                cand = CAND.rearrange("p (a b) -> p a b", a=TOPK)
                a = TVf[:, bass.ds(i * 64 + (256 * t + 32 * h), TOPK)]
                b = TVf[:, bass.ds(i * 64 + (256 * t + 32 * h + TOPK), TOPK)]
                link(nc.vector.tensor_tensor(cand, a.unsqueeze(2).to_broadcast([P, TOPK, TOPK]),
                                             b.unsqueeze(1).to_broadcast([P, TOPK, TOPK]), ALU.add))
                best16(BV[:, t % 2, 2 * i + h, :], BIu[:, 2 * i + h, :], CAND, CAND2)

            def summed(t, i):
                dve.wait_ge(sem("eq_ready"), i + (4 * t + 1))
                for h in range(PH // 2):
                    num = TFf[:, bass.ds(i * 64 + 16 * h, TOPK)].unsqueeze(1).to_broadcast([P, TOPK, TOPK])
                    last = nc.vector.scalar_tensor_tensor(EQ[:, h], EQ[:, h], 0.0, num, ALU.is_equal, ALU.mult)
                last.then_inc(sem("eq_numbers"), 1)
                dve.wait_ge(sem("eq_numbers"), i + (4 * t + 1))
                nc.vector.tensor_reduce(N12[:, t % 2].rearrange("p s u -> p (s u)")[:, bass.ds(i * 64, 64)],
                                        EQ.rearrange("p h k a -> p (h k) a"), AX, ALU.add).then_inc(sem("eq_summed"), 1)

            def gated_rows(t, i, js):
                for j in js:
                    if j % 4 == 0:
                        dve.wait_ge(sem("gm_ready"), i * 8 + (32 * t + j // 4 + 1))
                    tok = i * 32 + j
                    nc.vector.tensor_scalar(OHB[:, j % 16, :], con("iota"), LST[:, t % 2, 1, bass.ds(tok, 1)],
                                            LST[:, t % 2, 2, bass.ds(tok, 1)], ALU.is_equal, ALU.mult)\
                        .then_inc(sem("onehot_ready"), 1)

            dve.sem_inc(sem("eq_summed"), 1)
            for s_ in range(NT + 2):
                if s_ < NT:
                    wait(dve, "list_turned", s_ - 1)
                if s_ >= 2:
                    dve.wait_ge(sem("list_stored"), s_ - 1)

                def turn(i):
                    for h in range(2):
                        if s_ >= 2:
                            gated_rows(s_ - 2, i, range(16 * h, 16 * h + 8))
                        if s_ < NT:
                            pairs(s_, i, h)
                        if s_ >= 2:
                            gated_rows(s_ - 2, i, range(16 * h + 8, 16 * h + 16))
                    if 1 <= s_ <= NT:
                        summed(s_ - 1, i)

                if s_ < NT:
                    for i in range(4):
                        turn(i)
                else:
                    with dve.Fori(0, 4) as i:
                        turn(i)
                if 1 <= s_ <= NT:
                    t = s_ - 1
                    dve.wait_ge(sem("best_exp"), t + 1)
                    dve.wait_ge(sem("eq_summed"), 4 * t + 5)
                    link(nc.vector.tensor_reduce(zg, BV[:, t % 2], AX, ALU.add))
                    link(nc.vector.reciprocal(zg, zg))
                    nc.vector.tensor_tensor(BV[:, t % 2], BV[:, t % 2], zg.unsqueeze(2).to_broadcast([P, PH, TOPK]),
                                            ALU.mult).then_inc(sem("list_ready"), 1)
                if s_ < NT:
                    link(nc.vector.tensor_copy(zs8, BV[:, s_ % 2, :, 0]))
                    nc.vector.tensor_tensor(BV[:, s_ % 2], BV[:, s_ % 2], zs8.unsqueeze(2).to_broadcast([P, PH, TOPK]),
                                            ALU.subtract).then_inc(sem("best_shifted"), 1)
                    bi = BIu.rearrange("p h k -> p (h k)")
                    nc.vector.tensor_scalar(PABu[:, 0], bi, 4, None, ALU.logical_shift_right)
                    link(nc.vector.tensor_scalar(PABu[:, 1], bi, 15, None, ALU.bitwise_and))
                    nc.vector.tensor_copy(TF, TI[:, s_].rearrange("p (h s) k -> p s h k", s=2))
                    nc.vector.tensor_copy(PAB, PABu).then_inc(sem("places_ready"), 1)
            barrier(dve, "dve")
            for t in range(NT):
                nc.vector.memset(YA[:, t, :], 0.0)
            dve.drain().then_inc(sem("acc_done"), 1)
            dve.wait_ge(sem("acc_done"), 1)
            nc.vector.memset(WF[:, 0, 0:1], 0.0).then_inc(sem("w_done"), 2)

            def step(c, g8, b, u, v):
                n = 0
                for half in range(2):
                    if u:
                        for m in range(4 * half, 4 * half + 4):
                            split_low(dve, plus(c, n + LEAD))
                            dve.wait_ge(sem("gelu_done"), g8 + (m + 5))
                            dve.wait_ge(sem(f"gates_landed{m % 4}"), (g8 * 4 + 16) if m < 4 else (g8 * 4 + 32))
                            dve.wait_ge(sem("w_done"), g8 + (m + 2))
                            nc.vector.tensor_tensor(WF[:, m % 2, :], GE[:, m % 2, :], GR_[:, m % 4, :], ALU.mult)\
                                .then_inc(sem("w_done"), 1)
                            dve.wait_ge(sem("w_high"), g8 + (m + 1))
                            nc.vector.tensor_tensor(WGTr[:, b, 1, m, :], WF[:, m % 2, :], WGT[:, b, 0, m, :],
                                                    ALU.subtract).then_inc(sem("w_low"), 1)
                            n += 1
                    if v:
                        for q in range(4):
                            split_low(dve, plus(c, n + LEAD))
                            n += 1
                        dve.wait_ge(sem("chunk_used"), number(c, n))
                        for t in range(NT):
                            acc = YA[:, t, half * 512:(half + 1) * 512]
                            last = nc.vector.tensor_tensor(acc, acc, PS[:, t, :], ALU.add)
                        last.then_inc(sem("acc_done"), 1)
            experts(dve, step)
            barrier(dve, "dve")
            dve.wait_ge(sem("x3_back"), 16)
            for t in range(NT):
                link(nc.vector.tensor_tensor(YA[:, t, :], YA[:, t, :], GATE[:, 1, :], ALU.mult))
                link(nc.vector.tensor_tensor(X[:, t, :], YA[:, t, :], XN[:, t, :], ALU.add))
            nc.vector.memset(WF[:, 0, 0:1], 0.0).then_inc(sem("x4_ready"), 1)
            rms_dve(dve, link, "final")
            dve.wait_ge(sem("row_landed"), 48)
            for t in range(NT):
                nc.vector.scalar_tensor_tensor(X[:, t, :], X[:, t, :], rstd[:, t:t + 1], ROW[:, :], ALU.mult, ALU.mult)\
                    .then_inc(sem("out_ready"), 1)

        @block.tensor
        def _(pe):
            pe.wait_ge(sem("const_landed"), 16)
            norm_turn(pe, "pe", "pre1")
            for b in range(6):
                w = 512 if b < 5 else TAIL
                wait(pe, "proj_stored", b - 1)
                for q in range(4):
                    mm_n2(pe, (4 * b + q, 0, 0), q, 4 * (b % 2), w)
            barrier(pe, "pe")
            barrier(pe, "pe")
            for n in range(20):
                wait(pe, "head_stored", n - 7)
                o = ROPED[n]
                for t in range(NT):
                    last = nc.tensor.transpose(PS[0:64, n % 8, t * P:(t + 1) * P], PJ[:, t, o:o + DK], ident)
                last.then_inc(sem("head_turned"), 1)
            pe.wait_ge(sem("head_stored"), 20)
            def rt_out(h):
                pe.wait_ge(sem("rt_decayed"), 4 * h + 4)
                for t in range(NT):
                    for j in range(t + 1):
                        o = sr_at[j] + (t - j) * P
                        last = nc.tensor.matmul(PS[:, 4 + t, h * P:(h + 1) * P], SR[:, h % 2, o:o + P],
                                                PJ[:, j, RV + h * P:RV + (h + 1) * P], start=(j == 0), stop=(j == t))
                last.then_inc(sem("rt_out"), 1)

            for h in range(RH):
                for j in range(NT):
                    u = 4 * h + j
                    wait(pe, "rt_decayed", u - 3)
                    nc.tensor.matmul(PS[:, u % 4, 0:S - j * P], RT[0:64, 4 + h, j * P:(j + 1) * P],
                                     RT[0:64, h, j * P:S], start=True, stop=True).then_inc(sem("rt_scores"), 1)
                if h >= 1:
                    rt_out(h - 1)
            rt_out(RH - 1)
            barrier(pe, "pe")
            for w in range(2):
                pe.wait_ge(sem("cmp_dup"), w + 1)
                for g in range(2):
                    for t in range(NT):
                        last = nc.tensor.transpose(PS[:, g, t * P:(t + 1) * P],
                                                   DUP[:, t, g].rearrange("p j x -> p (j x)"), ident)
                last.then_inc(sem("cmp_turned"), 1)
                pe.wait_ge(sem("blk_low"), w + 1)
                for q in range(4):
                    c = (FIRST["cmp"] + 4 * w + q, 0, 0)
                    pe.wait_ge(sem("low_done"), number(c, 1))
                    wh = WHr[:, slot(c), :].rearrange("p (k n) -> p k n", k=4)
                    wl = WLr[:, slot(c), :].rearrange("p (k n) -> p k n", k=4)
                    for kk in range(4):
                        k = 4 * q + kk
                        for f in range(2):
                            fs = slice(f * P, (f + 1) * P)
                            last = mm3(PS[:, 2 + f, 0:64], (wh[:, kk, fs], wl[:, kk, fs]),
                                       (BLHr[:, k, :], BLLr[:, k, :]), k == 0, k == 15)
                    last.then_inc(sem("chunk_used"), 1)
                pe.wait_ge(sem("hid_gelu"), w + 1)
                pe.wait_ge(sem("w2_landed"), 32)
                if w == 0:
                    for f in range(2):
                        last = nc.tensor.matmul(PS[0:64, 4, 0:64], HIDK[:, f, :], W2[:, 0, f, :],
                                                start=(f == 0), stop=(f == 1))
                    last.then_inc(sem("kc_ready"), 1)
                    pe.wait_ge(sem("kc_roped"), 1)
                    nc.tensor.transpose(PS[0:64, 5, 0:64], KC[0:64, 0, :], ident[0:64, 0:64]).then_inc(sem("kct_ready"), 1)
                else:
                    for g in range(2):
                        for f in range(2):
                            last = nc.tensor.matmul(PS[:, 6 + g, 0:64], HID[:, f, g].rearrange("p r n -> p (r n)"), W2[:, 1, f, :],
                                                    start=(f == 0), stop=(f == 1))
                    last.then_inc(sem("vc_ready"), 1)
            barrier(pe, "pe")
            for t in range(NT):
                for h in range(NH):
                    g = h // 4
                    last = nc.tensor.matmul(PS[:, t, 32 * h:32 * h + 32], QT[0:64, h, t * P:(t + 1) * P],
                                            KCT[0:64, 32 * g:32 * g + 32], start=True, stop=True)
            last.then_inc(sem("cs_ready"), 1)
            pe.wait_ge(sem("cmp_probs"), 1)
            for t in range(NT):
                for g in range(2):
                    u = 2 * t + g
                    last = nc.tensor.transpose(PS[:, 4 + u // 4, (u % 4) * P:(u % 4 + 1) * P],
                                               E4[:, t, 4 * g:4 * g + 4, :].rearrange("p h n -> p (h n)"), ident)
            last.then_inc(sem("cmp_pt"), 1)
            pe.wait_ge(sem("cmp_pt_stored"), 1)
            for t in range(NT):
                for g in range(2):
                    last = nc.tensor.matmul(PS[:, t, 256 * g:256 * g + 256], PTC[:, 2 * t + g, :],
                                            VBD[:, g].rearrange("p r n -> p (r n)"), start=True, stop=True)
            last.then_inc(sem("cmp_out"), 1)
            barrier(pe, "pe")
            pe.wait_ge(sem("ca_low"), 1)
            for s in range(len(units) + 2):
                if s < len(units):
                    b, t, h = units[s]
                    wait(pe, "at_exp", s - 1)
                    nc.tensor.matmul(PS[:, s % 2, 0:(t + 1) * P], QT[0:64, h, t * P:(t + 1) * P],
                                     KT[0:64, 2 * b + h // 4, 0:(t + 1) * P], start=True, stop=False)
                    nc.tensor.matmul(PS[:, s % 2, t * P:(t + 1) * P], MASKr[:, 0, :], MASKr[:, 1, :],
                                     start=False, stop=True).then_inc(sem("at_scores"), 1)
                v, k = ada_at(s)
                if v < 6 and k < NK:
                    if k == 0:
                        wait(pe, "mod_taken", v)
                    c = (FIRST["ada"] + NK * v + k, 0, 0)
                    pe.wait_ge(sem("low_done"), number(c, 1))
                    for half in range(2):
                        hs = slice(half * 512, (half + 1) * 512)
                        last = mm3(PS[:, 6 + half, :], (CABr[:, 0, k, :], CABr[:, 1, k, :]),
                                   (WHr[:, slot(c), hs], WLr[:, slot(c), hs]), k == 0, k == NK - 1)
                    last.then_inc(sem("chunk_used"), 1)
                elif v < 6 and k == NK + 1 and v % 3 < 2:
                    pe.wait_ge(sem("mod_row"), v - v // 3 + 1)
                    for n in range(NK):
                        last = nc.tensor.matmul(PS[:, 6, n:n + 1], MODROW[:, n * P:(n + 1) * P], ident[:, 0:1],
                                                start=True, stop=True)
                    last.then_inc(sem("mod_turned"), 1)
                u = s - 1
                if 0 <= u < len(units):
                    b, t, h = units[u]
                    pe.wait_ge(sem("at_exp"), u + 1)
                    v = u - 2
                    if v >= 0:
                        pe.wait_ge(sem(f"at_stored{v % 2}"), v // 2 + 1)
                    for j in range(t + 1):
                        last = nc.tensor.transpose(PS[:, 2 + u % 2, j * P:(j + 1) * P], EX[:, u % 2, j * P:(j + 1) * P], ident)
                    last.then_inc(sem("at_turned"), 1)
                u = s - 2
                if u >= 0:
                    b, t, h = units[u]
                    n = u // 8
                    pe.wait_ge(sem(f"at_stored{u % 2}"), u // 2 + 1)
                    if h == 0:
                        wait(pe, "at_taken", n - 1)
                    o = (VSL, VWN)[b] + 64 * (h // 4)
                    for j in range(t + 1):
                        last = nc.tensor.matmul(PS[:, 4 + n % 2, h * DK:(h + 1) * DK], PT[:, u % 2, j * P:(j + 1) * P],
                                                PJ[:, j, o:o + DK], start=(j == 0), stop=(j == t))
                    last.then_inc(sem("at_pv"), 1)
            barrier(pe, "pe")
            turn_pe(pe, "mix", Y)
            barrier(pe, "pe")
            for k in range(NK):
                mm_n1(pe, (FIRST["wout"] + k, 0, 0), (HHr[:, k, :], HLr[:, k, :]), k == 0, k == NK - 1)
            add_normed(pe, "pe", "mixpost")
            norm_turn(pe, "pe", "pre2")
            cu = FIRST["up"]
            with pe.Fori(0, NF // 2) as i:
                for j in range(4):
                    pe.wait_ge(sem("up_free"), i * 4 + (j + 1))
                    mm_t(pe, (cu + j, i, 4), PS[:, j, :])
            barrier(pe, "pe")
            for k in range(NF):
                pe.wait_ge(sem("gt_low"), k + 1)
                mm_n1(pe, (FIRST["down"] + k, 0, 0), (GSHr[:, k % 4, :], GSLr[:, k % 4, :]),
                      k == 0, k == NF - 1)
            add_normed(pe, "pe", "ffpost")
            norm_turn(pe, "pe", "pre3")
            c0 = FIRST["win2"]
            for m in range(24):
                wait(pe, "p2_stored", m - 3)
                mm_t(pe, (c0 + m, 0, 0), PS[:, m % 4, :])
            for q in range(4):
                mm_n2(pe, (c0 + 24 + q, 0, 0), q, 4)
            barrier(pe, "pe")
            pe.wait_ge(sem("cv_sq"), 1)
            for n in range(4):
                last = nc.tensor.matmul(PS[:, n, :], con("ones"), CC[:, n, :], start=True, stop=True)
            last.then_inc(sem("cv_sums"), 1)
            barrier(pe, "pe")
            for n in range(8):
                kl, ql = (SC9, SC8) if n < 7 else (HK, HQ)
                if n < 7:
                    pe.wait_ge(sem("lv_ready"), n + 1)
                for h in range(4):
                    wait(pe, "lv_taken", 4 * (n - 2) + h + 1)
                    for c in range(4):
                        cs = slice(c * P, (c + 1) * P)
                        last = nc.tensor.matmul(PS[:, 4 * (n % 2) + h, cs], kl[:, h, cs], ql[:, h, cs], start=True, stop=True)
                    last.then_inc(sem("lv_scores"), 1)
            barrier(pe, "pe")
            pe.wait_ge(sem("kd_ready"), 1)
            for h in range(4):
                for c in range(3):
                    cs = slice(c * P, (c + 1) * P)
                    last = nc.tensor.transpose(PS[:, 4 + h, cs], SC9[:, h, cs], ident)
            last.then_inc(sem("kd_turned"), 1)
            pe.wait_ge(sem("kd_stored"), 1)
            for c in range(3):
                for h in range(4):
                    last = nc.tensor.matmul(PS[:, 4 + c, h * P:(h + 1) * P], SC8[:, h, c * P:(c + 1) * P],
                                            HV[:, c, h * P:(h + 1) * P], start=True, stop=True)
                last.then_inc(sem("kv_ready"), 1)
            pe.wait_ge(sem("qx_ready"), 1)
            for c in range(4):
                wait(pe, "state_ready", c)
                cs = slice(c * P, (c + 1) * P)
                for h in range(4):
                    last = nc.tensor.matmul(PS[:, h, cs], HV[:, c, h * P:(h + 1) * P], HF[:, h, cs], start=True, stop=(c == 0))
                    if c:
                        last = nc.tensor.matmul(PS[:, h, cs], STATE[:, c - 1, h, :], CC[:, h, cs], start=False, stop=True)
            last.then_inc(sem("o_done"), 1)
            pe.wait_ge(sem("o_sq"), 1)
            for h in range(4):
                last = nc.tensor.matmul(PS[:, 4 + h, :], con("ones"), SC9[:, h, :], start=True, stop=True)
            last.then_inc(sem("o_sums"), 1)
            barrier(pe, "pe")
            for k in range(NK):
                mm_n1(pe, (FIRST["wout2"] + k, 0, 0), (HHr[:, k, :], HLr[:, k, :]), k == 0, k == NK - 1)
            barrier(pe, "pe")
            norm_turn(pe, "pe", "pre4")
            pe.wait_ge(sem("subkeys_landed"), 16)
            c0 = FIRST["query"]
            for m in range(17):
                if m < 16:
                    wait(pe, "query_stored", m - 3)
                    mm_t(pe, (c0 + m, 0, 0), PS[:, m % 4, :])
                if m >= 1:
                    n = m - 1
                    pe.wait_ge(sem("query_stored"), n + 1)
                    wait(pe, "scores_stored", n - 3)
                    for t in range(NT):
                        last = nc.tensor.matmul(PS[:, 4 + n % 4, t * P:(t + 1) * P], QE[:, n % 2, t * P:(t + 1) * P],
                                                SUBK[:, n, :], start=True, stop=True)
                    last.then_inc(sem("keys_scored"), 1)
            barrier(pe, "pe")
            pe.sem_inc(sem("gm_ready"), 4)
            for s_ in range(1, NT + 2):
                t = s_ - 2
                if t >= 0:
                    with pe.Fori(0, 8) as i:
                        for q in range(4):
                            pe.wait_ge(sem("gm_stored"), i * 4 + (32 * t + q + 1))
                            if q % 2 == 0:
                                pe.wait_ge(sem("rows_ready"), i * 2 + (16 * t + q // 2 + 1))
                            for j in range(4 * q, 4 * q + 4):
                                pe.wait_ge(sem("onehot_ready"), i * 16 + (P * t + j + 1))
                                last = nc.tensor.matmul(PS[:, q, (j % 4) * P:(j % 4 + 1) * P], OHA[:, j, :], OHB[:, j, :],
                                                        start=True, stop=True)
                            last.then_inc(sem("gm_ready"), 1)
                if s_ <= NT:
                    t = s_ - 1
                    pe.wait_ge(sem("list_ready"), t + 1)
                    wait(pe, "list_stored", t)
                    for n, src in enumerate((N12[:, t % 2, 0], N12[:, t % 2, 1], BV[:, t % 2].rearrange("p h k -> p (h k)"))):
                        last = nc.tensor.transpose(PS[:, 4, n * P:(n + 1) * P], src, ident)
                    last.then_inc(sem("list_turned"), 1)
            barrier(pe, "pe")

            def step(c, g8, b, u, v):
                n = 0
                for half in range(2):
                    if u:
                        for m in range(4 * half, 4 * half + 4):
                            pe.wait_ge(sem("gelu_done"), g8 + (m + 1))
                            mm_t(pe, plus(c, n), PS[:, 4 + m % 4, :])
                            n += 1
                    if v:
                        pe.wait_ge(sem("acc_done"), (g8 // 4 + (half - 1)) if isinstance(g8, int)
                                   else (acc_of(c) + half))
                        for q in range(4):
                            cc = plus(c, n)
                            pe.wait_ge(sem("low_done"), number(cc, 1))
                            pe.wait_ge(sem("w_low"), g8 + (2 * q + 2 - GROUP))
                            for r in range(2):
                                i2 = 2 * q + r
                                for t in range(NT):
                                    ts = slice(t * P, (t + 1) * P)
                                    rs = slice(r * 512, (r + 1) * 512)
                                    last = mm3(PS[:, t, :], (WGTr[:, 1 - b, 0, i2, ts], WGTr[:, 1 - b, 1, i2, ts]),
                                               (WHr[:, slot(cc), rs], WLr[:, slot(cc), rs]), i2 == 0, i2 == GROUP - 1)
                            last.then_inc(sem("chunk_used"), 1)
                            n += 1

            def acc_of(c):
                s_ = (c[0] - FIRST["experts"] - GROUP) // (2 * GROUP)
                return c[1] * 4 + (2 * s_ + 1)
            experts(pe, step)
            barrier(pe, "pe")


def kernel(**inputs):
    import concourse.bacc as bacc
    from concourse.bass_utils import run_bass_kernel_spmd

    nc = bacc.Bacc("TRN2", target_bir_lowering=False, num_devices=1)
    v = {k: np.asarray(a) for k, a in inputs.items()}

    def tiles(a, n):
        return a.reshape(n, P).T

    def columns(w):
        return w.reshape(NK, P, -1, P).transpose(2, 1, 0, 3).reshape(-1, P, NK * P)

    small, decay, levels = constants()
    par = [tiles(v["norm_mix_pre"][0], 8), tiles(v["norm_ffn_pre"][0], 8), tiles(v["norm1_w_2"][0], 8),
           tiles(v["norm2_w_2"][0], 8), tiles(v["ret_gn_w"][0], 4), tiles(v["b_ada_2"][0], 48),
           tiles(v["c_2"][0], 8), tiles(v["hgrn_lb_logits_2"][0], 4), tiles(v["hgrn_lb_logits_2"][1], 4),
           tiles(v["hgrn_onorm_w_2"][0], 4), tiles(v["conv_onorm_w_2"][0], 4),
           v["conv_w_2"][0].reshape(3, 4, P).transpose(2, 1, 0).reshape(P, 12),
           v["ffn_conv"][0].reshape(3, 2, NF, P).transpose(3, 2, 1, 0).reshape(P, 132)]
    up = columns(v["ffn_w_up"][0])
    w2 = v["w_in_2"][0]
    w2c = columns(w2)
    arrays = {
        "x": v["x"][0],
        "const": np.concatenate([small[n] for n, _ in CONST_COLS], axis=1),
        "param": np.concatenate(par, axis=1),
        "decay": decay, "levels": levels,
        "nm_post": v["norm_mix_post"][0], "nf_post": v["norm_ffn_post"][0], "final_w": v["final_norm_w_2"],
        "w_in": v["w_in"][0],
        "cmp_w1": np.stack([v["cmp_k_w1"][0], v["cmp_v_w1"][0]]).reshape(2, 4, 4, P, 256).transpose(0, 1, 3, 2, 4)
                    .reshape(8, P, 1024),
        "cmp_w2": np.stack([v["cmp_k_w2"][0], v["cmp_v_w2"][0]]),
        "cmp_pos": np.stack([v["cmp_k_pos"][0], v["cmp_v_pos"][0]]).reshape(2, 16, 2, DK).transpose(2, 3, 0, 1)
                     .reshape(P, 2, 16),
        "w_out": v["w_out"][0],
        "ffn_up": np.stack([up[:NF], up[NF:]], axis=1).reshape(2 * NF, P, 1024),
        "ffn_down": v["ffn_w_down"][0],
        "w_ada": v["w_ada_2"][0],
        "bada_gate": v["b_ada_2"][0].reshape(6, D)[[2, 5]],
        "win2": np.concatenate([w2c[0:8], w2c[12:28],
                                w2[:, 1024:1536].reshape(4, 2, P, 512).transpose(0, 2, 1, 3).reshape(4, P, 1024)]),
        "w_out2": v["w_out_2"][0],
        "query": columns(v["peer_w_query_2"][0]),
        "subk": v["peer_sub_keys_2"][0].reshape(16, PK, P).transpose(2, 0, 1),
        "peer_u": v["peer_u_2"][0].reshape(P, P, NK, P).transpose(1, 3, 2, 0).reshape(P, P, 1024),
        "peer_v": v["peer_v_2"][0],
    }
    arrays = {k: np.ascontiguousarray(a) for k, a in arrays.items()}
    d = {}
    for name, a in arrays.items():
        d[name] = nc.dram_tensor("in_" + name, a.shape, mybir.dt.from_np(a.dtype), kind="ExternalInput").ap()
    d["gate_matrices"] = nc.dram_tensor("gate_matrices", (S // 64, P, P, 64), F32, kind="Internal").ap()
    d["x3"] = nc.dram_tensor("x3", (P, NT, D), F32, kind="Internal").ap()
    d["out"] = nc.dram_tensor("out_0", (S, D), F32, kind="ExternalOutput").ap()
    build(nc, d)
    r = run_bass_kernel_spmd(nc, [{"in_" + k: a for k, a in arrays.items()}], core_ids=[0])
    return r.results[0]["out_0"].reshape(1, S, D)
```

```python
from contextlib import ExitStack

import numpy as np
import concourse.bass as bass
from concourse import mybir

F32 = mybir.dt.float32
F32R = mybir.dt.float32r
U32 = mybir.dt.uint32
I32 = mybir.dt.int32
ACT = mybir.ActivationFunctionType
ALU = mybir.AluOpType
AX = mybir.AxisListType.X

P = 128
D = 1024
S = 512
NT = S // P
NK = D // P
EPS = 1e-6
GN_EPS = 1e-5
NEG = -1e30
RQ, RK, RV, RG, NQ = 0, 256, 512, 1024, 1536
KCM, VCM, KSL, VSL, KWN, VWN, NG = 2048, 2176, 2304, 2432, 2560, 2688, 2816
IN_COLS = 2840
TAIL = IN_COLS - 5 * 512
RH, NH, GR = 4, 8, 2
DK = 64
DFF = 2816
NF = DFF // P
CW = 1024
RING = 4
LEAD = 3
GROUP = 8
NGRP = P // GROUP
PH, PK, TOPK = 8, 128, 16

PHASES = [("win", 24), ("cmp", 8), ("ada", 6 * NK), ("wout", 8), ("up", 2 * NF), ("down", NF),
          ("win2", 28), ("wout2", 8), ("query", 16), ("experts", 2 * P)]
FIRST = {}
_n = 0
for _name, _count in PHASES:
    FIRST[_name] = _n
    _n += _count
CHUNKS = _n


def constants():
    f = np.float32
    inv = 1.0 / (10000.0 ** (np.arange(0, DK, 2, dtype=np.float64) / DK))

    def angles(pos):
        a = (pos.astype(f)[:, None] * inv.astype(f)[None, :]).astype(np.float64)
        c, s = np.cos(a), np.sin(a)
        return np.concatenate([c, c], 1).astype(f), np.concatenate([-s, s], 1).astype(f)

    cols = {}
    cols["ident"] = np.eye(P, dtype=f)
    cols["mean"] = np.full((P, P), 1.0 / P, f)
    cols["eps"] = np.full((P, 1), EPS, f)
    c, s = angles(np.arange(S))
    cols["cos"] = c.reshape(NT, P, DK).transpose(1, 0, 2).reshape(P, -1)
    cols["sin"] = s.reshape(NT, P, DK).transpose(1, 0, 2).reshape(P, -1)
    end = np.tile(np.arange(32) * 16 + 31, 4)
    c, s = angles(end)
    cols["ccos"], cols["csin"] = c, s
    i = np.arange(P)
    cols["causal"] = np.where(i[None, :] > i[:, None], NEG, 0.0).astype(f)
    t = np.arange(S).reshape(NT, P)
    ok = (end[None, None, :32] <= t[:, :, None]) & (np.arange(32) < 31)
    ok = ok.transpose(1, 0, 2).reshape(P, -1)
    cols["cmp_ok"] = ok.astype(f)
    cols["cmp_no"] = np.where(ok, 0.0, NEG).astype(f)
    cols["iota"] = np.tile(i.astype(f), (P, 1))
    cols["four"] = (i[:, None] // 32 == np.arange(4)[None, :]).astype(f)
    small = cols
    gamma = 1.0 - 2.0 ** (-5.0 - np.arange(RH))
    x = np.arange(S)[None, None, :] - i[:, None, None]
    decay = np.where(x >= 0, np.exp(np.log(gamma)[None, :, None] * np.maximum(x, 0)), 0.0) * DK ** -0.5
    lev = np.zeros((P, 8, P), np.uint32)
    for n, m in enumerate((64, 32, 16, 8, 4, 2, 1)):
        lev[:, n] = ((i[:, None] // (2 * m) == i[None, :] // (2 * m)) & (i[:, None] % (2 * m) < m)
                     & (i[None, :] % (2 * m) >= m))
    lev[:, 7] = np.eye(P)
    return small, decay.astype(f).reshape(P, -1), lev.reshape(P, -1)


CONST_COLS = [("ident", P), ("mean", P), ("eps", 1), ("cos", NT * DK), ("sin", NT * DK), ("ccos", DK), ("csin", DK),
              ("causal", P), ("cmp_ok", NT * 32), ("cmp_no", NT * 32), ("iota", P), ("four", 4)]
PARAM_COLS = [("nmp", 8), ("nfp", 8), ("n1", 8), ("n2", 8), ("gn", 4), ("bada", 48), ("c", 8), ("lb0", 4),
              ("lb1", 4), ("onorm", 4), ("conorm", 4), ("conv", 12), ("ffconv", 132)]


def offsets(cols):
    at, n = {}, 0
    for name, w in cols:
        at[name] = (n, w)
        n += w
    return at, n


def build(nc, d):
    const_at, n_const = offsets(CONST_COLS)
    param_at, n_param = offsets(PARAM_COLS)
    with ExitStack() as ctx:
        place = {}

        def sb(name, cols, dt=F32):
            place[name] = nc.sbuf_base
            return ctx.enter_context(nc.sbuf_tensor(name, [P, cols], dt))

        def over(parent, name, first, cols, dt):
            return nc.alloc_sbuf_tensor_at(name, [P, cols], dt, offset=(place[parent] + 31) // 32 * 32 + 4 * first)[:, :]

        sems = {}

        def sem(name):
            if name not in sems:
                sems[name] = ctx.enter_context(nc.semaphore(name))
            return sems[name]

        CON, PAR = sb("CON", n_const), sb("PAR", n_param)
        X = sb("X", NT * D)[:, :].rearrange("p (t n) -> p t n", t=NT)
        HHr = sb("HH", NK * S, F32R)[:, :].rearrange("p (k t) -> p k t", k=NK)
        HLr = sb("HL", NK * S, F32R)[:, :].rearrange("p (k t) -> p k t", k=NK)
        HH, HL = HHr.bitcast(F32), HLr.bitcast(F32)
        RAW = sb("RAW", RING * CW)[:, :].rearrange("p (r n) -> p r n", r=RING)
        WHr = sb("WH", RING * CW, F32R)[:, :].rearrange("p (r n) -> p r n", r=RING)
        WLr = sb("WL", RING * CW, F32R)[:, :].rearrange("p (r n) -> p r n", r=RING)
        WH = WHr.bitcast(F32)
        ROW = sb("ROW", D)
        GATE = sb("GATE", 2 * D)[:, :].rearrange("p (g n) -> p g n", g=2)
        MISC = sb("MISC", 1024)
        A = sb("A", 22528)
        PS = ctx.enter_context(nc.psum_tensor("PS", [P, 8, 512], F32))

        def con(name):
            o, w = const_at[name]
            return CON[:, o:o + w]

        def par(name, a=0, b=None):
            o, w = param_at[name]
            return PAR[:, o + a:o + (w if b is None else b)]

        used_misc = [0]

        def misc(n):
            used_misc[0] += n
            assert used_misc[0] <= 1024
            return MISC[:, used_misc[0] - n:used_misc[0]]

        ident = con("ident")
        sumsq, rstd = misc(4), misc(4)

        def wait(eng, s, v):
            if not (isinstance(v, int) and v <= 0):
                eng.wait_ge(sem(s), v)

        PHASE_ENDS = ["projection", "compression", "compressed attention", "attention", "turn",
                      "up", "states", "queries", "gates", "experts"]

        def barrier(eng, name):
            eng.drain().then_inc(sem("phase_ended"), 1)
            after(eng, name)

        def after(eng, name):
            eng.wait_ge(sem("phase_ended"), 3 * (PHASE_ENDS.index(name) + 1))

        def link_for(eng, name):
            count = [0]

            def link(ins):
                count[0] += 1
                ins.then_inc(sem(name), 1)
                eng.wait_ge(sem(name), count[0])

            def mark(ins):
                count[0] += 1
                ins.then_inc(sem(name), 1)
                return count[0]

            def until(n):
                eng.wait_ge(sem(name), n)
            link.mark, link.until = mark, until
            return link

        def slot(c):
            return c[0] % RING

        def plus(c, n):
            return (c[0] + n, c[1], c[2])

        def number(c, n=0):
            return c[0] + n + c[2] * c[1] if not isinstance(c[1], int) else c[0] + n

        def landed(c):
            if isinstance(c[1], int):
                return 16 * (c[0] // RING + 1)
            return 16 * (c[0] // RING + 1) + c[1] * (16 * c[2] // RING)

        def split_high(act, c, w=CW):
            if c[0] >= CHUNKS:
                return
            act.wait_ge(sem(f"raw_landed{slot(c)}"), landed(c))
            wait(act, "chunk_used", number(c, 1 - RING))
            nc.scalar.activation(WHr[:, slot(c), 0:w], RAW[:, slot(c), 0:w], ACT.Copy).then_inc(sem("high_done"), 1)

        def split_low(dve, c, w=CW):
            if c[0] >= CHUNKS:
                return
            dve.wait_ge(sem("high_done"), number(c, 1))
            nc.vector.tensor_tensor(WLr[:, slot(c), 0:w], RAW[:, slot(c), 0:w], WH[:, slot(c), 0:w],
                                    ALU.subtract).then_inc(sem("low_done"), 1)

        def mm3(out, L, R, first, last):
            nc.tensor.matmul(out, L[0], R[0], start=first, stop=False)
            nc.tensor.matmul(out, L[0], R[1], start=False, stop=False)
            return nc.tensor.matmul(out, L[1], R[0], start=False, stop=last)

        def tile_ready(pe, tag, k):
            if tag is not None:
                pe.wait_ge(sem("tile_low"), NK * TURNS.index(tag) + k + 1)

        def mm_t(pe, c, out, tag=None):
            pe.wait_ge(sem("low_done"), number(c, 1))
            wh = WHr[:, slot(c), :].rearrange("p (k n) -> p k n", k=NK)
            wl = WLr[:, slot(c), :].rearrange("p (k n) -> p k n", k=NK)
            for k in range(NK):
                tile_ready(pe, tag, k)
                last = mm3(out, (wh[:, k, :], wl[:, k, :]), (HHr[:, k, :], HLr[:, k, :]), k == 0, k == NK - 1)
            last.then_inc(sem("chunk_used"), 1)

        def mm_n2(pe, c, q, bank, w=512, tag=None):
            pe.wait_ge(sem("low_done"), number(c, 1))
            wh = WHr[:, slot(c), 0:2 * w].rearrange("p (k n) -> p k n", k=2)
            wl = WLr[:, slot(c), 0:2 * w].rearrange("p (k n) -> p k n", k=2)
            for kk in range(2):
                k = 2 * q + kk
                tile_ready(pe, tag, max(k, NT - 1))
                for t in range(NT):
                    ts = slice(t * P, (t + 1) * P)
                    last = mm3(PS[:, bank + t, 0:w], (HHr[:, k, ts], HLr[:, k, ts]), (wh[:, kk, :], wl[:, kk, :]),
                               k == 0, k == NK - 1)
            last.then_inc(sem("chunk_used"), 1)

        def mm_n1(pe, c, L, first, final):
            pe.wait_ge(sem("low_done"), number(c, 1))
            for t in range(NT):
                ts = slice(t * P, (t + 1) * P)
                for h in range(2):
                    hs = slice(h * 512, (h + 1) * 512)
                    last = mm3(PS[:, 2 * t + h, :], (L[0][:, ts], L[1][:, ts]),
                               (WHr[:, slot(c), hs], WLr[:, slot(c), hs]), first, final)
            last.then_inc(sem("chunk_used"), 1)

        XN = A[:, 0:4096].rearrange("p (t n) -> p t n", t=NT)
        JUNK = A[:, 4096:5120]
        TMP = A[:, 5120:6144].rearrange("p (r n) -> p r n", r=2)
        NORMS = ["pre1", "mixpost", "pre2", "ffpost", "pre3", "pre4", "final"]
        TURNS = ["pre1", "mix", "pre2", "pre3", "pre4"]
        ADDED = ["pre2", "pre3", "pre4", "final"]
        ROWED = ["pre1", "pre2", "pre3", "pre4"]

        def rms_act(act, link, src, tag, n=NT):
            for t in range(n):
                if tag in ADDED:
                    act.wait_ge(sem("rows_added"), NT * ADDED.index(tag) + t + 1)
                ins = nc.scalar.activation(JUNK if len(src(t).shape) == 2 else JUNK.rearrange("p (a b) -> p a b", a=2),
                                           src(t), ACT.Square, accum_out=sumsq[:, t:t + 1])
                if t < n - 1:
                    link(ins)
            ins.then_inc(sem("rms_squares"), 1)
            act.wait_ge(sem("rms_mean"), NORMS.index(tag) + 1)
            nc.scalar.activation(rstd, rstd, ACT.Sqrt).then_inc(sem("rms_root"), 1)

        def rms_dve(dve, link, tag):
            dve.wait_ge(sem("rms_squares"), NORMS.index(tag) + 1)
            nc.vector.tensor_scalar(rstd, sumsq, 1.0 / D, EPS, ALU.mult, ALU.add).then_inc(sem("rms_mean"), 1)
            dve.wait_ge(sem("rms_root"), NORMS.index(tag) + 1)
            link(nc.vector.reciprocal(rstd, rstd))

        def turn_pe(pe, tag, src):
            for k in range(NK):
                for t in range(NT):
                    if k == 0 and src is XN:
                        pe.wait_ge(sem("rows_normed"), NT * ROWED.index(tag) + t + 1)
                    last = nc.tensor.transpose(PS[:, k, t * P:(t + 1) * P], src[:, t, k * P:(k + 1) * P], ident)
                last.then_inc(sem("tile_turned"), 1)

        def turn_dve(dve, link, tag, scale, bias=None, ready=None):
            for k in range(NK):
                n = NK * TURNS.index(tag) + k
                dve.wait_ge(sem("tile_turned"), n + 1)
                wait(dve, "tile_high", n - 1)
                sc = scale(k)
                if sc is None:
                    ins = nc.vector.tensor_copy(TMP[:, k % 2, :], PS[:, k, :])
                elif bias is None:
                    ins = nc.vector.tensor_scalar(TMP[:, k % 2, :], PS[:, k, :], sc, None, ALU.mult)
                else:
                    ins = nc.vector.tensor_scalar(TMP[:, k % 2, :], PS[:, k, :], sc, bias(k), ALU.mult, ALU.add)
                ins.then_inc(sem("tile_scaled"), 1)
                dve.wait_ge(sem("tile_high"), n + 1)
                nc.vector.tensor_tensor(HLr[:, k, :], TMP[:, k % 2, :], HH[:, k, :], ALU.subtract)\
                    .then_inc(sem("tile_low"), 1)

        def turn_act(act, tag):
            for k in range(NK):
                act.wait_ge(sem("tile_scaled"), NK * TURNS.index(tag) + k + 1)
                nc.scalar.activation(HHr[:, k, :], TMP[:, k % 2, :], ACT.Copy).then_inc(sem("tile_high"), 1)

        def norm_turn(eng, who, tag, link=None, scale=None, bias=None):
            if who == "act":
                rms_act(eng, link, lambda t: X[:, t, :], tag)
                turn_act(eng, tag)
            elif who == "dve":
                rms_dve(eng, link, tag)
                for t in range(NT):
                    nc.vector.tensor_scalar(XN[:, t, :], X[:, t, :], rstd[:, t:t + 1], None,
                                            ALU.mult).then_inc(sem("rows_normed"), 1)
                turn_dve(eng, link, tag, scale, bias)
            else:
                turn_pe(eng, tag, XN)

        def banks(t):
            return PS[:, 2 * t:2 * t + 2, :]

        def add_rows(eng, weigh):
            first = row_count[0]
            row_count[0] += NT
            for t in range(NT + 1):
                if t < NT:
                    weigh(t, XN[:, t, :].rearrange("p (a b) -> p a b", a=2)).then_inc(sem("rows_weighted"), 1)
                if t >= 1:
                    eng.wait_ge(sem("rows_weighted"), first + t)
                    nc.vector.tensor_tensor(X[:, t - 1, :], X[:, t - 1, :], XN[:, t - 1, :], ALU.add)\
                        .then_inc(sem("rows_added"), 1)
            eng.wait_ge(sem("rows_added"), first + NT)

        row_count = [0]

        def add_normed(eng, who, tag, link=None):
            name, n = {"mixpost": ("wout", NK), "ffpost": ("down", NF)}[tag]
            if who != "pe":
                eng.wait_ge(sem("chunk_used"), FIRST[name] + n)
            if who == "act":
                rms_act(eng, link, banks, tag)
            elif who == "dve":
                rms_dve(eng, link, tag)
                eng.wait_ge(sem("row_landed"), 16 * {"mixpost": 1, "ffpost": 2}[tag])
                row = ROW[:, :].rearrange("p (a b) -> p a b", a=2)
                add_rows(eng, lambda t, out: nc.vector.scalar_tensor_tensor(out, banks(t), rstd[:, t:t + 1], row,
                                                                            ALU.mult, ALU.mult))

        PJ = A[:, 0:NT * IN_COLS].rearrange("p (t n) -> p t n", t=NT)
        o1 = NT * IN_COLS
        Y = A[:, o1:o1 + 4096].rearrange("p (t n) -> p t n", t=NT)
        o2 = o1 + 4096
        R1 = over("HH", "HH_scratch", 0, 4096, F32)
        R2 = over("HL", "HL_scratch", 0, 4096, F32)
        RT = R1.rearrange("p (k t) -> p k t", k=8)
        QT = R2.rearrange("p (k t) -> p k t", k=8)
        KT = A[:, o2:o2 + 2048].rearrange("p (k t) -> p k t", k=4)
        o3 = o2 + 2048
        W3 = A[:, o3:22528]
        assert 22528 - o3 >= 4608
        def head_bank(n):
            return n if n < 8 else 2 + n % 2

        ROPED = [(RQ + 64 * h) for h in range(8)] + [NQ + 64 * h for h in range(8)] + \
                [KSL, KSL + 64, KWN, KWN + 64]

        def rope(link, o, n):
            for t in range(NT):
                src = PJ[:, t, o:o + n * DK].rearrange("p (h x) -> p h x", x=DK)
                c = con("cos")[:, t * DK:(t + 1) * DK].unsqueeze(1).to_broadcast([P, n, DK])
                s = con("sin")[:, t * DK:(t + 1) * DK].unsqueeze(1)
                a = W3[:, 2048:2048 + n * DK].rearrange("p (h x) -> p h x", x=DK)
                b = W3[:, 2560:2560 + n * DK].rearrange("p (h x) -> p h x", x=DK)
                nc.vector.tensor_tensor(a, src, c, ALU.mult)
                nc.vector.tensor_tensor(b[:, :, 0:32], src[:, :, 32:64], s[:, :, 0:32].to_broadcast([P, n, 32]), ALU.mult)
                link(nc.vector.tensor_tensor(b[:, :, 32:64], src[:, :, 0:32],
                                             s[:, :, 32:64].to_broadcast([P, n, 32]), ALU.mult))
                last = nc.vector.tensor_tensor(src, a, b, ALU.add)
                if t < NT - 1:
                    link(last)
            last.then_inc(sem("roped"), 1)
            dve_roped[0] += 1
            nc.vector.wait_ge(sem("roped"), dve_roped[0])

        dve_roped = [0]
        ROPES = {0: (RQ, 8), 3: (NQ, 8), 4: (KSL, 2), 5: (KWN, 2)}

        DEC = W3[:, 0:2048].rearrange("p (h x) -> p h x", h=RH)
        SR = W3[:, 2048:2048 + 2 * 1280].rearrange("p (r x) -> p r x", r=2)
        sr_at = [0, 512, 896, 1152]
        bn6, mv = misc(16 * 6), misc(32)

        DUP = R1[:, 0:2048].rearrange("p (w t g j x) -> p w t g j x", w=2, t=NT, g=2, j=2)
        BLK = R1[:, 2048:4096].rearrange("p (w k m) -> p w k m", w=2, k=16)
        BLHr = over("A", "BLH", o3, 2048, F32R).rearrange("p (w k m) -> p w k m", w=2, k=16)
        BLLr = over("A", "BLL", o3 + 2048, 2048, F32R).rearrange("p (w k m) -> p w k m", w=2, k=16)
        BLH = BLHr.bitcast(F32)
        HT = DUP.rearrange("p w t g j x -> p (w t g j x)")[:, 0:512].rearrange("p (w n) -> p w n", w=2)
        HID = W3[:, 4096:4608].rearrange("p (f g r n) -> p f g r n", f=2, g=2, r=4)
        HIDK = misc(128).rearrange("p (f m) -> p f m", f=2)
        W2 = W3[:, 4608:4864].rearrange("p (w f n) -> p w f n", w=2, f=2)
        POS = W3[:, 4864:4896].rearrange("p (w k) -> p w k", w=2)
        KC = misc(192).rearrange("p (a n) -> p a n", a=3)
        KCT = misc(64)
        VBD = PJ[:, 0, RQ:RQ + 512].rearrange("p (g r n) -> p g r n", g=2, r=4)
        CT = [[PJ[:, 2 * w + g, RQ:RQ + 512] for g in range(2)] for w in range(2)]
        E4 = R1[:, 0:1024].rearrange("p (t h n) -> p t h n", t=NT, h=NH)
        PTC = R1[:, 1024:2048].rearrange("p (u t) -> p u t", u=8)
        mx4, z4 = misc(32), misc(32)
        gates = misc(NT * 24).rearrange("p (t g h) -> p t g h", t=NT, g=3)
        EX = W3[:, 0:1024].rearrange("p (r x) -> p r x", r=2)
        PT = W3[:, 1024:2048].rearrange("p (r x) -> p r x", r=2)
        OT = W3[:, 2048:3072].rearrange("p (r x) -> p r x", r=2)
        nmax, zsum = misc(64), misc(64)

        units = [(b, t, h) for b in range(2) for t in range(NT) for h in range(NH)]

        GT = A[:, 0:NF * S].rearrange("p (k t) -> p k t", k=NF)
        CV = A[:, NF * S:NF * S + 2048].rearrange("p (r t) -> p r t", r=4)
        GSHr = over("A", "GSH", NF * S + 2048, 2048, F32R).rearrange("p (r t) -> p r t", r=4)
        GSLr = over("A", "GSL", NF * S + 4096, 2048, F32R).rearrange("p (r t) -> p r t", r=4)
        GSH = GSHr.bitcast(F32)

        CA = misc(8)
        CABr = over("HH", "CAB", 2048, 2048, F32R).rearrange("p (s k n) -> p s k n", s=2, k=NK)
        CAB = CABr.bitcast(F32)
        MOD = misc(32)
        MASKr = over("A", "MASK", o3 + 4640, 2 * P, F32R).rearrange("p (s n) -> p s n", s=2)
        MODROW = W3[:, 3072:4096]
        ADA_EVERY = 10

        def ada_at(s):
            return (s // ADA_EVERY, s % ADA_EVERY) if s < 6 * ADA_EVERY else (6, 0)

        LEVELS = (64, 32, 16, 8, 4, 2, 1)
        def reg(n, k=4):
            return A[:, n * 2048:(n + 1) * 2048].rearrange("p (k t) -> p k t", k=k)

        def flat(r):
            return r.rearrange("p k t -> p (k t)")

        HQ, HF, HG, HV, CB, CC, CX = (reg(n) for n in range(7))
        HK, SC8, SC9 = reg(7), reg(8), reg(9)
        BB = reg(10)
        EE = HV
        LEVEL = ROW[:, :].bitcast(U32).rearrange("p (n t) -> p n t", n=8)
        STATE = flat(HK)[:, 0:3 * 4 * P].rearrange("p (c h n) -> p c h n", c=3, h=4)
        lb, oml, lbt = misc(4), misc(4), misc(12)
        eb = misc(16)

        SS = A[:, 0:8192].rearrange("p (t f n) -> p t f n", t=NT, f=16)
        SUBK = A[:, 8192:10240].rearrange("p (f n) -> p f n", f=16)
        QE = A[:, 10240:11264].rearrange("p (r t) -> p r t", r=2)
        XF = X.rearrange("p t n -> p (t n)")
        TV = XF[:, 0:1024].rearrange("p (t f k) -> p t f k", t=NT, f=16)
        TIU = XF[:, 1024:2048].rearrange("p (t f k) -> p t f k", t=NT, f=16)
        BV = XF[:, 2048:2304].rearrange("p (r h k) -> p r h k", r=2, h=PH)
        BI = XF[:, 2304:2432].rearrange("p (h k) -> p h k", h=PH)
        CAND, CAND2 = XF[:, 2432:2688], XF[:, 2688:2944]
        PAB = XF[:, 2944:3200].rearrange("p (s u) -> p s u", s=2)
        N12 = XF[:, 3200:3712].rearrange("p (r s u) -> p r s u", r=2, s=2)
        TFf = XF[:, 3712:3968]
        TF = TFf.rearrange("p (s h k) -> p s h k", s=2, h=PH)
        EQ = A[:, 20480:21504].rearrange("p (h k a) -> p h k a", h=PH // 2, k=TOPK)
        LST = A[:, 21504:22272].rearrange("p (r l t) -> p r l t", r=2, l=3)
        zg, zs8 = misc(8), misc(8)
        def apart(t, r):
            if t < 2:
                return OHB[:, 8 * (r % 2):8 * (r % 2) + 8, :]
            return XF[:, 1024 * (r % 2):1024 * (r % 2) + 1024].rearrange("p (r n) -> p r n", r=8)

        HALF = 64
        STG = A[:, 0:16384].rearrange("p (r i t) -> p r i t", r=2, i=P)
        OHA = A[:, 16384:18432].rearrange("p (r n) -> p r n", r=16)
        OHB = A[:, 18432:20480].rearrange("p (r n) -> p r n", r=16)
        WGTr = over("A", "WGT", 0, 16384, F32R).rearrange("p (b s i t) -> p b s i t", b=2, s=2, i=GROUP)
        WGT = WGTr.bitcast(F32)
        GR_ = A[:, 16384:18432].rearrange("p (r t) -> p r t", r=4)
        GE = A[:, 18432:19456].rearrange("p (r t) -> p r t", r=2)
        WF = A[:, 19456:20480].rearrange("p (r t) -> p r t", r=2)
        YA = X
        X3 = R1.rearrange("p (t n) -> p t n", t=NT)

        ffc = par("ffconv").rearrange("p (m w) -> p m w", w=3)
        def experts(eng, step):
            cx = FIRST["experts"]
            step((cx, 0, 0), 0, 0, True, False)
            with eng.Fori(0, (NGRP - 2) // 2) as i:
                for s in range(2):
                    step((cx + GROUP + 2 * GROUP * s, i, 4 * GROUP), i * (2 * GROUP) + GROUP * (1 + s), (1 + s) % 2,
                         True, True)
            step((cx + GROUP + 2 * GROUP * (NGRP - 2), 0, 0), GROUP * (NGRP - 1), 1, True, True)
            step((cx + GROUP + 2 * GROUP * (NGRP - 1), 0, 0), GROUP * NGRP, 0, False, True)

        block = ctx.enter_context(nc.Block())
        dr = d

        @block.sync
        def _(sp):
            def load(c, src, w=CW):
                v = number(c, 1 - RING)
                wait(sp, "low_done", v)
                dst = RAW[:, slot(c), 0:w]
                if len(src.shape) == 3:
                    dst = dst.rearrange("p (a b) -> p a b", a=src.shape[1])
                sp.dma_start(dst, src).then_inc(sem(f"raw_landed{slot(c)}"), 16)

            win = dr["w_in"].rearrange("(q k p) n -> q p k n", q=4, p=P)
            for b in range(6):
                w = 512 if b < 5 else TAIL
                for q in range(4):
                    load((4 * b + q, 0, 0), win[q, :, :, b * 512:b * 512 + w], 2 * w)
            c0 = FIRST["cmp"]
            for n in range(8):
                load((c0 + n, 0, 0), dr["cmp_w1"][n])

            def looped(name, n, src, per=4):
                c0 = FIRST[name]
                with sp.Fori(0, n // per) as i:
                    for j in range(per):
                        load((c0 + j, i, per), src(i * per + j))

            c0 = FIRST["ada"]
            ada = dr["w_ada"].rearrange("(k p) (v n) -> v k p n", p=P, v=6)
            with sp.Fori(0, 6) as i:
                for k in range(NK):
                    load((c0 + k, i, NK), ada[i, k])
            c0 = FIRST["wout"]
            for k in range(NK):
                load((c0 + k, 0, 0), dr["w_out"][k * P:(k + 1) * P, :])
            looped("up", 2 * NF, lambda m: dr["ffn_up"][m])
            c0 = FIRST["down"]
            for k in range(NF):
                load((c0 + k, 0, 0), dr["ffn_down"][k * P:(k + 1) * P, :])
            looped("win2", 28, lambda m: dr["win2"][m])
            looped("wout2", 8, lambda m: dr["w_out2"].rearrange("(k p) n -> k p n", p=P)[m])
            looped("query", 16, lambda m: dr["query"][m])
            vv = dr["peer_v"].rearrange("(a g q r) n -> g q a r n", a=P, g=NGRP, r=2)

            def step(c, g8, b, u, v):
                n = 0
                g = g8 // GROUP if isinstance(g8, int) else group_of(c)
                for half in range(2):
                    if u:
                        for m in range(4 * half, 4 * half + 4):
                            load(plus(c, n), dr["peer_u"][g8 + m])
                            n += 1
                    if v:
                        for q in range(4):
                            load(plus(c, n), vv[g - 1, q][:, :, half * 512:(half + 1) * 512])
                            n += 1

            def group_of(c):
                return c[1] * 2 + (c[0] - FIRST["experts"] + GROUP) // (2 * GROUP)
            experts(sp, step)

        @block.gpsimd
        def _(pool):
            xt = dr["x"].rearrange("(t p) n -> p t n", p=P)
            pool.dma_start(X, xt).then_inc(sem("x_landed"), 16)
            pool.dma_start(CON[:, :], dr["const"]).then_inc(sem("const_landed"), 16)
            pool.dma_start(PAR[:, :], dr["param"]).then_inc(sem("param_landed"), 16)
            pool.dma_start(ROW[:, :], dr["nm_post"].partition_broadcast(P)).then_inc(sem("row_landed"), 16)
            for g in range(2):
                pool.dma_start(GATE[:, g, :], dr["bada_gate"][g].partition_broadcast(P)).then_inc(sem("gb_landed"), 16)
            after(pool, "projection")
            pool.dma_start(DEC, dr["decay"].rearrange("p (h x) -> p h x", h=RH)).then_inc(sem("decay_landed"), 16)
            pool.dma_start(W2, dr["cmp_w2"].rearrange("w (f p) n -> p w f n", p=P)).then_inc(sem("w2_landed"), 16)
            pool.dma_start(POS, dr["cmp_pos"]).then_inc(sem("w2_landed"), 16)
            pool.wait_ge(sem("rt_scores"), 4 * RH)
            for w in range(2):
                o = (KCM, VCM)[w]
                for t in range(NT):
                    src = PJ[:, t, o:o + 128].rearrange("p (g x) -> p g x", g=2).unsqueeze(2).to_broadcast([P, 2, 2, 64])
                    last = nc.gpsimd.tensor_copy(DUP[:, w, t], src)
                last.then_inc(sem("cmp_dup"), 1)
            nc.gpsimd.memset(BLK, 0.0).then_inc(sem("blk_zero"), 1)
            pool.wait_ge(sem("blk_zero"), 1)
            pool.wait_ge(sem("w2_landed"), 32)
            for w in range(2):
                pool.wait_ge(sem("cmp_stored"), w + 1)
                for jj in range(2):
                    for g in range(2):
                        ps = slice(64 * jj, 64 * jj + 64)
                        for half in range(2):
                            src = CT[w][g][ps, :].rearrange("p (n k j) -> p k n j", k=8, j=2)[:, :, half:half + 31, jj]
                            last = nc.gpsimd.tensor_tensor(
                                BLK[ps, w, 8 * half:8 * half + 8, 32 * g:32 * g + 31], src,
                                POS[ps, w, 8 * half:8 * half + 8].unsqueeze(2).to_broadcast([64, 8, 31]), ALU.add)
                last.then_inc(sem("blk_ready"), 1)
            pool.wait_ge(sem("rows_weighted"), NT)
            pool.dma_start(ROW[:, :], dr["nf_post"].partition_broadcast(P)).then_inc(sem("row_landed"), 16)
            pool.wait_ge(sem("rows_weighted"), 2 * NT)
            pool.dma_start(ROW[:, :], dr["levels"].bitcast(F32)).then_inc(sem("levels_landed"), 16)
            pool.wait_ge(sem("rows_added"), 3 * NT)
            pool.dma_start(ROW[:, :], dr["final_w"].partition_broadcast(P)).then_inc(sem("row_landed"), 16)
            pool.dma_start(dr["x3"], X).then_inc(sem("x3_saved"), 16)
            pool.dma_start(SUBK, dr["subk"]).then_inc(sem("subkeys_landed"), 16)

            def places_apart(t, i):
                pool.wait_ge(sem("eq_summed"), i + (4 * t + 1))
                p3 = PAB.rearrange("p s u -> p (s u)")[:, bass.ds(i * 64, 64)].rearrange("p (h k) -> p h k", k=TOPK).unsqueeze(3)
                it = con("iota")[:, 0:TOPK].unsqueeze(1).unsqueeze(1)
                nc.gpsimd.tensor_tensor(EQ, p3.to_broadcast([P, PH // 2, TOPK, TOPK]),
                                        it.to_broadcast([P, PH // 2, TOPK, TOPK]), ALU.subtract).then_inc(sem("eq_ready"), 1)

            def rows_apart(t, i, rs):
                for r in rs:
                    if t < 2:
                        pool.wait_ge(sem("gm_ready"), i * 8 + (32 * t + 2 * r + 2))
                    else:
                        pool.wait_ge(sem("onehot_ready"), i * 4 + (16 * t + r - 1))
                    rows = apart(t, r)
                    nums = LST[:, t % 2, 1, bass.ds(i * 32 + 8 * r, 8)].unsqueeze(2).to_broadcast([P, 8, P])
                    nc.gpsimd.tensor_tensor(rows, con("iota").unsqueeze(1).to_broadcast([P, 8, P]), nums,
                                            ALU.subtract).then_inc(sem("rows_apart"), 1)

            for s_ in range(1, NT + 2):
                if s_ <= NT:
                    pool.wait_ge(sem("places_ready"), s_)
                if s_ >= 2:
                    pool.wait_ge(sem("list_stored"), s_ - 1)
                with pool.Fori(0, 4) as i:
                    if s_ >= 2:
                        rows_apart(s_ - 2, i, range(2))
                    if s_ <= NT:
                        places_apart(s_ - 1, i)
                    if s_ >= 2:
                        rows_apart(s_ - 2, i, range(2, 4))
            pool.wait_ge(sem("chunk_used"), FIRST["experts"] + GROUP + 2 * GROUP * (NGRP - 2) + 3 * GROUP // 2)
            pool.dma_start(X3, dr["x3"]).then_inc(sem("x3_back"), 16)
            pool.wait_ge(sem("x3_back"), 16)
            for t in range(NT):
                pool.wait_ge(sem("out_ready"), t + 1)
                pool.dma_start(dr["out"][t * P:(t + 1) * P, :], X[:, t, :]).then_inc(sem("out_landed"), 16)
            pool.wait_ge(sem("out_landed"), 16 * NT)
            for r in range(2):
                pool.wait_ge(sem(f"gates_written{r}"), 16 * NT)

        @block.scalar
        def _(act):
            link = link_for(act, "act_step")
            for n in range(LEAD):
                split_high(act, (n, 0, 0))
            act.wait_ge(sem("const_landed"), 16)
            act.wait_ge(sem("param_landed"), 16)
            act.wait_ge(sem("x_landed"), 16)
            norm_turn(act, "act", "pre1", link)
            for b in range(6):
                w = 512 if b < 5 else TAIL
                for q in range(4):
                    n = 4 * b + q + LEAD
                    split_high(act, (n, 0, 0), CW if n < 20 or n >= 24 else 2 * TAIL)
                act.wait_ge(sem("chunk_used"), 4 * b + 4)
                for t in range(NT):
                    last = nc.scalar.activation(PJ[:, t, b * 512:b * 512 + w], PS[:, 4 * (b % 2) + t, 0:w], ACT.Copy)
                last.then_inc(sem("proj_stored"), 1)
                if b == 3:
                    nc.scalar.activation(PJ[:, :, RG:RG + 512], PJ[:, :, RG:RG + 512], ACT.Silu)
            barrier(act, "projection")
            nc.scalar.activation(gates.rearrange("p t g h -> p t (g h)"), PJ[:, :, NG:NG + 24], ACT.Sigmoid)

            def store_heads(ns):
                for n in ns:
                    act.wait_ge(sem("head_turned"), n + 1)
                    dst = RT[0:64, n, :] if n < 8 else QT[0:64, n - 8, :] if n < 16 else KT[0:64, n - 16, :]
                    nc.scalar.activation(dst, PS[0:64, head_bank(n), :], ACT.Copy,
                                         scale=DK ** -0.5 if 8 <= n < 16 else 1.0).then_inc(sem("head_stored"), 1)
            store_heads(range(8))
            for w in range(2):
                act.wait_ge(sem("cmp_turned"), w + 1)
                for g in range(2):
                    last = nc.scalar.activation(CT[w][g], PS[:, 2 * w + g, :], ACT.Copy)
                last.then_inc(sem("cmp_stored"), 1)
            act.wait_ge(sem("gn_var"), 1)
            nc.scalar.activation(mv.rearrange("p (u s) -> p u s", s=2)[:, :, 1], mv.rearrange("p (u s) -> p u s", s=2)[:, :, 1],
                                 ACT.Sqrt).then_inc(sem("gn_root"), 1)
            store_heads(range(8, 20))
            for w in range(2):
                act.wait_ge(sem("blk_ready"), w + 1)
                nc.scalar.activation(BLHr[:, w], BLK[:, w], ACT.Copy).then_inc(sem("blk_high"), 1)
            for w in range(2):
                for q in range(4):
                    split_high(act, (FIRST["cmp"] + 4 * w + q + LEAD, 0, 0))
                act.wait_ge(sem("chunk_used"), FIRST["cmp"] + 4 * w + 4)
                nc.scalar.activation(HT[0:64, w, :], PS[0:64, w, 0:256], ACT.Gelu_apprx_tanh).then_inc(sem("hid_gelu"), 1)
            barrier(act, "compression")
            link(nc.scalar.activation(CA, par("c"), ACT.Silu))
            nc.scalar.activation(CABr[:, 0], CA.unsqueeze(2).to_broadcast([P, NK, P]), ACT.Copy)\
                .then_inc(sem("ca_high"), 1)
            nc.scalar.activation(MASKr[:, 0, :], ident, ACT.Copy)
            nc.scalar.activation(MASKr[:, 1, :], con("causal"), ACT.Copy)
            act.wait_ge(sem("cmp_shifted"), 1)
            nc.scalar.activation(E4, E4, ACT.Exp).then_inc(sem("cmp_exp"), 1)
            act.wait_ge(sem("cmp_pt"), 1)
            for n in range(2):
                last = nc.scalar.activation(PTC[:, 4 * n:4 * n + 4, :], PS[:, 4 + n, :].rearrange("p (a b) -> p a b", a=4), ACT.Copy)
            last.then_inc(sem("cmp_pt_stored"), 1)
            barrier(act, "compressed attention")
            for s in range(len(units) + 1):
                if s < len(units):
                    b, t, h = units[s]
                    w = (t + 1) * P
                    act.wait_ge(sem("at_max"), s + 1)
                    wait(act, "at_turned", s - 1)
                    nc.scalar.activation(EX[:, s % 2, 0:w], PS[:, s % 2, 0:w], ACT.Exp, bias=nmax[:, s:s + 1],
                                         accum_out=zsum[:, s:s + 1]).then_inc(sem("at_exp"), 1)
                u = s - 1
                if u >= 0 and u % 2 == 0:
                    w = (units[u][1] + 1) * P
                    act.wait_ge(sem("at_turned"), u + 1)
                    wait(act, "at_pv", u - 1)
                    nc.scalar.activation(PT[:, u % 2, 0:w], PS[:, 2 + u % 2, 0:w], ACT.Copy).then_inc(sem("at_stored0"), 1)
                v, k = ada_at(s)
                if v < 6 and k < NK:
                    split_high(act, (FIRST["ada"] + NK * v + k + LEAD, 0, 0))
                elif v in (0, 1, 3, 4) and k == NK:
                    act.wait_ge(sem("chunk_used"), FIRST["ada"] + NK * (v + 1))
                    wait(act, "mod_taken", v)
                    nc.scalar.activation(MODROW.rearrange("p (a b) -> p a b", a=2), PS[:, 6:8, :], ACT.Copy)\
                        .then_inc(sem("mod_row"), 1)
            barrier(act, "attention")
            turn_act(act, "mix")
            barrier(act, "turn")
            for k in range(NK):
                split_high(act, (FIRST["wout"] + k + LEAD, 0, 0))
            add_normed(act, "act", "mixpost", link)
            norm_turn(act, "act", "pre2", link)
            nc.scalar.preload_act_table(ACT.Gelu_apprx_tanh)
            cu = FIRST["up"]
            with act.Fori(0, NF // 2) as i:
                for j in range(4):
                    split_high(act, (cu + j + LEAD, i, 4))
                    act.wait_ge(sem("chunk_used"), i * 4 + (cu + j + 1))
                    act.wait_ge(sem("up_free"), i * 4 + (j + 1))
                    nc.scalar.activation(CV[:, j, :], PS[:, j, :], ACT.Copy,
                                         scale=ffc[:, i * 4 + j, 2:3]).then_inc(sem("up_tap"), 1)
                    if j % 2 == 1:
                        act.wait_ge(sem("up_conv"), i * 4 + j)
                        nc.scalar.activation(CV[:, j - 1, :], CV[:, j - 1, :], ACT.Gelu_apprx_tanh)\
                            .then_inc(sem("up_gelu"), 1)
            barrier(act, "up")
            for k in range(NF):
                if k == 0:
                    for m in range(3):
                        nc.scalar.activation(GSHr[:, m, :], GT[:, m, :], ACT.Copy).then_inc(sem("gt_high"), 1)
                c = FIRST["down"] + k
                split_high(act, (c + LEAD, 0, 0))
                if k + 3 < NF:
                    act.wait_ge(sem("chunk_used"), c)
                    nc.scalar.activation(GSHr[:, (k + 3) % 4, :], GT[:, k + 3, :], ACT.Copy)\
                        .then_inc(sem("gt_high"), 1)
            add_normed(act, "act", "ffpost", link)
            act.wait_ge(sem("lb_shifted"), 1)
            nc.scalar.activation(lbt[:, 4:12], lbt[:, 4:12], ACT.Exp).then_inc(sem("lb_exp"), 1)
            norm_turn(act, "act", "pre3", link)
            c0 = FIRST["win2"]
            for m in range(24):
                split_high(act, (c0 + m + LEAD, 0, 0))
                kind, n = m // 4, m % 4
                act.wait_ge(sem("chunk_used"), c0 + m + 1)
                src = PS[:, m % 4, :]
                if kind == 0:
                    nc.scalar.activation(HF[:, n, :], src, ACT.Sigmoid)
                    ins = nc.scalar.activation(HK[:, n, :], src, ACT.Sigmoid, scale=-1.0)
                elif kind == 5:
                    ins = nc.scalar.activation(HG[:, n, :], src, ACT.Silu)
                else:
                    ins = nc.scalar.activation((HQ, CB, CC, CX)[kind - 1][:, n, :], src, ACT.Copy)
                ins.then_inc(sem("p2_stored"), 1)
                if m == 5:
                    act.wait_ge(sem("f_ready"), 1)
                    nc.scalar.activation(HF, HF, ACT.Ln).then_inc(sem("logf"), 1)
                if m >= 8 and m % 2 == 0 and (m - 8) // 2 < len(LEVELS):
                    n = (m - 8) // 2
                    act.wait_ge(sem("lv_diff"), n + 1)
                    e = flat(EE).rearrange("p (b s m) -> p b s m", s=2, m=LEVELS[n])
                    nc.scalar.activation(e[:, :, 0, :], e[:, :, 0, :], ACT.Exp, scale=-1.0)
                    nc.scalar.activation(e[:, :, 1, :], e[:, :, 1, :], ACT.Exp).then_inc(sem("lv_exp"), 1)
            for m in range(24, 28):
                split_high(act, (c0 + m + LEAD, 0, 0))
            act.wait_ge(sem("chunk_used"), c0 + 28)
            act.wait_ge(sem("lv_ready"), len(LEVELS))
            for t in range(NT):
                last = nc.scalar.activation(HV[:, t, :], PS[:, t, :], ACT.Copy)
            last.then_inc(sem("v_stored"), 1)
            act.wait_ge(sem("cv_done"), 1)
            nc.scalar.activation(CC, CB, ACT.Square).then_inc(sem("cv_sq"), 1)
            nc.scalar.activation(CX, BB, ACT.Exp)
            nc.scalar.activation(eb, flat(BB)[:, 127::128], ACT.Exp)
            act.wait_ge(sem("dk_diff"), 1)
            nc.scalar.activation(SC9, SC9, ACT.Exp).then_inc(sem("dk_exp"), 1)
            act.wait_ge(sem("kd_turned"), 1)
            for h in range(4):
                last = nc.scalar.activation(SC8[:, h, 0:384], PS[:, 4 + h, 0:384], ACT.Copy)
            last.then_inc(sem("kd_stored"), 1)
            act.wait_ge(sem("cv_sums"), 1)
            link(nc.scalar.activation(CC, PS[:, 0:4, :], ACT.Ln, bias=con("eps")))
            nc.scalar.activation(CC, CC, ACT.Exp, scale=-0.5).then_inc(sem("cv_rstd"), 1)
            act.wait_ge(sem("o_done"), 1)
            nc.scalar.activation(SC9, PS[:, 0:4, :], ACT.Square).then_inc(sem("o_sq"), 1)
            for hh in range(2):
                rs = SC9[:, 2 * hh:2 * hh + 2, :]
                act.wait_ge(sem("o_sums"), 2 * hh + 2)
                link(nc.scalar.activation(rs, PS[:, 4 + 2 * hh:6 + 2 * hh, :], ACT.Ln, bias=con("eps")))
                nc.scalar.activation(rs, rs, ACT.Exp, scale=-0.5).then_inc(sem("o_rstd"), 1)
            act.wait_ge(sem("cv_normed"), 1)
            nc.scalar.activation(HHr[:, 4:8, :], CB, ACT.Copy).then_inc(sem("y2_high"), 1)
            for n in range(2):
                hs = slice(2 * n, 2 * n + 2)
                act.wait_ge(sem("y2_ready"), n + 1)
                nc.scalar.activation(HHr[:, hs, :], SC8[:, hs, :], ACT.Copy).then_inc(sem("y2_high"), 1)
            barrier(act, "states")
            for k in range(NK):
                split_high(act, (FIRST["wout2"] + k + LEAD, 0, 0))
            norm_turn(act, "act", "pre4", link)
            c0 = FIRST["query"]
            for m in range(17):
                if m < 16:
                    split_high(act, (c0 + m + LEAD, 0, 0))
                    act.wait_ge(sem("chunk_used"), c0 + m + 1)
                    wait(act, "keys_scored", m - 1)
                    nc.scalar.activation(QE[:, m % 2, :], PS[:, m % 4, :], ACT.Copy).then_inc(sem("query_stored"), 1)
                if m >= 1:
                    n = m - 1
                    act.wait_ge(sem("keys_scored"), n + 1)
                    nc.scalar.activation(SS[:, :, n, :], PS[:, 4 + n % 4, :].rearrange("p (t n) -> p t n", t=NT),
                                         ACT.Copy).then_inc(sem("scores_stored"), 1)
            barrier(act, "queries")
            act.sem_inc(sem("gm_stored"), 4)
            gm = dr["gate_matrices"]
            for s_ in range(NT + 2):
                for u in (2 * s_ - 4, 2 * s_ - 3):
                    if u < 0:
                        continue

                    def store(i, qs):
                        for q in qs:
                            act.wait_ge(sem("gm_ready"), i * 4 + (16 * u + q + 5))
                            dst = STG[:, u % 2].rearrange("p i t -> p t i")[:, bass.ds(i * 16 + 4 * q, 4), :]
                            nc.scalar.activation(dst, PS[:, q, :].rearrange("p (t n) -> p t n", t=4), ACT.Copy)\
                                .then_inc(sem("gm_stored"), 1)

                    wait(act, f"gates_written{u % 2}", 16 * (u // 2))
                    with act.Fori(0, 4) as i:
                        store(i, range(4))
                    act.wait_ge(sem("gm_stored"), 16 * (u + 1) + 4)
                    act.dma_start(gm[u], STG[:, u % 2]).then_inc(sem(f"gates_written{u % 2}"), 16)
                if 1 <= s_ <= NT:
                    act.wait_ge(sem("list_turned"), s_)
                    nc.scalar.activation(LST[:, (s_ - 1) % 2], PS[:, 4, 0:3 * P].rearrange("p (l t) -> p l t", l=3), ACT.Copy)\
                        .then_inc(sem("list_stored"), 1)
                if s_ < NT:
                    act.wait_ge(sem("best_shifted"), s_ + 1)
                    nc.scalar.activation(BV[:, s_ % 2], BV[:, s_ % 2], ACT.Exp).then_inc(sem("best_exp"), 1)
            barrier(act, "gates")
            cx = FIRST["experts"]
            nc.scalar.preload_act_table(ACT.Gelu)
            act.sem_inc(sem("gelu_done"), 4)

            def load_gates(e, m):
                act.dma_start(GR_[:, m % 4, :].rearrange("p (u t) -> p u t", t=HALF),
                              gm.rearrange("u p i t -> i p u t")[e]).then_inc(sem(f"gates_landed{m % 4}"), 16)

            def high(e, m, b):
                act.wait_ge(sem("w_done"), e + 3)
                nc.scalar.activation(WGTr[:, b, 0, m, :], WF[:, m % 2, :], ACT.Copy).then_inc(sem("w_high"), 1)
                if not (isinstance(e, int) and e + 4 >= P):
                    load_gates(e + 4, m)

            for r in range(2):
                act.wait_ge(sem(f"gates_written{r}"), 16 * NT)
            for m in range(4):
                load_gates(m, m)

            def step(c, g8, b, u, v):
                n = 0
                for half in range(2):
                    if u:
                        for m in range(4 * half, 4 * half + 4):
                            split_high(act, plus(c, n + LEAD))
                            act.wait_ge(sem("chunk_used"), number(c, n + 1))
                            act.wait_ge(sem("w_done"), g8 + (m + 1))
                            nc.scalar.activation(GE[:, m % 2, :], PS[:, 4 + m % 4, :], ACT.Gelu)\
                                .then_inc(sem("gelu_done"), 1)
                            high(g8 + m, m, b)
                            n += 1
                    if v:
                        for q in range(4):
                            split_high(act, plus(c, n + LEAD))
                            n += 1
            experts(act, step)
            barrier(act, "experts")
            rms_act(act, link, lambda t: X[:, t, :], "final")

        @block.vector
        def _(dve):
            link = link_for(dve, "dve_step")
            for n in range(LEAD):
                split_low(dve, (n, 0, 0))
            dve.wait_ge(sem("param_landed"), 16)
            dve.wait_ge(sem("x_landed"), 16)
            norm_turn(dve, "dve", "pre1", link, lambda k: par("nmp", k, k + 1))
            for b in range(6):
                for q in range(4):
                    n = 4 * b + q + LEAD
                    split_low(dve, (n, 0, 0), CW if n < 20 or n >= 24 else 2 * TAIL)
                if b - 1 in ROPES:
                    dve.wait_ge(sem("proj_stored"), b)
                    rope(link, *ROPES[b - 1])
            barrier(dve, "projection")
            rope(link, *ROPES[5])
            dve.wait_ge(sem("decay_landed"), 16)
            for u in range(4 * RH):
                h, j = u // 4, u % 4
                w = S - j * P
                dve.wait_ge(sem("rt_scores"), u + 1)
                if j == 0:
                    wait(dve, "rt_out", h - 1)
                nc.vector.tensor_tensor(SR[:, h % 2, sr_at[j]:sr_at[j] + w], PS[:, u % 4, 0:w], DEC[:, h, 0:w],
                                        ALU.mult).then_inc(sem("rt_decayed"), 1)
            dve.wait_ge(sem("rt_out"), RH)
            for t in range(NT):
                for h in range(RH):
                    u = t * 4 + h
                    last = nc.vector.bn_stats(bn6[:, 6 * u:6 * u + 6], PS[:, 4 + t, h * P:(h + 1) * P])
            link(last)
            for u in range(16):
                last = nc.vector.bn_aggr(mv[:, 2 * u:2 * u + 2], bn6[:, 6 * u:6 * u + 6])
            link(last)
            var = mv.rearrange("p (u s) -> p u s", s=2)[:, :, 1]
            nc.vector.tensor_scalar(var, var, GN_EPS, None, ALU.add).then_inc(sem("gn_var"), 1)
            dve.wait_ge(sem("gn_root"), 1)
            link(nc.vector.reciprocal(var, var))
            for t in range(NT):
                for h in range(RH):
                    u = t * 4 + h
                    link(nc.vector.tensor_scalar(Y[:, t, h * P:(h + 1) * P], PS[:, 4 + t, h * P:(h + 1) * P],
                                                 mv[:, 2 * u:2 * u + 1], mv[:, 2 * u + 1:2 * u + 2],
                                                 ALU.subtract, ALU.mult))
                link(nc.vector.tensor_tensor(Y[:, t, 0:512], Y[:, t, 0:512], PJ[:, t, RG:RG + 512], ALU.mult))
            for w in range(2):
                dve.wait_ge(sem("blk_high"), w + 1)
                nc.vector.tensor_tensor(BLLr[:, w], BLK[:, w], BLH[:, w], ALU.subtract).then_inc(sem("blk_low"), 1)
            for q in range(8):
                split_low(dve, (FIRST["cmp"] + q + LEAD, 0, 0))
            for w in range(2):
                dve.wait_ge(sem("hid_turned"), w + 1)
                for f in range(2):
                    if w == 0:
                        last = nc.vector.tensor_copy(HIDK[:, f, :], PS[:, 2, 64 * f:64 * f + 64])
                    for g in range(2):
                        if w == 1:
                            src = PS[:, 3, 64 * f + 32 * g:64 * f + 32 * g + 32]
                            last = nc.vector.tensor_copy(HID[:, f, g], src.unsqueeze(1).to_broadcast([P, 4, 32]))
                last.then_inc(sem("hid_stored"), 1)
                if w == 0:
                    dve.wait_ge(sem("kc_ready"), 1)
                    src = PS[0:64, 4, 0:64]
                    link(nc.vector.tensor_copy(KC[0:64, 0, :], src))
                    nc.vector.tensor_tensor(KC[0:64, 1, :], KC[0:64, 0, :], con("ccos")[0:64, :], ALU.mult)
                    nc.vector.tensor_tensor(KC[0:64, 2, 0:32], KC[0:64, 0, 32:64], con("csin")[0:64, 0:32], ALU.mult)
                    link(nc.vector.tensor_tensor(KC[0:64, 2, 32:64], KC[0:64, 0, 0:32], con("csin")[0:64, 32:64], ALU.mult))
                    nc.vector.tensor_tensor(KC[0:64, 0, :], KC[0:64, 1, :], KC[0:64, 2, :], ALU.add)\
                        .then_inc(sem("kc_roped"), 1)
                    dve.wait_ge(sem("kct_ready"), 1)
                    nc.vector.tensor_copy(KCT[0:64, :], PS[0:64, 5, 0:64]).then_inc(sem("kct_stored"), 1)
                else:
                    dve.wait_ge(sem("vc_ready"), 1)
                    for g in range(2):
                        last = nc.vector.tensor_tensor(
                            VBD[:, g], PS[:, 6 + g, 0:64].unsqueeze(1).to_broadcast([P, 4, 64]),
                            con("four").unsqueeze(2).to_broadcast([P, 4, 64]), ALU.mult)
                    link(last)
            barrier(dve, "compression")
            dve.wait_ge(sem("ca_high"), 1)
            nc.vector.tensor_tensor(CABr[:, 1], CA.unsqueeze(2).to_broadcast([P, NK, P]), CAB[:, 0], ALU.subtract)\
                .then_inc(sem("ca_low"), 1)
            dve.wait_ge(sem("cs_ready"), 1)
            sc = PS[:, 0:4, 0:256].rearrange("p t (h n) -> p t h n", h=NH)
            ok = con("cmp_ok").rearrange("p (t n) -> p t n", t=NT)
            no = con("cmp_no").rearrange("p (t n) -> p t n", t=NT)
            for t in range(NT):
                last = nc.vector.tensor_tensor(E4[:, t], sc[:, t], ok[:, t].unsqueeze(1).to_broadcast([P, NH, 32]), ALU.mult)
            link(last)
            for t in range(NT):
                last = nc.vector.tensor_tensor(E4[:, t], E4[:, t], no[:, t].unsqueeze(1).to_broadcast([P, NH, 32]), ALU.add)
            link(last)
            E4f = E4.rearrange("p t h n -> p (t h) n")
            link(nc.vector.tensor_reduce(mx4, E4f, AX, ALU.max))
            nc.vector.tensor_tensor(E4f, E4f, mx4.unsqueeze(2).to_broadcast([P, 32, 32]), ALU.subtract)\
                .then_inc(sem("cmp_shifted"), 1)
            dve.wait_ge(sem("cmp_exp"), 1)
            for t in range(NT):
                last = nc.vector.tensor_tensor(E4[:, t], E4[:, t], ok[:, t].unsqueeze(1).to_broadcast([P, NH, 32]), ALU.mult)
            link(last)
            link(nc.vector.tensor_reduce(z4, E4f, AX, ALU.add))
            link(nc.vector.tensor_scalar(z4, z4, 1e-30, None, ALU.max))
            link(nc.vector.reciprocal(z4, z4))
            nc.vector.tensor_tensor(E4f, E4f, z4.unsqueeze(2).to_broadcast([P, 32, 32]), ALU.mult)\
                .then_inc(sem("cmp_probs"), 1)
            dve.wait_ge(sem("cmp_out"), 1)
            for t in range(NT):
                last = nc.vector.tensor_tensor(
                    Y[:, t, 512:1024].rearrange("p (h n) -> p h n", h=NH), PS[:, t, :].rearrange("p (h n) -> p h n", h=NH),
                    gates[:, t, 0, :].unsqueeze(2).to_broadcast([P, NH, DK]), ALU.mult)
            link(last)
            barrier(dve, "compressed attention")
            for s in range(len(units) + 2):
                if s < len(units):
                    b, t, h = units[s]
                    w = (t + 1) * P
                    dve.wait_ge(sem("at_scores"), s + 1)
                    nc.vector.tensor_reduce(nmax[:, s:s + 1], PS[:, s % 2, 0:w], AX, ALU.max, negate=True)\
                        .then_inc(sem("at_max"), 1)
                u = s - 1
                if 0 <= u < len(units) and u % 2 == 1:
                    w = (units[u][1] + 1) * P
                    dve.wait_ge(sem("at_turned"), u + 1)
                    wait(dve, "at_pv", u - 1)
                    nc.vector.tensor_copy(PT[:, u % 2, 0:w], PS[:, 2 + u % 2, 0:w]).then_inc(sem("at_stored1"), 1)
                v, k = ada_at(s)
                if v < 6 and k < NK:
                    if v + k > 0:
                        split_low(dve, (FIRST["ada"] + NK * v + k + LEAD - 1, 0, 0))
                elif v < 6 and k == NK and v % 3 == 2:
                    dve.wait_ge(sem("chunk_used"), FIRST["ada"] + NK * (v + 1))
                    dve.wait_ge(sem("gb_landed"), 32)
                    g2 = GATE[:, v // 3, :].rearrange("p (a b) -> p a b", a=2)
                    nc.vector.tensor_tensor(g2, g2, PS[:, 6:8, :], ALU.add).then_inc(sem("mod_taken"), 1)
                elif v < 6 and k == NK + 1 and v % 3 < 2:
                    dve.wait_ge(sem("mod_turned"), v - v // 3 + 1)
                    md = MOD[:, 16 * (v // 3) + 8 * (v % 3):16 * (v // 3) + 8 * (v % 3) + 8]
                    last = nc.vector.tensor_tensor(md, PS[:, 6, 0:8], par("bada", 8 * v, 8 * v + 8), ALU.add)
                    if v % 3 == 1:
                        link(last)
                        last = nc.vector.scalar_tensor_tensor(md, md, 1.0, par(("n1", "n2")[v // 3]), ALU.add, ALU.mult)
                    last.then_inc(sem("mod_taken"), 1)
                u = s - 2
                if u >= 0 and u % 8 == 7:
                    b, t, _ = units[u]
                    n = u // 8
                    dve.wait_ge(sem("at_pv"), u + 1)
                    zs = zsum[:, 8 * n:8 * n + 8]
                    link(nc.vector.reciprocal(zs, zs))
                    link(nc.vector.tensor_tensor(zs, zs, gates[:, t, 1 + b, :], ALU.mult))
                    ot = OT[:, n % 2, :].rearrange("p (h n) -> p h n", h=NH)
                    nc.vector.tensor_tensor(ot, PS[:, 4 + n % 2, :].rearrange("p (h n) -> p h n", h=NH),
                                            zs.unsqueeze(2).to_broadcast([P, NH, DK]), ALU.mult)\
                        .then_inc(sem("at_taken"), 1)
                    dve.wait_ge(sem("at_taken"), n + 1)
                    link(nc.vector.tensor_tensor(Y[:, t, 512:1024], Y[:, t, 512:1024], OT[:, n % 2, :], ALU.add))
            split_low(dve, (FIRST["wout"] + LEAD - 1, 0, 0))
            barrier(dve, "attention")
            turn_dve(dve, link, "mix", lambda k: par("gn", k, k + 1) if k < 4 else None)
            barrier(dve, "turn")
            for k in range(NK):
                split_low(dve, (FIRST["wout"] + k + LEAD, 0, 0))
            add_normed(dve, "dve", "mixpost", link)
            norm_turn(dve, "dve", "pre2", link, lambda k: par("nfp", k, k + 1))
            cu = FIRST["up"]
            for j in range(4):
                nc.vector.memset(CV[:, j, 0:1], 0.0).then_inc(sem("up_free"), 1)
            with dve.Fori(0, NF // 2) as i:
                for j in range(4):
                    split_low(dve, (cu + j + LEAD, i, 4))
                    dve.wait_ge(sem("up_tap"), i * 4 + (j + 1))
                    nc.vector.scalar_tensor_tensor(CV[:, j, 1:], PS[:, j, 0:S - 1], ffc[:, i * 4 + j, 1:2], CV[:, j, 1:],
                                                   ALU.mult, ALU.add).then_inc(sem("up_mid"), 1)
                    dve.wait_ge(sem("up_mid"), i * 4 + (j + 1))
                    nc.vector.scalar_tensor_tensor(CV[:, j, 2:], PS[:, j, 0:S - 2], ffc[:, i * 4 + j, 0:1], CV[:, j, 2:],
                                                   ALU.mult, ALU.add).then_inc(sem("up_conv"), 1)
                    if j % 2 == 1:
                        dve.wait_ge(sem("up_conv"), i * 4 + (j + 1))
                        dve.wait_ge(sem("up_gelu"), i * 2 + (j // 2 + 1))
                        nc.vector.tensor_tensor(GT[:, i * 2 + j // 2, :], CV[:, j - 1, :], CV[:, j, :], ALU.mult)\
                            .then_inc(sem("up_free"), 2)
            barrier(dve, "up")
            for k in range(NF):
                if k == 0:
                    for m in range(3):
                        dve.wait_ge(sem("gt_high"), m + 1)
                        nc.vector.tensor_tensor(GSLr[:, m, :], GT[:, m, :], GSH[:, m, :], ALU.subtract)\
                            .then_inc(sem("gt_low"), 1)
                c = FIRST["down"] + k
                split_low(dve, (c + LEAD, 0, 0))
                if k + 3 < NF:
                    m = k + 3
                    dve.wait_ge(sem("gt_high"), m + 1)
                    nc.vector.tensor_tensor(GSLr[:, m % 4, :], GT[:, m, :], GSH[:, m % 4, :], ALU.subtract)\
                        .then_inc(sem("gt_low"), 1)
            add_normed(dve, "dve", "ffpost", link)
            l0, l1 = par("lb0"), par("lb1")
            link(nc.vector.tensor_tensor(lbt[:, 0:4], l0, l1, ALU.max))
            nc.vector.tensor_tensor(lbt[:, 4:8], l0, lbt[:, 0:4], ALU.subtract)
            nc.vector.tensor_tensor(lbt[:, 8:12], l1, lbt[:, 0:4], ALU.subtract).then_inc(sem("lb_shifted"), 1)
            dve.wait_ge(sem("lb_exp"), 1)
            link(nc.vector.tensor_tensor(lbt[:, 0:4], lbt[:, 4:8], lbt[:, 8:12], ALU.add))
            link(nc.vector.reciprocal(lbt[:, 0:4], lbt[:, 0:4]))
            link(nc.vector.tensor_tensor(lb, lbt[:, 4:8], lbt[:, 0:4], ALU.mult))
            link(nc.vector.tensor_scalar(oml, lb, -1.0, 1.0, ALU.mult, ALU.add))
            norm_turn(dve, "dve", "pre3", link, lambda k: MOD[:, 8 + k:9 + k], lambda k: MOD[:, k:k + 1])
            ST = HF
            cw = par("conv").rearrange("p (n w) -> p n w", w=3)

            def take(n):
                for h in range(4):
                    dve.wait_ge(sem("lv_scores"), 4 * n + h + 1)
                    last = nc.vector.copy_predicated(
                        ST[:, h, :].rearrange("p (c t) -> p c t", c=4),
                        LEVEL[:, n, :].unsqueeze(1).to_broadcast([P, 4, P]),
                        PS[:, 4 + h, :].rearrange("p (c t) -> p c t", c=4))
                    last.then_inc(sem("lv_taken"), 1)
                dve.wait_ge(sem("lv_taken"), 4 * n + 4)

            def differences(n):
                m = LEVELS[n]
                b = flat(BB).rearrange("p (b x) -> p b x", x=2 * m)
                e = flat(EE).rearrange("p (b x) -> p b x", x=2 * m)
                nc.vector.tensor_tensor(e, b, b[:, :, m - 1:m].to_broadcast([P, S * 4 // (2 * m), 2 * m]), ALU.subtract)\
                    .then_inc(sem("lv_diff"), 1)

            def decayed(n):
                wait(dve, "lv_scores", 4 * n)
                dve.wait_ge(sem("lv_exp"), n + 1)
                view = lambda r: flat(r).rearrange("p (b s m) -> p b s m", s=2, m=LEVELS[n])
                nc.vector.tensor_tensor(view(SC8)[:, :, 1, :], view(HQ)[:, :, 1, :], view(EE)[:, :, 1, :], ALU.mult)
                nc.vector.tensor_tensor(view(SC9)[:, :, 0, :], view(HK)[:, :, 0, :], view(EE)[:, :, 0, :], ALU.mult)\
                    .then_inc(sem("lv_ready"), 1)
                dve.wait_ge(sem("lv_ready"), n + 1)

            def convolve(n):
                link(nc.vector.tensor_scalar(CX[:, n, :], CC[:, n, :], cw[:, n, 2:3], None, ALU.mult))
                for w in (1, 0):
                    d_ = 2 - w
                    link(nc.vector.scalar_tensor_tensor(CX[:, n, d_:], CC[:, n, 0:S - d_], cw[:, n, w:w + 1], CX[:, n, d_:],
                                                        ALU.mult, ALU.add))

            for m in range(28):
                split_low(dve, (FIRST["win2"] + m + LEAD, 0, 0))
                if m == 4:
                    dve.wait_ge(sem("p2_stored"), 4)
                    for h in range(4):
                        last = nc.vector.tensor_scalar(HF[:, h, :], HF[:, h, :], oml[:, h:h + 1], lb[:, h:h + 1],
                                                       ALU.mult, ALU.add)
                    last.then_inc(sem("f_ready"), 1)
                    for h in range(4):
                        nc.vector.tensor_scalar(HK[:, h, :], HK[:, h, :], oml[:, h:h + 1], None, ALU.mult)
                    link(nc.vector.memset(SC8, 1.0))
                    link(nc.vector.memset(flat(SC8)[:, 0::P], 0.0))
                if m == 6:
                    dve.wait_ge(sem("logf"), 1)
                    link(nc.vector.tensor_tensor_scan(flat(BB), flat(SC8), flat(HF), 0.0, ALU.mult, ALU.add))
                    nc.vector.memset(HF, 0.0)
                    nc.vector.memset(SC8, 0.0)
                    link(nc.vector.memset(SC9, 0.0))
                if m == 8:
                    dve.wait_ge(sem("levels_landed"), 16)
                    dve.wait_ge(sem("p2_stored"), 8)
                n = (m - 8) // 2
                if m >= 8 and m % 2 == 0 and n < len(LEVELS):
                    differences(n)
                if m >= 9 and m % 2 == 1 and n < len(LEVELS):
                    decayed(n)
                if m >= 11 and m % 2 == 1 and n - 1 < 8:
                    take(n - 1)
                if m == 22:
                    dve.wait_ge(sem("p2_stored"), 20)
                    link(nc.vector.tensor_tensor(CC, CC, CX, ALU.mult))
                if 24 <= m:
                    convolve(m - 24)
            nc.vector.tensor_tensor(CB, CB, CX, ALU.mult).then_inc(sem("cv_done"), 1)
            b = flat(BB).rearrange("p (b x) -> p b x", x=P)
            nc.vector.tensor_tensor(flat(SC9).rearrange("p (b x) -> p b x", x=P), b[:, :, P - 1:P].to_broadcast([P, 16, P]), b,
                                    ALU.subtract).then_inc(sem("dk_diff"), 1)
            dve.wait_ge(sem("dk_exp"), 1)
            nc.vector.tensor_tensor(SC9, SC9, HK, ALU.mult).then_inc(sem("kd_ready"), 1)
            nc.vector.tensor_tensor(CX, CX, HQ, ALU.mult).then_inc(sem("qx_ready"), 1)
            for c in range(3):
                dve.wait_ge(sem("kv_ready"), c + 1)
                for h in range(4):
                    ps = PS[:, 4 + c, h * P:(h + 1) * P]
                    if c == 0:
                        last = nc.vector.tensor_copy(STATE[:, 0, h, :], ps)
                    else:
                        last = nc.vector.scalar_tensor_tensor(STATE[:, c, h, :], STATE[:, c - 1, h, :],
                                                              eb[:, 4 * h + c:4 * h + c + 1], ps, ALU.mult, ALU.add)
                last.then_inc(sem("state_ready"), 1)
                dve.wait_ge(sem("state_ready"), c + 1)
            dve.wait_ge(sem("cv_rstd"), 1)
            for n in range(4):
                last = nc.vector.scalar_tensor_tensor(CB[:, n, :], CB[:, n, :], par("conorm", n, n + 1), CC[:, n, :],
                                                      ALU.mult, ALU.mult)
            last.then_inc(sem("cv_normed"), 1)
            dve.wait_ge(sem("cv_normed"), 1)
            for h in range(4):
                dve.wait_ge(sem("o_rstd"), h // 2 + 1)
                last = nc.vector.scalar_tensor_tensor(SC8[:, h, :], PS[:, h, :], par("onorm", h, h + 1), SC9[:, h, :],
                                                      ALU.mult, ALU.mult)
            link(last)
            for n in range(2):
                hs = slice(2 * n, 2 * n + 2)
                nc.vector.tensor_tensor(SC8[:, hs, :], SC8[:, hs, :], HG[:, hs, :], ALU.mult).then_inc(sem("y2_ready"), 1)
            dve.wait_ge(sem("y2_high"), 1)
            nc.vector.tensor_tensor(HLr[:, 4:8, :], CB, HH[:, 4:8, :], ALU.subtract)
            for n in range(2):
                hs = slice(2 * n, 2 * n + 2)
                dve.wait_ge(sem("y2_high"), n + 2)
                nc.vector.tensor_tensor(HLr[:, hs, :], SC8[:, hs, :], HH[:, hs, :], ALU.subtract)
            barrier(dve, "states")
            for k in range(NK):
                split_low(dve, (FIRST["wout2"] + k + LEAD, 0, 0))
            dve.wait_ge(sem("chunk_used"), FIRST["wout2"] + NK)
            add_rows(dve, lambda t, out: nc.vector.tensor_tensor(out, banks(t), GATE[:, 0, :].rearrange(
                "p (a b) -> p a b", a=2), ALU.mult))
            norm_turn(dve, "dve", "pre4", link, lambda k: MOD[:, 24 + k:25 + k], lambda k: MOD[:, 16 + k:17 + k])
            TI = TIU.bitcast(U32)
            c0 = FIRST["query"]

            mark, until = link.mark, link.until

            def best16(vals, idx, src, done):
                for n in range(len(src)):
                    if done[n]:
                        until(done[n])
                    done[n] = mark(nc.vector.max(vals[n][:, 0:8], src[n]))
                for n in range(len(src)):
                    until(done[n])
                    done[n] = mark(nc.vector.max_index(idx[n][:, 0:8], vals[n][:, 0:8], src[n]))
                for n in range(len(src)):
                    until(done[n])
                    done[n] = mark(nc.vector.match_replace(src[n], vals[n][:, 0:8], src[n], -3.0e38))
                for n in range(len(src)):
                    until(done[n])
                    done[n] = mark(nc.vector.max(vals[n][:, 8:16], src[n]))
                for n in range(len(src)):
                    until(done[n])
                    done[n] = mark(nc.vector.max_index(idx[n][:, 8:16], vals[n][:, 8:16], src[n]))

            BIu = BI.bitcast(U32)
            PABu = PAB.bitcast(U32)
            free_after = [0, 0]

            def pairs(t, i):
                vals = [BV[:, t % 2, 2 * i + h, :] for h in range(2)]
                idx = [BIu[:, 2 * i + h, :] for h in range(2)]
                src = (CAND, CAND2)
                done = free_after
                for h in range(2):
                    if done[h]:
                        until(done[h])
                    a = TV[:, t, 4 * i + 2 * h, :].unsqueeze(2).to_broadcast([P, TOPK, TOPK])
                    b = TV[:, t, 4 * i + 2 * h + 1, :].unsqueeze(1).to_broadcast([P, TOPK, TOPK])
                    done[h] = mark(nc.vector.tensor_tensor(src[h].rearrange("p (a b) -> p a b", a=TOPK), a, b, ALU.add))
                best16(vals, idx, src, done)
                return done[1]

            for m in range(17):
                if m < 16:
                    split_low(dve, (c0 + m + LEAD, 0, 0))
                if m >= 1:
                    f = m - 1
                    dve.wait_ge(sem("scores_stored"), m)
                    done = [0] * NT
                    best16([TV[:, t, f, :] for t in range(NT)], [TI[:, t, f, :] for t in range(NT)],
                           [SS[:, t, f, :] for t in range(NT)], done)
                    until(done[-1])
                    if f % 4 == 3:
                        pairs(0, f // 4)
            barrier(dve, "queries")

            def summed(t, i):
                dve.wait_ge(sem("eq_ready"), i + (4 * t + 1))
                for h in range(PH // 2):
                    num = TFf[:, bass.ds(i * 64 + 16 * h, TOPK)].unsqueeze(1).to_broadcast([P, TOPK, TOPK])
                    last = nc.vector.scalar_tensor_tensor(EQ[:, h], EQ[:, h], 0.0, num, ALU.is_equal, ALU.mult)
                last.then_inc(sem("eq_numbers"), 1)
                dve.wait_ge(sem("eq_numbers"), i + (4 * t + 1))
                nc.vector.tensor_reduce(N12[:, t % 2].rearrange("p s u -> p (s u)")[:, bass.ds(i * 64, 64)],
                                        EQ.rearrange("p h k a -> p (h k) a"), AX, ALU.add).then_inc(sem("eq_summed"), 1)

            def onehot_rows(t, i, r):
                dve.wait_ge(sem("gm_ready"), i * 8 + (32 * t + 2 * r + 2))
                rs = slice(8 * (r % 2), 8 * (r % 2) + 8)

                def each(n):
                    return LST[:, t % 2, n, bass.ds(i * 32 + 8 * r, 8)].unsqueeze(2).to_broadcast([P, 8, P])
                nc.vector.tensor_tensor(OHA[:, rs, :], con("iota").unsqueeze(1).to_broadcast([P, 8, P]), each(0),
                                        ALU.is_equal)
                dve.wait_ge(sem("rows_apart"), i * 4 + (16 * t + r + 1))
                nc.vector.scalar_tensor_tensor(OHB[:, rs, :], apart(t, r), 0.0, each(2), ALU.is_equal, ALU.mult)\
                    .then_inc(sem("onehot_ready"), 1)

            dve.sem_inc(sem("eq_summed"), 1)
            for s_ in range(NT + 2):
                if s_ < NT:
                    wait(dve, "list_turned", s_ - 1)
                if s_ >= 2:
                    dve.wait_ge(sem("list_stored"), s_ - 1)

                def turn(i):
                    last = 0
                    for r in range(4):
                        if r == 2 and 1 <= s_ < NT:
                            last = pairs(s_, i)
                        if s_ >= 2:
                            onehot_rows(s_ - 2, i, r)
                    if 1 <= s_ <= NT:
                        summed(s_ - 1, i)
                    return last

                if s_ == 0:
                    until(max(free_after))
                elif s_ < NT:
                    for i in range(4):
                        last = turn(i)
                    until(last)
                else:
                    with dve.Fori(0, 4) as i:
                        turn(i)
                if 1 <= s_ <= NT:
                    t = s_ - 1
                    dve.wait_ge(sem("best_exp"), t + 1)
                    dve.wait_ge(sem("eq_summed"), 4 * t + 5)
                    link(nc.vector.tensor_reduce(zg, BV[:, t % 2], AX, ALU.add))
                    link(nc.vector.reciprocal(zg, zg))
                    nc.vector.tensor_tensor(BV[:, t % 2], BV[:, t % 2], zg.unsqueeze(2).to_broadcast([P, PH, TOPK]),
                                            ALU.mult).then_inc(sem("list_ready"), 1)
                if s_ < NT:
                    link(nc.vector.tensor_copy(zs8, BV[:, s_ % 2, :, 0]))
                    nc.vector.tensor_tensor(BV[:, s_ % 2], BV[:, s_ % 2], zs8.unsqueeze(2).to_broadcast([P, PH, TOPK]),
                                            ALU.subtract).then_inc(sem("best_shifted"), 1)
                    bi = BIu.rearrange("p h k -> p (h k)")
                    nc.vector.tensor_scalar(PABu[:, 0], bi, 4, None, ALU.logical_shift_right)
                    link(nc.vector.tensor_scalar(PABu[:, 1], bi, 15, None, ALU.bitwise_and))
                    nc.vector.tensor_copy(TF, TI[:, s_].rearrange("p (h s) k -> p s h k", s=2))
                    nc.vector.tensor_copy(PAB, PABu).then_inc(sem("places_ready"), 1)
            barrier(dve, "gates")
            for t in range(NT):
                nc.vector.memset(YA[:, t, :], 0.0)
            dve.drain().then_inc(sem("acc_done"), 1)
            dve.wait_ge(sem("acc_done"), 1)
            nc.vector.memset(WF[:, 0, 0:1], 0.0).then_inc(sem("w_done"), 2)

            def step(c, g8, b, u, v):
                n = 0
                for half in range(2):
                    if u:
                        for m in range(4 * half, 4 * half + 4):
                            split_low(dve, plus(c, n + LEAD))
                            dve.wait_ge(sem("gelu_done"), g8 + (m + 5))
                            dve.wait_ge(sem(f"gates_landed{m % 4}"), (g8 * 4 + 16) if m < 4 else (g8 * 4 + 32))
                            dve.wait_ge(sem("w_done"), g8 + (m + 2))
                            nc.vector.tensor_tensor(WF[:, m % 2, :], GE[:, m % 2, :], GR_[:, m % 4, :], ALU.mult)\
                                .then_inc(sem("w_done"), 1)
                            dve.wait_ge(sem("w_high"), g8 + (m + 1))
                            nc.vector.tensor_tensor(WGTr[:, b, 1, m, :], WF[:, m % 2, :], WGT[:, b, 0, m, :],
                                                    ALU.subtract).then_inc(sem("w_low"), 1)
                            n += 1
                    if v:
                        for q in range(4):
                            split_low(dve, plus(c, n + LEAD))
                            n += 1
                        dve.wait_ge(sem("chunk_used"), number(c, n))
                        for t in range(NT):
                            acc = YA[:, t, half * 512:(half + 1) * 512]
                            last = nc.vector.tensor_tensor(acc, acc, PS[:, t, :], ALU.add)
                        last.then_inc(sem("acc_done"), 1)
            experts(dve, step)
            barrier(dve, "experts")
            dve.wait_ge(sem("x3_back"), 16)
            for t in range(NT):
                nc.vector.tensor_tensor(YA[:, t, :], YA[:, t, :], GATE[:, 1, :], ALU.mult).then_inc(sem("rows_weighted"), 1)
            for t in range(NT):
                dve.wait_ge(sem("rows_weighted"), 3 * NT + t + 1)
                nc.vector.tensor_tensor(X[:, t, :], YA[:, t, :], X3[:, t, :], ALU.add).then_inc(sem("rows_added"), 1)
            dve.wait_ge(sem("rows_added"), 4 * NT)
            rms_dve(dve, link, "final")
            dve.wait_ge(sem("row_landed"), 48)
            for t in range(NT):
                nc.vector.scalar_tensor_tensor(X[:, t, :], X[:, t, :], rstd[:, t:t + 1], ROW[:, :], ALU.mult, ALU.mult)\
                    .then_inc(sem("out_ready"), 1)

        @block.tensor
        def _(pe):
            pe.wait_ge(sem("const_landed"), 16)
            norm_turn(pe, "pe", "pre1")
            for b in range(6):
                w = 512 if b < 5 else TAIL
                wait(pe, "proj_stored", b - 1)
                for q in range(4):
                    mm_n2(pe, (4 * b + q, 0, 0), q, 4 * (b % 2), w, "pre1" if b == 0 else None)
            barrier(pe, "projection")

            def turn_heads(ns):
                for n in ns:
                    wait(pe, "head_stored", n - 7 if n < 8 else n - 1)
                    o = ROPED[n]
                    if n >= 18:
                        pe.wait_ge(sem("roped"), len(ROPES))
                    for t in range(NT):
                        last = nc.tensor.transpose(PS[0:64, head_bank(n), t * P:(t + 1) * P], PJ[:, t, o:o + DK], ident)
                    last.then_inc(sem("head_turned"), 1)
            turn_heads(range(8))
            pe.wait_ge(sem("head_stored"), 8)
            def rt_out(h):
                pe.wait_ge(sem("rt_decayed"), 4 * h + 4)
                for t in range(NT):
                    for j in range(t + 1):
                        o = sr_at[j] + (t - j) * P
                        last = nc.tensor.matmul(PS[:, 4 + t, h * P:(h + 1) * P], SR[:, h % 2, o:o + P],
                                                PJ[:, j, RV + h * P:RV + (h + 1) * P], start=(j == 0), stop=(j == t))
                last.then_inc(sem("rt_out"), 1)

            for h in range(RH):
                for j in range(NT):
                    u = 4 * h + j
                    wait(pe, "rt_decayed", u - 3)
                    nc.tensor.matmul(PS[:, u % 4, 0:S - j * P], RT[0:64, 4 + h, j * P:(j + 1) * P],
                                     RT[0:64, h, j * P:S], start=True, stop=True).then_inc(sem("rt_scores"), 1)
                if h >= 1:
                    rt_out(h - 1)
            rt_out(RH - 1)
            for w in range(2):
                pe.wait_ge(sem("cmp_dup"), w + 1)
                for g in range(2):
                    for t in range(NT):
                        last = nc.tensor.transpose(PS[:, 2 * w + g, t * P:(t + 1) * P],
                                                   DUP[:, w, t, g].rearrange("p j x -> p (j x)"), ident)
                last.then_inc(sem("cmp_turned"), 1)
            pe.wait_ge(sem("cmp_stored"), 2)
            turn_heads(range(8, 20))
            for w in range(2):
                pe.wait_ge(sem("blk_low"), w + 1)
                for q in range(4):
                    c = (FIRST["cmp"] + 4 * w + q, 0, 0)
                    pe.wait_ge(sem("low_done"), number(c, 1))
                    wh = WHr[:, slot(c), :].rearrange("p (k n) -> p k n", k=4)
                    wl = WLr[:, slot(c), :].rearrange("p (k n) -> p k n", k=4)
                    for kk in range(4):
                        k = 4 * q + kk
                        last = mm3(PS[0:64, w, 0:256], (BLHr[:, w, k, :], BLLr[:, w, k, :]),
                                   (wh[:, kk, :], wl[:, kk, :]), k == 0, k == 15)
                    last.then_inc(sem("chunk_used"), 1)
            pe.wait_ge(sem("head_stored"), 20)
            for w in range(2):
                pe.wait_ge(sem("hid_gelu"), w + 1)
                for f in range(2):
                    last = nc.tensor.transpose(PS[:, 2 + w, 64 * f:64 * f + 64], HT[0:64, w, f * P:(f + 1) * P],
                                               ident[0:64, 0:64])
                last.then_inc(sem("hid_turned"), 1)
            pe.wait_ge(sem("hid_stored"), 1)
            for f in range(2):
                last = nc.tensor.matmul(PS[0:64, 4, 0:64], HIDK[:, f, :], W2[:, 0, f, :], start=(f == 0), stop=(f == 1))
            last.then_inc(sem("kc_ready"), 1)
            pe.wait_ge(sem("kc_roped"), 1)
            nc.tensor.transpose(PS[0:64, 5, 0:64], KC[0:64, 0, :], ident[0:64, 0:64]).then_inc(sem("kct_ready"), 1)
            pe.wait_ge(sem("hid_stored"), 2)
            for g in range(2):
                for f in range(2):
                    last = nc.tensor.matmul(PS[:, 6 + g, 0:64], HID[:, f, g].rearrange("p r n -> p (r n)"), W2[:, 1, f, :],
                                            start=(f == 0), stop=(f == 1))
            last.then_inc(sem("vc_ready"), 1)
            barrier(pe, "compression")
            for t in range(NT):
                for h in range(NH):
                    g = h // 4
                    last = nc.tensor.matmul(PS[:, t, 32 * h:32 * h + 32], QT[0:64, h, t * P:(t + 1) * P],
                                            KCT[0:64, 32 * g:32 * g + 32], start=True, stop=True)
            last.then_inc(sem("cs_ready"), 1)
            pe.wait_ge(sem("cmp_probs"), 1)
            for t in range(NT):
                for g in range(2):
                    u = 2 * t + g
                    last = nc.tensor.transpose(PS[:, 4 + u // 4, (u % 4) * P:(u % 4 + 1) * P],
                                               E4[:, t, 4 * g:4 * g + 4, :].rearrange("p h n -> p (h n)"), ident)
            last.then_inc(sem("cmp_pt"), 1)
            pe.wait_ge(sem("cmp_pt_stored"), 1)
            for t in range(NT):
                for g in range(2):
                    last = nc.tensor.matmul(PS[:, t, 256 * g:256 * g + 256], PTC[:, 2 * t + g, :],
                                            VBD[:, g].rearrange("p r n -> p (r n)"), start=True, stop=True)
            last.then_inc(sem("cmp_out"), 1)
            barrier(pe, "compressed attention")
            pe.wait_ge(sem("ca_low"), 1)
            for s in range(len(units) + 2):
                if s < len(units):
                    b, t, h = units[s]
                    wait(pe, "at_exp", s - 1)
                    nc.tensor.matmul(PS[:, s % 2, 0:(t + 1) * P], QT[0:64, h, t * P:(t + 1) * P],
                                     KT[0:64, 2 * b + h // 4, 0:(t + 1) * P], start=True, stop=False)
                    nc.tensor.matmul(PS[:, s % 2, t * P:(t + 1) * P], MASKr[:, 0, :], MASKr[:, 1, :],
                                     start=False, stop=True).then_inc(sem("at_scores"), 1)
                v, k = ada_at(s)
                if v < 6 and k < NK:
                    if k == 0:
                        wait(pe, "mod_taken", v)
                    c = (FIRST["ada"] + NK * v + k, 0, 0)
                    pe.wait_ge(sem("low_done"), number(c, 1))
                    for half in range(2):
                        hs = slice(half * 512, (half + 1) * 512)
                        last = mm3(PS[:, 6 + half, :], (CABr[:, 0, k, :], CABr[:, 1, k, :]),
                                   (WHr[:, slot(c), hs], WLr[:, slot(c), hs]), k == 0, k == NK - 1)
                    last.then_inc(sem("chunk_used"), 1)
                elif v < 6 and k == NK + 1 and v % 3 < 2:
                    pe.wait_ge(sem("mod_row"), v - v // 3 + 1)
                    for n in range(NK):
                        last = nc.tensor.matmul(PS[:, 6, n:n + 1], MODROW[:, n * P:(n + 1) * P], ident[:, 0:1],
                                                start=True, stop=True)
                    last.then_inc(sem("mod_turned"), 1)
                u = s - 1
                if 0 <= u < len(units):
                    b, t, h = units[u]
                    pe.wait_ge(sem("at_exp"), u + 1)
                    v = u - 2
                    if v >= 0:
                        pe.wait_ge(sem(f"at_stored{v % 2}"), v // 2 + 1)
                    for j in range(t + 1):
                        last = nc.tensor.transpose(PS[:, 2 + u % 2, j * P:(j + 1) * P], EX[:, u % 2, j * P:(j + 1) * P], ident)
                    last.then_inc(sem("at_turned"), 1)
                u = s - 2
                if u >= 0:
                    b, t, h = units[u]
                    n = u // 8
                    pe.wait_ge(sem(f"at_stored{u % 2}"), u // 2 + 1)
                    if h == 0:
                        wait(pe, "at_taken", n - 1)
                    o = (VSL, VWN)[b] + 64 * (h // 4)
                    for j in range(t + 1):
                        last = nc.tensor.matmul(PS[:, 4 + n % 2, h * DK:(h + 1) * DK], PT[:, u % 2, j * P:(j + 1) * P],
                                                PJ[:, j, o:o + DK], start=(j == 0), stop=(j == t))
                    last.then_inc(sem("at_pv"), 1)
            barrier(pe, "attention")
            turn_pe(pe, "mix", Y)
            barrier(pe, "turn")
            for k in range(NK):
                mm_n1(pe, (FIRST["wout"] + k, 0, 0), (HHr[:, k, :], HLr[:, k, :]), k == 0, k == NK - 1)
            add_normed(pe, "pe", "mixpost")
            norm_turn(pe, "pe", "pre2")
            cu = FIRST["up"]
            for k in range(NK):
                tile_ready(pe, "pre2", k)
            with pe.Fori(0, NF // 2) as i:
                for j in range(4):
                    pe.wait_ge(sem("up_free"), i * 4 + (j + 1))
                    mm_t(pe, (cu + j, i, 4), PS[:, j, :])
            barrier(pe, "up")
            for k in range(NF):
                pe.wait_ge(sem("gt_low"), k + 1)
                mm_n1(pe, (FIRST["down"] + k, 0, 0), (GSHr[:, k % 4, :], GSLr[:, k % 4, :]),
                      k == 0, k == NF - 1)
            add_normed(pe, "pe", "ffpost")
            norm_turn(pe, "pe", "pre3")
            c0 = FIRST["win2"]
            def level_scores(n):
                kl, ql = (SC9, SC8) if n < len(LEVELS) else (HK, HQ)
                if n < len(LEVELS):
                    pe.wait_ge(sem("lv_ready"), n + 1)
                for h in range(4):
                    wait(pe, "lv_taken", 4 * (n - 1) + h + 1)
                    for c in range(4):
                        cs = slice(c * P, (c + 1) * P)
                        last = nc.tensor.matmul(PS[:, 4 + h, cs], kl[:, h, cs], ql[:, h, cs], start=True, stop=True)
                    last.then_inc(sem("lv_scores"), 1)

            for m in range(28):
                if m < 24:
                    wait(pe, "p2_stored", m - 3)
                    mm_t(pe, (c0 + m, 0, 0), PS[:, m % 4, :], "pre3" if m == 0 else None)
                else:
                    pe.wait_ge(sem("p2_stored"), 24)
                    mm_n2(pe, (c0 + m, 0, 0), m - 24, 0)
                if m >= 10 and m % 2 == 0 and (m - 10) // 2 < 8:
                    level_scores((m - 10) // 2)
            pe.wait_ge(sem("v_stored"), 1)
            pe.wait_ge(sem("cv_sq"), 1)
            for n in range(4):
                last = nc.tensor.matmul(PS[:, n, :], con("mean"), CC[:, n, :], start=True, stop=True)
            last.then_inc(sem("cv_sums"), 1)
            pe.wait_ge(sem("kd_ready"), 1)
            pe.wait_ge(sem("lv_taken"), 32)
            for h in range(4):
                for c in range(3):
                    cs = slice(c * P, (c + 1) * P)
                    last = nc.tensor.transpose(PS[:, 4 + h, cs], SC9[:, h, cs], ident)
            last.then_inc(sem("kd_turned"), 1)
            pe.wait_ge(sem("kd_stored"), 1)
            for c in range(3):
                for h in range(4):
                    last = nc.tensor.matmul(PS[:, 4 + c, h * P:(h + 1) * P], SC8[:, h, c * P:(c + 1) * P],
                                            HV[:, c, h * P:(h + 1) * P], start=True, stop=True)
                last.then_inc(sem("kv_ready"), 1)
            pe.wait_ge(sem("qx_ready"), 1)
            pe.wait_ge(sem("cv_rstd"), 1)
            for c in range(4):
                wait(pe, "state_ready", c)
                cs = slice(c * P, (c + 1) * P)
                for h in range(4):
                    last = nc.tensor.matmul(PS[:, h, cs], HV[:, c, h * P:(h + 1) * P], HF[:, h, cs], start=True, stop=(c == 0))
                    if c:
                        last = nc.tensor.matmul(PS[:, h, cs], STATE[:, c - 1, h, :], CX[:, h, cs], start=False, stop=True)
            last.then_inc(sem("o_done"), 1)
            pe.wait_ge(sem("o_sq"), 1)
            for h in range(4):
                last = nc.tensor.matmul(PS[:, 4 + h, :], con("mean"), SC9[:, h, :], start=True, stop=True)
                last.then_inc(sem("o_sums"), 1)
            barrier(pe, "states")
            for k in range(NK):
                mm_n1(pe, (FIRST["wout2"] + k, 0, 0), (HHr[:, k, :], HLr[:, k, :]), k == 0, k == NK - 1)
            norm_turn(pe, "pe", "pre4")
            pe.wait_ge(sem("subkeys_landed"), 16)
            c0 = FIRST["query"]
            for m in range(17):
                if m < 16:
                    wait(pe, "query_stored", m - 3)
                    mm_t(pe, (c0 + m, 0, 0), PS[:, m % 4, :], "pre4" if m == 0 else None)
                if m >= 1:
                    n = m - 1
                    pe.wait_ge(sem("query_stored"), n + 1)
                    wait(pe, "scores_stored", n - 3)
                    for t in range(NT):
                        last = nc.tensor.matmul(PS[:, 4 + n % 4, t * P:(t + 1) * P], QE[:, n % 2, t * P:(t + 1) * P],
                                                SUBK[:, n, :], start=True, stop=True)
                    last.then_inc(sem("keys_scored"), 1)
            barrier(pe, "queries")
            pe.sem_inc(sem("gm_ready"), 4)
            for s_ in range(1, NT + 2):
                t = s_ - 2
                if t >= 0:
                    with pe.Fori(0, 8) as i:
                        for q in range(4):
                            pe.wait_ge(sem("gm_stored"), i * 4 + (32 * t + q + 1))
                            if q % 2 == 0:
                                pe.wait_ge(sem("onehot_ready"), i * 2 + (16 * t + q // 2 + 1))
                            for j in range(4 * q, 4 * q + 4):
                                last = nc.tensor.matmul(PS[:, q, (j % 4) * P:(j % 4 + 1) * P], OHA[:, j, :], OHB[:, j, :],
                                                        start=True, stop=True)
                            last.then_inc(sem("gm_ready"), 1)
                if s_ <= NT:
                    t = s_ - 1
                    pe.wait_ge(sem("list_ready"), t + 1)
                    wait(pe, "list_stored", t)
                    for n, src in enumerate((N12[:, t % 2, 0], N12[:, t % 2, 1], BV[:, t % 2].rearrange("p h k -> p (h k)"))):
                        last = nc.tensor.transpose(PS[:, 4, n * P:(n + 1) * P], src, ident)
                    last.then_inc(sem("list_turned"), 1)
            barrier(pe, "gates")

            def step(c, g8, b, u, v):
                n = 0
                for half in range(2):
                    if u:
                        for m in range(4 * half, 4 * half + 4):
                            pe.wait_ge(sem("gelu_done"), g8 + (m + 1))
                            mm_t(pe, plus(c, n), PS[:, 4 + m % 4, :])
                            n += 1
                    if v:
                        pe.wait_ge(sem("acc_done"), (g8 // 4 + (half - 1)) if isinstance(g8, int)
                                   else (acc_of(c) + half))
                        for q in range(4):
                            cc = plus(c, n)
                            pe.wait_ge(sem("low_done"), number(cc, 1))
                            pe.wait_ge(sem("w_low"), g8 + (2 * q + 2 - GROUP))
                            for r in range(2):
                                i2 = 2 * q + r
                                for t in range(NT):
                                    ts = slice(t * P, (t + 1) * P)
                                    rs = slice(r * 512, (r + 1) * 512)
                                    last = mm3(PS[:, t, :], (WGTr[:, 1 - b, 0, i2, ts], WGTr[:, 1 - b, 1, i2, ts]),
                                               (WHr[:, slot(cc), rs], WLr[:, slot(cc), rs]), i2 == 0, i2 == GROUP - 1)
                            last.then_inc(sem("chunk_used"), 1)
                            n += 1

            def acc_of(c):
                s_ = (c[0] - FIRST["experts"] - GROUP) // (2 * GROUP)
                return c[1] * 4 + (2 * s_ + 1)
            experts(pe, step)
            barrier(pe, "experts")


def kernel(**inputs):
    import concourse.bacc as bacc
    from concourse.bass_utils import run_bass_kernel_spmd

    nc = bacc.Bacc("TRN2", target_bir_lowering=False, num_devices=1)
    v = {k: np.asarray(a) for k, a in inputs.items()}

    def tiles(a, n):
        return a.reshape(n, P).T

    def columns(w):
        return w.reshape(NK, P, -1, P).transpose(2, 1, 0, 3).reshape(-1, P, NK * P)

    small, decay, levels = constants()
    par = [tiles(v["norm_mix_pre"][0], 8), tiles(v["norm_ffn_pre"][0], 8), tiles(v["norm1_w_2"][0], 8),
           tiles(v["norm2_w_2"][0], 8), tiles(v["ret_gn_w"][0], 4), tiles(v["b_ada_2"][0], 48),
           tiles(v["c_2"][0], 8), tiles(v["hgrn_lb_logits_2"][0], 4), tiles(v["hgrn_lb_logits_2"][1], 4),
           tiles(v["hgrn_onorm_w_2"][0], 4), tiles(v["conv_onorm_w_2"][0], 4),
           v["conv_w_2"][0].reshape(3, 4, P).transpose(2, 1, 0).reshape(P, 12),
           v["ffn_conv"][0].reshape(3, 2, NF, P).transpose(3, 2, 1, 0).reshape(P, 132)]
    up = columns(v["ffn_w_up"][0])
    w2 = v["w_in_2"][0]
    w2c = columns(w2)
    arrays = {
        "x": v["x"][0],
        "const": np.concatenate([small[n] for n, _ in CONST_COLS], axis=1),
        "param": np.concatenate(par, axis=1),
        "decay": decay, "levels": levels,
        "nm_post": v["norm_mix_post"][0], "nf_post": v["norm_ffn_post"][0], "final_w": v["final_norm_w_2"],
        "w_in": v["w_in"][0],
        "cmp_w1": np.stack([v["cmp_k_w1"][0], v["cmp_v_w1"][0]]).reshape(2, 4, 4, P, 256).transpose(0, 1, 3, 2, 4)
                    .reshape(8, P, 1024),
        "cmp_w2": np.stack([v["cmp_k_w2"][0], v["cmp_v_w2"][0]]),
        "cmp_pos": np.stack([v["cmp_k_pos"][0], v["cmp_v_pos"][0]]).reshape(2, 16, 2, DK).transpose(2, 3, 0, 1)
                     .reshape(P, 2, 16),
        "w_out": v["w_out"][0],
        "ffn_up": np.stack([up[:NF], up[NF:]], axis=1).reshape(2 * NF, P, 1024),
        "ffn_down": v["ffn_w_down"][0],
        "w_ada": v["w_ada_2"][0],
        "bada_gate": v["b_ada_2"][0].reshape(6, D)[[2, 5]],
        "win2": np.concatenate([w2c[4:8], w2c[0:4], w2c[16:28], w2c[12:16],
                                w2[:, 1024:1536].reshape(4, 2, P, 512).transpose(0, 2, 1, 3).reshape(4, P, 1024)]),
        "w_out2": v["w_out_2"][0],
        "query": columns(v["peer_w_query_2"][0]),
        "subk": v["peer_sub_keys_2"][0].reshape(16, PK, P).transpose(2, 0, 1),
        "peer_u": v["peer_u_2"][0].reshape(P, P, NK, P).transpose(1, 3, 2, 0).reshape(P, P, 1024),
        "peer_v": v["peer_v_2"][0],
    }
    arrays = {k: np.ascontiguousarray(a) for k, a in arrays.items()}
    d = {}
    for name, a in arrays.items():
        d[name] = nc.dram_tensor("in_" + name, a.shape, mybir.dt.from_np(a.dtype), kind="ExternalInput").ap()
    d["gate_matrices"] = nc.dram_tensor("gate_matrices", (S // 64, P, P, 64), F32, kind="Internal").ap()
    d["x3"] = nc.dram_tensor("x3", (P, NT, D), F32, kind="Internal").ap()
    d["out"] = nc.dram_tensor("out_0", (S, D), F32, kind="ExternalOutput").ap()
    build(nc, d)
    r = run_bass_kernel_spmd(nc, [{"in_" + k: a for k, a in arrays.items()}], core_ids=[0])
    return r.results[0]["out_0"].reshape(1, S, D)
```
